# Optimizing a Trainium2 kernel written in Bass

```python
import jax, jax.numpy as jnp
from jax import lax
import numpy as np
import math

D_MODEL = 1024
BATCH = 1
SEQ = 256
DEPTH = 2

N_MIXERS = 2
HEAD_DIM = 64
MEM_LEN = 256
MEM_HEADS = 4
MEM_WIDTH = MEM_HEADS * HEAD_DIM
MIX_WIDTH = D_MODEL - MEM_WIDTH
CONV_WIDTH = 31
MOBA_HEADS = MIX_WIDTH // HEAD_DIM
MOBA_BLOCK = 256
MOBA_TOPK = 3
Q_CHUNK = 64
N_GROUPS = 4
EXPERTS_PER_GROUP = 8
EXPERT_TOPK = 2
D_EXPERT = 512
LN_EPS = 1e-5
DEEPNORM_ALPHA = (2 * DEPTH) ** 0.25
DEEPNORM_BETA = (8 * DEPTH) ** -0.25
N_CONV_LAYERS = (DEPTH + 1) // 2
N_MOBA_LAYERS = DEPTH // 2


def layer_norm(x, g, b):
    xf = x.astype(jnp.float32)
    mu = jnp.mean(xf, axis=-1, keepdims=True)
    var = jnp.mean(jnp.square(xf - mu), axis=-1, keepdims=True)
    return ((xf - mu) * lax.rsqrt(var + LN_EPS) * g + b).astype(x.dtype)

def conformer_conv(u, dw_w, dw_b, ln_g, ln_b):
    a, gate = jnp.split(u, 2, axis=-1)
    h = a * jax.nn.sigmoid(gate)
    h = lax.conv_general_dilated(
        h, dw_w[:, None, :], window_strides=(1,),
        padding=[(CONV_WIDTH - 1, 0)],
        dimension_numbers=('NWC', 'WIO', 'NWC'),
        feature_group_count=MIX_WIDTH) + dw_b
    h = layer_norm(h, ln_g, ln_b)
    return jax.nn.silu(h)

def memory_attention(q, mem_k, mem_v):
    s = jnp.einsum('bshd,bmhd->bhsm', q, mem_k).astype(jnp.float32) * (HEAD_DIM ** -0.5)
    p = jax.nn.softmax(s, axis=-1).astype(q.dtype)
    return jnp.einsum('bhsm,bmhd->bshd', p, mem_v)

def moba_attention(q, k, v):
    b_, h_, s_, hd = q.shape
    n_blocks = -(-s_ // MOBA_BLOCK)
    s_pad = n_blocks * MOBA_BLOCK
    pad = ((0, 0), (0, 0), (0, s_pad - s_), (0, 0))
    q, k, v = jnp.pad(q, pad), jnp.pad(k, pad), jnp.pad(v, pad)
    k_blk = k.reshape(b_, h_, n_blocks, MOBA_BLOCK, hd)
    v_blk = v.reshape(b_, h_, n_blocks, MOBA_BLOCK, hd)
    k_mean = jnp.mean(k_blk.astype(jnp.float32), axis=3)
    n_sel = min(MOBA_TOPK, n_blocks - 1)
    scale = hd ** -0.5
    b_idx = jnp.arange(b_)[:, None, None, None]
    h_idx = jnp.arange(h_)[None, :, None, None]

    def chunk(ci):
        start = ci * Q_CHUNK
        q_c = lax.dynamic_slice_in_dim(q, start, Q_CHUNK, axis=2)
        own = start // MOBA_BLOCK
        q_pos = start + jnp.arange(Q_CHUNK)
        k_own = lax.dynamic_index_in_dim(k_blk, own, axis=2, keepdims=False)
        v_own = lax.dynamic_index_in_dim(v_blk, own, axis=2, keepdims=False)
        k_pos = own * MOBA_BLOCK + jnp.arange(MOBA_BLOCK)
        s_own = jnp.einsum('bhqd,bhkd->bhqk', q_c, k_own).astype(jnp.float32) * scale
        s_own = jnp.where(k_pos[None, :] <= q_pos[:, None], s_own, -jnp.inf)
        if n_sel == 0:
            p = jax.nn.softmax(s_own, axis=-1).astype(v.dtype)
            return jnp.einsum('bhqk,bhkd->bhqd', p, v_own)
        gate = jnp.einsum('bhqd,bhnd->bhqn', q_c.astype(jnp.float32), k_mean)
        gate = jnp.where(jnp.arange(n_blocks) < own, gate, -jnp.inf)
        _, idx = lax.top_k(gate, n_sel)
        valid = idx < own
        k_sel = k_blk[b_idx, h_idx, idx]
        v_sel = v_blk[b_idx, h_idx, idx]
        s_sel = jnp.einsum('bhqd,bhqnkd->bhqnk', q_c, k_sel).astype(jnp.float32) * scale
        s_sel = jnp.where(valid[..., None], s_sel, -jnp.inf)
        s_sel = s_sel.reshape(b_, h_, Q_CHUNK, n_sel * MOBA_BLOCK)
        p = jax.nn.softmax(jnp.concatenate([s_own, s_sel], axis=-1), axis=-1).astype(v.dtype)
        p_own = p[..., :MOBA_BLOCK]
        p_sel = p[..., MOBA_BLOCK:].reshape(b_, h_, Q_CHUNK, n_sel, MOBA_BLOCK)
        return (jnp.einsum('bhqk,bhkd->bhqd', p_own, v_own)
                + jnp.einsum('bhqnk,bhqnkd->bhqd', p_sel, v_sel))

    outs = lax.map(chunk, jnp.arange(s_pad // Q_CHUNK))
    out = jnp.moveaxis(outs, 0, 2).reshape(b_, h_, s_pad, hd)
    return out[:, :, :s_]

def hierarchical_moe(x, w_rg, b_rg, w_re, b_re, w_gate, w_up, w_down):
    b_, s_, d_ = x.shape
    t = x.reshape(-1, d_)
    n_tok = t.shape[0]
    rows = jnp.arange(n_tok)
    g_logits = jnp.dot(t, w_rg).astype(jnp.float32) + b_rg
    g_prob = jax.nn.softmax(g_logits, axis=-1)
    g_idx = jnp.argmax(g_logits, axis=-1)
    g_w = g_prob[rows, g_idx]
    e_logits = (jnp.dot(t, w_re).astype(jnp.float32) + b_re).reshape(n_tok, N_GROUPS, EXPERTS_PER_GROUP)
    e_sel = e_logits[rows, g_idx]
    top_v, top_i = lax.top_k(e_sel, EXPERT_TOPK)
    top_w = jax.nn.softmax(top_v, axis=-1) * g_w[:, None]
    within = jnp.sum(jax.nn.one_hot(top_i, EXPERTS_PER_GROUP, dtype=jnp.float32) * top_w[..., None], axis=1)
    combine = (jax.nn.one_hot(g_idx, N_GROUPS, dtype=jnp.float32)[:, :, None]
               * within[:, None, :]).astype(t.dtype)
    out = jnp.zeros_like(t)
    for g in range(N_GROUPS):
        h = (jax.nn.silu(jnp.einsum('td,edf->tef', t, w_gate[g]))
             * jnp.einsum('td,edf->tef', t, w_up[g]))
        out = out + jnp.einsum('tef,efd->td', h * combine[:, g, :, None], w_down[g])
    return out.reshape(b_, s_, d_)

def first_inputs(seed: int = 0) -> dict:
    key = jax.random.key(seed)
    ks = jax.random.split(key, 24)
    f32 = jnp.float32
    nrm = lambda k, shape, scale: jax.random.normal(k, shape, f32) * scale
    na, nb, L = N_CONV_LAYERS, N_MOBA_LAYERS, DEPTH
    G, E, F, D = N_GROUPS, EXPERTS_PER_GROUP, D_EXPERT, D_MODEL
    return {
        "x": nrm(ks[0], (BATCH, SEQ, D), 1.0),
        "mem": nrm(ks[1], (BATCH, MEM_LEN, D), 1.0),
        "w_mem_kv": nrm(ks[2], (D, 2 * MEM_WIDTH), D ** -0.5),
        "conv_w_in": nrm(ks[3], (na, D, 2 * MIX_WIDTH + MEM_WIDTH), D ** -0.5),
        "conv_dw_w": nrm(ks[4], (na, CONV_WIDTH, MIX_WIDTH), CONV_WIDTH ** -0.5),
        "conv_dw_b": nrm(ks[5], (na, MIX_WIDTH), 0.02),
        "conv_ln_g": 1.0 + nrm(ks[6], (na, MIX_WIDTH), 0.02),
        "conv_ln_b": nrm(ks[7], (na, MIX_WIDTH), 0.02),
        "moba_w_in": nrm(ks[8], (nb, D, 3 * MIX_WIDTH + MEM_WIDTH), D ** -0.5),
        "w_o": nrm(ks[9], (L, D, D), D ** -0.5 * DEEPNORM_BETA),
        "ln1_g": 1.0 + nrm(ks[10], (L, D), 0.02),
        "ln1_b": nrm(ks[11], (L, D), 0.02),
        "w_rg": nrm(ks[12], (L, D, G), D ** -0.5),
        "b_rg": nrm(ks[13], (L, G), 0.01),
        "w_re": nrm(ks[14], (L, D, G * E), D ** -0.5),
        "b_re": nrm(ks[15], (L, G * E), 0.01),
        "w_gate": nrm(ks[16], (L, G, E, D, F), D ** -0.5),
        "w_up": nrm(ks[17], (L, G, E, D, F), D ** -0.5),
        "w_down": nrm(ks[18], (L, G, E, F, D), F ** -0.5 * DEEPNORM_BETA),
        "ln2_g": 1.0 + nrm(ks[19], (L, D), 0.02),
        "ln2_b": nrm(ks[20], (L, D), 0.02),
    }

def first_block(x, mem, w_mem_kv, conv_w_in, conv_dw_w, conv_dw_b, conv_ln_g, conv_ln_b,
              moba_w_in, w_o, ln1_g, ln1_b, w_rg, b_rg, w_re, b_re, w_gate, w_up, w_down,
              ln2_g, ln2_b):
    b_, s_, _ = x.shape
    mem_kv = jnp.dot(mem, w_mem_kv).reshape(b_, MEM_LEN, 2, MEM_HEADS, HEAD_DIM)
    mem_k, mem_v = mem_kv[:, :, 0], mem_kv[:, :, 1]
    for i in range(DEPTH):
        j = i // N_MIXERS
        if i % N_MIXERS == 0:
            u = jnp.dot(x, conv_w_in[j])
            y_mix = conformer_conv(u[..., :2 * MIX_WIDTH], conv_dw_w[j], conv_dw_b[j],
                                   conv_ln_g[j], conv_ln_b[j])
            q_mem = u[..., 2 * MIX_WIDTH:]
        else:
            u = jnp.dot(x, moba_w_in[j])
            qkv = u[..., :3 * MIX_WIDTH].reshape(b_, s_, 3, MOBA_HEADS, HEAD_DIM)
            qkv = jnp.transpose(qkv, (2, 0, 3, 1, 4))
            y_mix = moba_attention(qkv[0], qkv[1], qkv[2])
            y_mix = jnp.transpose(y_mix, (0, 2, 1, 3)).reshape(b_, s_, MIX_WIDTH)
            q_mem = u[..., 3 * MIX_WIDTH:]
        y_mem = memory_attention(q_mem.reshape(b_, s_, MEM_HEADS, HEAD_DIM), mem_k, mem_v)
        y_mem = y_mem.reshape(b_, s_, MEM_WIDTH)
        y = jnp.dot(jnp.concatenate([y_mix, y_mem], axis=-1), w_o[i])
        x = layer_norm(DEEPNORM_ALPHA * x + y, ln1_g[i], ln1_b[i])
        f = hierarchical_moe(x, w_rg[i], b_rg[i], w_re[i], b_re[i], w_gate[i], w_up[i], w_down[i])
        x = layer_norm(DEEPNORM_ALPHA * x + f, ln2_g[i], ln2_b[i])
    return x


ROPE_THETA = 10000.0
NORM_EPS = 1e-6
Q_BLOCK = 128
BIG = 1e9

NSA_HEADS = 8
NSA_KV_GROUPS = 2
NSA_HEADS_PER_GROUP = NSA_HEADS // NSA_KV_GROUPS
CMP_BLOCK = 32
CMP_STRIDE = 16
CMP_HIDDEN = 256
SLC_BLOCK = 64
SLC_TOPK = 16
WINDOW = 512
NSA_WIDTH = NSA_HEADS * HEAD_DIM
NSA_KV_WIDTH = NSA_KV_GROUPS * HEAD_DIM

DIFF_HEADS = 4
DIFF_QK_WIDTH = DIFF_HEADS * 2 * HEAD_DIM
DIFF_V_DIM = 2 * HEAD_DIM
DIFF_WIDTH = DIFF_HEADS * DIFF_V_DIM

SGU_CHUNK = 128
SGU_GROUPS = 4
SGU_WIDTH = 512
SGU_GROUP_DIM = SGU_WIDTH // SGU_GROUPS

N_BRANCHES = 3
BRANCH_WIDTH = 512
D_FF = -(-8 * D_MODEL // (3 * 256)) * 256

IN_SPLITS = [NSA_WIDTH, 6 * NSA_KV_WIDTH, NSA_HEADS * 3,
             DIFF_QK_WIDTH, DIFF_QK_WIDTH, DIFF_WIDTH, 2 * SGU_WIDTH]
D_IN = sum(IN_SPLITS)
IN_OFFSETS = [int(v) for v in np.cumsum(IN_SPLITS)[:-1]]


def rmsnorm(x, g):
    xf = x.astype(jnp.float32)
    y = xf * lax.rsqrt(jnp.mean(xf * xf, axis=-1, keepdims=True) + NORM_EPS)
    return y.astype(x.dtype) * g

def rope(x, positions):
    half = x.shape[-1] // 2
    inv_freq = ROPE_THETA ** (-jnp.arange(half, dtype=jnp.float32) / half)
    ang = positions.astype(jnp.float32)[..., None] * inv_freq
    cos = jnp.cos(ang)[:, :, None, :].astype(x.dtype)
    sin = jnp.sin(ang)[:, :, None, :].astype(x.dtype)
    x1, x2 = x[..., :half], x[..., half:]
    return jnp.concatenate([x1 * cos - x2 * sin, x2 * cos + x1 * sin], axis=-1)

def masked_softmax(logits, mask):
    lf = jnp.where(mask, logits.astype(jnp.float32), -1e30)
    p = jax.nn.softmax(lf, axis=-1)
    return jnp.where(mask, p, 0.0)

def map_query_blocks(fn, seq):
    out = lax.map(fn, jnp.arange(seq // Q_BLOCK))
    nb, b, t, w = out.shape
    return out.transpose(1, 0, 2, 3).reshape(b, nb * t, w)

def nsa_attention(q, k_cmp, v_cmp, k_slc, v_slc, k_win, v_win, gates, positions,
                  pos_k, wk1, wk2, pos_v, wv1, wv2):
    B, S = q.shape[:2]
    G, HPG, d = NSA_KV_GROUPS, NSA_HEADS_PER_GROUP, HEAD_DIM
    scale = d ** -0.5
    q_rot = rope(q, positions)
    k_slc = rope(k_slc, positions)
    k_win = rope(k_win, positions)

    n_cmp = (S - CMP_BLOCK) // CMP_STRIDE + 1
    cmp_idx = np.arange(n_cmp)[:, None] * CMP_STRIDE + np.arange(CMP_BLOCK)[None, :]
    cmp_end = jnp.asarray(np.arange(n_cmp) * CMP_STRIDE + CMP_BLOCK - 1)

    def compress(kv, pos_emb, w1, w2):
        blocks = kv[:, cmp_idx] + pos_emb[:, None, :]
        blocks = blocks.transpose(0, 1, 3, 2, 4).reshape(B, n_cmp, G, CMP_BLOCK * d)
        return jax.nn.gelu(blocks @ w1) @ w2

    kc = compress(k_cmp, pos_k, wk1, wk2)
    vc = compress(v_cmp, pos_v, wv1, wv2)

    n_slc = S // SLC_BLOCK
    slc_k = min(SLC_TOPK, n_slc)
    c_start = np.arange(n_cmp)[:, None] * CMP_STRIDE
    s_start = np.arange(n_slc)[None, :] * SLC_BLOCK
    overlap = jnp.asarray(((c_start < s_start + SLC_BLOCK) &
                           (c_start + CMP_BLOCK > s_start)).astype(np.float32))
    slc_starts = jnp.arange(n_slc) * SLC_BLOCK
    blk_ids = jnp.arange(n_slc)

    kb = k_slc.reshape(B, n_slc, SLC_BLOCK, G, d).transpose(0, 3, 1, 2, 4)
    vb = v_slc.reshape(B, n_slc, SLC_BLOCK, G, d).transpose(0, 3, 1, 2, 4)
    gather = jax.vmap(jax.vmap(lambda blocks, ids: blocks[ids]))

    k_win_pad = jnp.pad(k_win, ((0, 0), (WINDOW, 0), (0, 0), (0, 0)))
    v_win_pad = jnp.pad(v_win, ((0, 0), (WINDOW, 0), (0, 0), (0, 0)))

    def block(i):
        s0 = i * Q_BLOCK
        t = s0 + jnp.arange(Q_BLOCK)
        qg = lax.dynamic_slice_in_dim(q, s0, Q_BLOCK, axis=1).reshape(B, Q_BLOCK, G, HPG, d)
        qrg = lax.dynamic_slice_in_dim(q_rot, s0, Q_BLOCK, axis=1).reshape(B, Q_BLOCK, G, HPG, d)
        gb = lax.dynamic_slice_in_dim(gates, s0, Q_BLOCK, axis=1).reshape(B, Q_BLOCK, G, HPG, 3)

        logit_c = jnp.einsum('btghd,bngd->bghtn', qg, kc) * scale
        p_c = masked_softmax(logit_c, cmp_end[None, :] <= t[:, None])
        o_cmp = jnp.einsum('bghtn,bngd->btghd', p_c.astype(vc.dtype), vc)

        imp = jnp.einsum('bghtn,nj->bgtj', p_c, overlap)
        eligible = slc_starts[None, :] <= t[:, None]
        cur = t // SLC_BLOCK
        forced = (blk_ids[None, :] == 0) | (blk_ids[None, :] == cur[:, None]) | \
                 (blk_ids[None, :] == cur[:, None] - 1)
        score = jnp.where(forced, BIG, jnp.where(eligible, imp, -BIG))
        _, idx = lax.top_k(score, slc_k)
        ks = gather(kb, idx).reshape(B, G, Q_BLOCK, slc_k * SLC_BLOCK, d)
        vs = gather(vb, idx).reshape(B, G, Q_BLOCK, slc_k * SLC_BLOCK, d)
        kpos = (idx[..., None] * SLC_BLOCK + jnp.arange(SLC_BLOCK)).reshape(B, G, Q_BLOCK, slc_k * SLC_BLOCK)
        mask_s = (kpos <= t[None, None, :, None])[:, :, None]
        logit_s = jnp.einsum('btghd,bgtkd->bghtk', qrg, ks) * scale
        p_s = masked_softmax(logit_s, mask_s)
        o_slc = jnp.einsum('bghtk,bgtkd->btghd', p_s.astype(vs.dtype), vs)

        kw = lax.dynamic_slice_in_dim(k_win_pad, s0, Q_BLOCK + WINDOW, axis=1)
        vw = lax.dynamic_slice_in_dim(v_win_pad, s0, Q_BLOCK + WINDOW, axis=1)
        wpos = s0 - WINDOW + jnp.arange(Q_BLOCK + WINDOW)
        mask_w = (wpos[None, :] <= t[:, None]) & (wpos[None, :] > t[:, None] - WINDOW) & (wpos[None, :] >= 0)
        logit_w = jnp.einsum('btghd,bkgd->bghtk', qrg, kw) * scale
        p_w = masked_softmax(logit_w, mask_w)
        o_win = jnp.einsum('bghtk,bkgd->btghd', p_w.astype(vw.dtype), vw)

        out = gb[..., 0:1] * o_cmp + gb[..., 1:2] * o_slc + gb[..., 2:3] * o_win
        return out.reshape(B, Q_BLOCK, NSA_WIDTH)

    return map_query_blocks(block, S)

def diff_attention(q, k, v, positions, lq1, lk1, lq2, lk2, subln_g, lambda_init):
    B, S = q.shape[:2]
    scale = HEAD_DIM ** -0.5
    q = rope(q, positions)
    k = rope(k, positions)
    lam = (jnp.exp(jnp.sum(lq1 * lk1).astype(jnp.float32))
           - jnp.exp(jnp.sum(lq2 * lk2).astype(jnp.float32)) + lambda_init)
    kpos = jnp.arange(S)

    def block(i):
        s0 = i * Q_BLOCK
        t = s0 + jnp.arange(Q_BLOCK)
        qb = lax.dynamic_slice_in_dim(q, s0, Q_BLOCK, axis=1)
        logits = jnp.einsum('bthd,bshd->bhts', qb, k) * scale
        p = masked_softmax(logits, kpos[None, :] <= t[:, None])
        p = p.reshape(B, DIFF_HEADS, 2, Q_BLOCK, S)
        a = p[:, :, 0] - lam * p[:, :, 1]
        o = jnp.einsum('bhts,bshe->bthe', a.astype(v.dtype), v)
        o = rmsnorm(o, subln_g) * (1.0 - lambda_init)
        return o.reshape(B, Q_BLOCK, DIFF_WIDTH)

    return map_query_blocks(block, S)

def chunked_sgu(uv, norm_g, w_s, b_s):
    B, S = uv.shape[:2]
    z = jax.nn.gelu(uv)
    u, v = z[..., :SGU_WIDTH], z[..., SGU_WIDTH:]
    v = rmsnorm(v, norm_g).reshape(B, S // SGU_CHUNK, SGU_CHUNK, SGU_GROUPS, SGU_GROUP_DIM)
    causal = jnp.tril(jnp.ones((SGU_CHUNK, SGU_CHUNK), dtype=bool))
    w = jnp.where(causal[None], w_s, 0.0)
    s = jnp.einsum('gts,bnsgc->bntgc', w, v) + b_s.T[:, :, None]
    return u * s.reshape(B, S, SGU_WIDTH)

def second_inputs(seed: int = 0) -> dict:
    key = jax.random.key(seed)
    ks = iter(jax.random.split(key, 40))
    L, D, d = DEPTH, D_MODEL, HEAD_DIM

    def normal(shape, scale):
        return jax.random.normal(next(ks), shape, jnp.float32) * scale

    def gain(shape):
        return 1.0 + normal(shape, 0.05)

    x = normal((BATCH, SEQ, D), 1.0)
    offset = jax.random.randint(next(ks), (BATCH, 1), 0, 4096, dtype=jnp.int32)
    positions = offset + jnp.arange(SEQ, dtype=jnp.int32)[None, :]
    return {
        "x": x,
        "positions": positions,
        "attn_norm": gain((L, D)),
        "w_in": normal((L, D, D_IN), D ** -0.5),
        "cmp_pos_k": normal((L, CMP_BLOCK, d), 0.1),
        "cmp_k_w1": normal((L, CMP_BLOCK * d, CMP_HIDDEN), (CMP_BLOCK * d) ** -0.5),
        "cmp_k_w2": normal((L, CMP_HIDDEN, d), CMP_HIDDEN ** -0.5),
        "cmp_pos_v": normal((L, CMP_BLOCK, d), 0.1),
        "cmp_v_w1": normal((L, CMP_BLOCK * d, CMP_HIDDEN), (CMP_BLOCK * d) ** -0.5),
        "cmp_v_w2": normal((L, CMP_HIDDEN, d), CMP_HIDDEN ** -0.5),
        "diff_lq1": normal((L, d), 0.1),
        "diff_lk1": normal((L, d), 0.1),
        "diff_lq2": normal((L, d), 0.1),
        "diff_lk2": normal((L, d), 0.1),
        "diff_subln": gain((L, DIFF_V_DIM)),
        "sgu_norm": gain((L, SGU_WIDTH)),
        "sgu_w": normal((L, SGU_GROUPS, SGU_CHUNK, SGU_CHUNK), 0.5 * SGU_CHUNK ** -0.5),
        "sgu_b": 1.0 + normal((L, SGU_GROUPS, SGU_CHUNK), 0.1),
        "w_branch_a": normal((L, NSA_WIDTH, D), NSA_WIDTH ** -0.5),
        "w_branch_b": normal((L, DIFF_WIDTH, D), DIFF_WIDTH ** -0.5),
        "w_branch_c": normal((L, SGU_WIDTH, D), SGU_WIDTH ** -0.5),
        "w_merge": normal((L, D, N_BRANCHES * D), D ** -0.5),
        "b_merge": normal((L, N_BRANCHES * D), 0.02),
        "w_out": normal((L, D, D), D ** -0.5),
        "ffn_norm": gain((L, D)),
        "w_ffn1": normal((L, D, D_FF), D ** -0.5),
        "w_ffn3": normal((L, D, D_FF), D ** -0.5),
        "w_ffn2": normal((L, D_FF, D), D_FF ** -0.5),
        "final_norm": gain((D,)),
    }

def second_block(x, positions, attn_norm, w_in, cmp_pos_k, cmp_k_w1, cmp_k_w2, cmp_pos_v, cmp_v_w1,
              cmp_v_w2, diff_lq1, diff_lk1, diff_lq2, diff_lk2, diff_subln, sgu_norm, sgu_w, sgu_b,
              w_branch_a, w_branch_b, w_branch_c, w_merge, b_merge, w_out, ffn_norm, w_ffn1,
              w_ffn3, w_ffn2, final_norm):
    B, S, D = x.shape
    for l in range(DEPTH):
        lambda_init = 0.8 - 0.6 * math.exp(-0.3 * l)
        h = rmsnorm(x, attn_norm[l])
        proj = h @ w_in[l]
        q_a, kv_a, g_a, q_b, k_b, v_b, uv_c = jnp.split(proj, IN_OFFSETS, axis=-1)
        k_cmp, v_cmp, k_slc, v_slc, k_win, v_win = [
            t.reshape(B, S, NSA_KV_GROUPS, HEAD_DIM) for t in jnp.split(kv_a, 6, axis=-1)]
        o_a = nsa_attention(q_a.reshape(B, S, NSA_HEADS, HEAD_DIM), k_cmp, v_cmp, k_slc, v_slc,
                            k_win, v_win, jax.nn.sigmoid(g_a).reshape(B, S, NSA_HEADS, 3), positions,
                            cmp_pos_k[l], cmp_k_w1[l], cmp_k_w2[l], cmp_pos_v[l], cmp_v_w1[l], cmp_v_w2[l])
        o_b = diff_attention(q_b.reshape(B, S, 2 * DIFF_HEADS, HEAD_DIM),
                             k_b.reshape(B, S, 2 * DIFF_HEADS, HEAD_DIM),
                             v_b.reshape(B, S, DIFF_HEADS, DIFF_V_DIM), positions,
                             diff_lq1[l], diff_lk1[l], diff_lq2[l], diff_lk2[l], diff_subln[l], lambda_init)
        o_c = chunked_sgu(uv_c, sgu_norm[l], sgu_w[l], sgu_b[l])
        gates = jax.nn.sigmoid(h @ w_merge[l] + b_merge[l]).reshape(B, S, N_BRANCHES, D)
        mixed = (gates[:, :, 0] * (o_a @ w_branch_a[l])
                 + gates[:, :, 1] * (o_b @ w_branch_b[l])
                 + gates[:, :, 2] * (o_c @ w_branch_c[l]))
        x = x + mixed @ w_out[l]
        h = rmsnorm(x, ffn_norm[l])
        x = x + (jax.nn.silu(h @ w_ffn1[l]) * (h @ w_ffn3[l])) @ w_ffn2[l]
    return rmsnorm(x, final_norm)


def setup_inputs(seed=0):
    out = dict(first_inputs(seed))
    for name, value in second_inputs(seed + 1).items():
        if name != "x":
            out[name + "_2"] = value
    return out


def reference(
    x, mem, w_mem_kv, conv_w_in, conv_dw_w, conv_dw_b, conv_ln_g, conv_ln_b, moba_w_in, w_o,
    ln1_g, ln1_b, w_rg, b_rg, w_re, b_re, w_gate, w_up, w_down, ln2_g, ln2_b, positions_2,
    attn_norm_2, w_in_2, cmp_pos_k_2, cmp_k_w1_2, cmp_k_w2_2, cmp_pos_v_2, cmp_v_w1_2,
    cmp_v_w2_2, diff_lq1_2, diff_lk1_2, diff_lq2_2, diff_lk2_2, diff_subln_2, sgu_norm_2,
    sgu_w_2, sgu_b_2, w_branch_a_2, w_branch_b_2, w_branch_c_2, w_merge_2, b_merge_2, w_out_2,
    ffn_norm_2, w_ffn1_2, w_ffn3_2, w_ffn2_2, final_norm_2,
):
    x = first_block(
        x, mem, w_mem_kv, conv_w_in, conv_dw_w, conv_dw_b, conv_ln_g, conv_ln_b, moba_w_in, w_o,
        ln1_g, ln1_b, w_rg, b_rg, w_re, b_re, w_gate, w_up, w_down, ln2_g, ln2_b,
    )
    return second_block(
        x, positions_2, attn_norm_2, w_in_2, cmp_pos_k_2, cmp_k_w1_2, cmp_k_w2_2, cmp_pos_v_2,
        cmp_v_w1_2, cmp_v_w2_2, diff_lq1_2, diff_lk1_2, diff_lq2_2, diff_lk2_2, diff_subln_2,
        sgu_norm_2, sgu_w_2, sgu_b_2, w_branch_a_2, w_branch_b_2, w_branch_c_2, w_merge_2,
        b_merge_2, w_out_2, ffn_norm_2, w_ffn1_2, w_ffn3_2, w_ffn2_2, final_norm_2,
    )


_drawn_inputs = setup_inputs


def setup_inputs(seed=0):
    import zlib

    import numpy as np

    out = dict(_drawn_inputs(seed))
    spreads = {}
    factors = {'conv_ln_g': 5.135,
     'conv_ln_b': 3.993,
     'b_rg': 7.473,
     'b_re': 5.455,
     'cmp_pos_k_2': 34.195,
     'cmp_pos_v_2': 3.013,
     'diff_lk1_2': 5.392,
     'diff_lk2_2': 22.432,
     'sgu_norm_2': 7.36,
     'b_merge_2': 8.0,
     'diff_subln_2': 2.715}
    for name, (base, spread) in spreads.items():
        noise = np.random.default_rng([zlib.crc32(name.encode()), seed]).standard_normal(out[name].shape)
        drawn = base * np.exp(spread * noise) if base else spread * noise
        out[name] = __import__('jax').numpy.asarray(drawn.astype(out[name].dtype))
    for name, factor in factors.items():
        out[name] = (out[name] * factor).astype(out[name].dtype)
    return out
```

```python
import math
import numpy as np
import concourse.bass as bass
from concourse import mybir
from contextlib import ExitStack

F = mybir.dt.float32
I32 = mybir.dt.int32
ACT = mybir.ActivationFunctionType
ALU = mybir.AluOpType
AX = mybir.AxisListType

D = 1024
T = 256
ALPHA = 4 ** 0.25
NRING = 7
UNIT = 4096
SCALE = 64 ** -0.5
NEG = -1e30
CAP = 64
D_FF = 2816


def constants():
    c = {}
    p = np.arange(128)
    c["ident"] = np.eye(128)
    c["ones"] = np.ones((128, 128))
    c["before"] = (p[:, None] < p[None, :]).astype(float)
    c["upto"] = (p[:, None] <= p[None, :]).astype(float)
    c["cmask"] = np.where(p[None, :] <= p[:, None], 0.0, NEG)
    perm = np.zeros((128, 128))
    for m in range(128):
        if m % 64 < 32:
            perm[m + 32, m] = -1.0
        else:
            perm[m - 32, m] = 1.0
    c["perm"] = perm
    c["iota"] = np.tile(np.arange(128), (128, 1))
    c["rev4"] = np.tile(np.arange(4, 0, -1), (128, 1))
    c["rev8"] = np.tile(np.arange(8, 0, -1), (128, 1))
    half = np.float32(10000.0) ** (-(np.arange(32, dtype=np.float32)) / np.float32(32))
    c["freq"] = half.astype(np.float32)[p % 32][:, None]
    n = np.arange(32)
    ok = np.stack([(n[None, :] < 15) & (n[None, :] * 16 + 31 <= (t * 128 + p)[:, None]) for t in range(2)], 1)
    c["m01"] = ok.reshape(128, 64).astype(float)
    c["madd"] = np.where(ok, 0.0, NEG).reshape(128, 64)
    at, cols = {}, []
    k = 0
    for name, a in c.items():
        at[name] = (k, a.shape[1])
        cols.append(a.astype(np.float32))
        k += a.shape[1]
    return at, np.ascontiguousarray(np.concatenate(cols, 1))


class Op:

    def __init__(self, eng, fn, deps):
        self.eng, self.fn, self.deps = eng, fn, deps
        self.sig = False
        self.n = 0


class Group:

    def __init__(self, sem, base=0):
        self.sem, self.total = sem, base


class Queues:

    def __init__(self, sems):
        self.sems = sems
        self.q = {e: [] for e in ("pe", "act", "dve", "pool", "sp")}
        self.last = {}
        self.fences = {e: [] for e in self.q}

    def add(self, eng, fn, deps=(), chain=False):
        deps = [d for d in deps if d is not None] + self.fences[eng]
        self.fences[eng] = []
        if chain and eng in self.last:
            deps.append(self.last[eng])
        for d in deps:
            if isinstance(d, Op):
                d.sig = True
        op = Op(eng, fn, deps)
        self.q[eng].append(op)
        self.last[eng] = op
        return op

    def pe(self, fn, *deps):
        return self.add("pe", fn, deps)

    def act(self, fn, *deps):
        return self.add("act", fn, deps, True)

    def dve(self, fn, *deps):
        return self.add("dve", fn, deps, True)

    def pool(self, fn, *deps):
        return self.add("pool", fn, deps, True)

    def dma(self, eng, group, out, in_, *deps):
        deps = [d for d in deps if d is not None]
        for d in deps:
            if isinstance(d, Op):
                d.sig = True
        op = Op(eng, lambda e, s=group.sem: e.dma_start(out, in_).then_inc(s, 16), [*deps])
        op.n = -1
        self.q[eng].append(op)
        group.total += 16

    def fence(self):
        for e in ("pe", "act", "dve", "pool"):
            self.fences[e] = [o for x, o in self.last.items() if x != e]

    def number(self):
        for ops in self.q.values():
            n = 0
            for o in ops:
                if o.sig:
                    n += 1
                    o.n = n

    def emit(self, eng, e):
        seen = {}
        for o in self.q[eng]:
            need = {}
            for d in o.deps:
                if isinstance(d, Op):
                    s, v = self.sems[d.eng], d.n
                elif isinstance(d, Group):
                    s, v = d.sem, d.total
                else:
                    s, v = d
                k = id(s)
                if seen.get(k, 0) < v and need.get(k, (s, 0))[1] < v:
                    need[k] = (s, v)
            for k, (s, v) in need.items():
                e.wait_ge(s, v)
                seen[k] = v
            ins = o.fn(e)
            if o.sig:
                ins.then_inc(self.sems[eng], 1)


class Bank:

    def __init__(self, ap):
        self.ap, self.free = ap, None


class Unit:

    def __init__(self, ap, got):
        self.ap, self.got, self.free = ap, got, None


def program(nc, I, out, stop=99):
    at, _ = constants()
    ctx = ExitStack()
    with ctx:
        def sb(name, n, dt=F):
            return ctx.enter_context(nc.sbuf_tensor(name, [128, n], dt))

        sems = {e: ctx.enter_context(nc.semaphore("s_" + e)) for e in ("pe", "act", "dve", "pool", "sp")}
        Q = Queues(sems)
        pe, act, dve, pool = Q.pe, Q.act, Q.dve, Q.pool
        nsem = [0]

        def group():
            nsem[0] += 1
            return Group(ctx.enter_context(nc.semaphore(f"d{nsem[0]}")))

        ring = sb("ring", NRING * UNIT)
        rsem = [ctx.enter_context(nc.semaphore(f"r{i}")) for i in range(NRING)]
        units = []

        def load(src, a, n):
            i = len(units)
            k = i % NRING
            ap = ring[:, k * UNIT:k * UNIT + a * n].rearrange("p (a n) -> p a n", a=a)
            u = Unit(ap, (rsem[k], 16 * (i // NRING + 1)))
            prev = units[i - NRING] if i >= NRING else None
            deps = []
            if prev is not None:
                prev.free.sig = True
                deps = [prev.free]
            g = Group(rsem[k])
            Q.dma("sp", g, ap, src, *deps)
            units.append(u)
            return u

        def major(w, n0, n1):
            return w.rearrange("(p c) n -> p c n", p=128)[:, :, n0:n1]

        X = sb("X", 2048)[:, :].rearrange("p (t d) -> p t d", t=2)
        XT = sb("XT", 2048)[:, :].rearrange("p (c t) -> p c t", c=8)
        GB = sb("GB", 2048)[:, :].rearrange("p (g d) -> p g d", g=2)
        _, cst_np = constants()
        CST = sb("CST", cst_np.shape[1])
        AR = sb("AR", 12800)
        SM = sb("SM", 512)
        VT = sb("VT", 132)
        NRM = sb("NRM", 32)
        WR = sb("WR", 2 * 8 * 36)
        BR = sb("BR", 72)
        W2 = sb("W2", 512)
        LAM = AR[:, 6144:6656]
        CS = sb("CS", 512)
        MK = sb("MK", 1024)[:, :].rearrange("p (j h m) -> p j h m", j=2, h=2)
        MV = sb("MV", 512)[:, :].rearrange("p (k d) -> p k d", k=2)
        FLAG = sb("FLAG", 2, I32)
        ps = ctx.enter_context(nc.psum_tensor("ps", [128, 8, 512], F))
        banks = [Bank(ps[:, i, :]) for i in range(8)]
        turn = [0]
        held = [0]

        def hold(n):
            held[0] = n

        def bank():
            turn[0] += 1
            return banks[turn[0] % (8 - held[0])]

        def C(name):
            k, n = at[name]
            return CST[:, k:k + n]

        smn = [0]

        def small(n):
            if smn[0] + n > 512:
                smn[0] = 0
            a = SM[:, smn[0]:smn[0] + n]
            smn[0] += n
            return a

        def area(k, n):
            return AR[:, k:k + n]

        def tr(out, in_, *deps):
            k = in_.shape[0]
            return pe(lambda e: e.transpose(out, in_, C("ident")[0:k, 0:k]), *deps)

        def mm(out, l, r, start, stop, *deps):
            return pe(lambda e: e.matmul(out, l, r, start=start, stop=stop), *deps)

        def vcopy(out, in_, *deps):
            return dve(lambda e: e.tensor_copy(out, in_), *deps)

        def acopy(out, in_, *deps):
            return act(lambda e: e.activation(out, in_, ACT.Copy), *deps)

        def pcopy(out, in_, *deps):
            return pool(lambda e: e.tensor_copy(out, in_), *deps)

        cp = [0]

        def copy(out, in_, *deps):
            cp[0] += 1
            return (vcopy if cp[0] % 2 else acopy)(out, in_, *deps)

        def tt(out, a, b, op, *deps):
            return dve(lambda e: e.tensor_tensor(out, a, b, op), *deps)

        def ts(out, a, s1, s2, op0, op1, *deps):
            return dve(lambda e: e.tensor_scalar(out, a, s1, s2, op0, op1) if op1 is not None
                       else e.tensor_scalar(out, a, s1, None, op0), *deps)

        def stt(out, a, s, b, op0, op1, *deps):
            return dve(lambda e: e.scalar_tensor_tensor(out, a, s, b, op0, op1), *deps)

        def fn(out, in_, f, *deps, bias=0.0, scale=1.0, acc=None):
            if acc is None:
                return act(lambda e: e.activation(out, in_, f, bias=bias, scale=scale), *deps)
            return act(lambda e: e.activation(out, in_, f, bias=bias, scale=scale, accum_out=acc), *deps)

        def rmax(out, in_, *deps):
            return dve(lambda e: e.reduce_max(out, in_, AX.X), *deps)

        def rsum(out, in_, *deps):
            return dve(lambda e: e.reduce_sum(out, in_, AX.X), *deps)

        def recip(out, in_, *deps):
            return dve(lambda e: e.reciprocal(out, in_), *deps)

        def bc(a, shape):
            return a.broadcast_to(shape)

        def mid(a, k):
            return a.unsqueeze(1).broadcast_to([a.shape[0], k, a.shape[1]])

        def end(a, k):
            return a.unsqueeze(len(a.shape)).broadcast_to([*a.shape, k])

        def rsqrt(out, v, scale, eps, *deps):
            n = v.shape[1]
            w, y, t = small(n), out, small(n)
            ts(w, v, scale, eps, ALU.mult, ALU.add, *deps)
            dve(lambda e: e.tensor_scalar(t.bitcast(I32), w.bitcast(I32), 1, None, ALU.logical_shift_right))
            dve(lambda e: e.tensor_scalar(y.bitcast(I32), t.bitcast(I32), -1.0, 1597463007.0, ALU.mult, ALU.add))
            for _ in range(3):
                tt(t, y, y, ALU.mult)
                stt(t, t, -0.5, w, ALU.mult, ALU.mult)
                o = stt(y, t, 1.5, y, ALU.add, ALU.mult)
            return o

        g0, g1, g2 = group(), group(), group()
        Q.dma("act", g0, CST[:, :], I["cst"])
        Q.dma("act", g0, X, I["x"][0].rearrange("(t p) d -> p t d", p=128))
        MEM = area(0, 2048).rearrange("p (t d) -> p t d", t=2)
        Q.dma("act", g0, MEM, I["mem"][0].rearrange("(t p) d -> p t d", p=128))
        VR = area(2048, 128)
        PR = area(2176, 128)
        DWR = area(2304, 768)
        ISB = area(3072, 256)
        for k, (name, n) in enumerate((("conv_dw_b", 6), ("conv_ln_g", 6), ("conv_ln_b", 6))):
            Q.dma("act", g1, VR[6 * k:6 * k + 6, :], I[name].rearrange("a (j p) -> (a j) p", p=128))
        Q.dma("act", g1, VR[18:66, :], I["b_merge_2"].rearrange("l (j p) -> (l j) p", p=128))
        Q.dma("act", g1, VR[66:68, :], I["diff_subln_2"])
        for k, name in enumerate(("cmp_pos_k_2", "cmp_pos_v_2")):
            Q.dma("act", g1, PR[32 * k:32 * k + 32, :], I[name].rearrange("l (j i) d -> (l j) (i d)", i=2))
        Q.dma("act", g1, DWR[0:31, :], I["conv_dw_w"][0])
        for l in range(2):
            Q.dma("act", g1, NRM[:, 8 * l:8 * l + 8], I["attn_norm_2"][l].rearrange("(p c) -> p c", c=8))
            Q.dma("act", g1, NRM[:, 16 + 8 * l:24 + 8 * l], I["ffn_norm_2"][l].rearrange("(p c) -> p c", c=8))
            w = WR[:, 288 * l:288 * l + 288].rearrange("p (c n) -> p c n", c=8)
            Q.dma("act", g1, w[:, :, 0:4], major(I["w_rg"][l], 0, 4))
            Q.dma("act", g1, w[:, :, 4:36], major(I["w_re"][l], 0, 32))
            Q.dma("act", g1, BR[:, 36 * l:36 * l + 4], I["b_rg"][l].partition_broadcast(128))
            Q.dma("act", g1, BR[:, 36 * l + 4:36 * l + 36], I["b_re"][l].partition_broadcast(128))
            for k, name in enumerate(("cmp_k_w2_2", "cmp_v_w2_2")):
                Q.dma("act", g2, W2[:, 256 * l + 128 * k:256 * l + 128 * k + 128].rearrange("p (c d) -> p c d", c=2),
                      I[name][l].rearrange("(c p) d -> p c d", p=128))
            for k, name in enumerate(("diff_lq1_2", "diff_lk1_2", "diff_lq2_2", "diff_lk2_2")):
                o = 256 * l + 64 * k
                Q.dma("act", g2, LAM[:, o:o + 64], I[name][l].partition_broadcast(128))
        IS = ISB.bitcast(I32)
        Q.dma("act", g2, IS, I["positions_2"][0].partition_broadcast(128))

        def load_gb(g, b, *deps):
            gr = group()
            Q.dma("act", gr, GB[:, 0, :], g.partition_broadcast(128), *deps)
            if b is not None:
                Q.dma("act", gr, GB[:, 1, :], b.partition_broadcast(128), *deps)
            return gr

        gb = load_gb(I["ln1_g"][0], I["ln1_b"][0])

        def transposed(dst, src, *deps, norm=None):
            o = None
            for t in range(2):
                sv = src[:, t, :].rearrange("p (d c) -> p c d", c=8)
                for c0 in (0, 4):
                    b = bank()
                    for c in range(4):
                        o = tr(b.ap[:, c * 128:c * 128 + 128], sv[:, c0 + c, :], b.free, *deps)
                    pv = b.ap.rearrange("p (c t) -> p c t", c=4)
                    if norm is None:
                        b.free = copy(dst[:, c0:c0 + 4, t * 128:t * 128 + 128], pv, o)
                    else:
                        b.free = tt(dst[:, c0:c0 + 4, t * 128:t * 128 + 128], pv,
                                    end(norm[:, c0:c0 + 4], 128), ALU.mult, o)
            return Q.last["dve"], Q.last["act"]

        def feat(u, n0, src, *deps, nk=8, b=None, half=0, done=True):
            b = b or bank()
            for c in range(nk):
                o = mm(b.ap[:, half * 256:half * 256 + 256], u.ap[:, c, n0:n0 + 128], src[:, c, :],
                       c == 0, c == nk - 1, b.free, u.got, *deps)
            u.free = o
            return b, o

        def toks(u, n0, n, t, src, *deps, nk=8):
            b = bank()
            for c in range(nk):
                o = mm(b.ap[:, 0:n], src[:, c, t * 128:t * 128 + 128], u.ap[:, c, n0:n0 + n],
                       c == 0, c == nk - 1, b.free, u.got, *deps)
            u.free = o
            return b, o

        def stats(t, src, *deps):
            st, mv = small(12), small(2)
            for k in range(2):
                dve(lambda e, k=k: e.bn_stats(st[:, 6 * k:6 * k + 6], src[:, t, 512 * k:512 * k + 512]), *deps)
            dve(lambda e: e.bn_aggr(mv, st.rearrange("p (g s) -> p g s", g=2)))
            return mv

        def layer_norm(gr):
            for t in range(2):
                mv = stats(t, X)
                r = small(1)
                rsqrt(r, mv[:, 1:2], 1.0, 1e-5)
                ts(X[:, t, :], X[:, t, :], mv[:, 0:1], r, ALU.subtract, ALU.mult)
                if t:
                    tt(X[:, t, :], X[:, t, :], GB[:, 0, :], ALU.mult, gr)
                    o = tt(X[:, t, :], X[:, t, :], GB[:, 1, :], ALU.add)
                else:
                    o = Q.last["dve"]
                    pool(lambda e: e.tensor_tensor(X[:, 0, :], X[:, 0, :], GB[:, 0, :], ALU.mult), gr, o)
                    o2 = pool(lambda e: e.tensor_tensor(X[:, 0, :], X[:, 0, :], GB[:, 1, :], ALU.add))
            return o, o2

        Pb = [None, None]
        PTb = [None]
        pbfree = [None, None]
        ptfree = [None]
        pbn = [0]

        def scores(q, kp, causal, gate, lam, *deps):
            i = pbn[0] % 2
            pbn[0] += 1
            P = Pb[i]
            last = []
            for t in range(2):
                ks = 128 * (t + 1) if causal else 256
                b = bank()
                S = b.ap[:, 0:2 * ks].rearrange("p (h k) -> p h k", h=2)
                o = mm(S, q[:, t * 128:t * 128 + 128], kp[:, :, 0:ks], True, True, b.free, *deps)
                m, nm, sm, r = small(2), small(2), small(2), small(2)
                if causal:
                    d = S[:, :, ks - 128:ks]
                    tt(d, d, mid(C("cmask"), 2), ALU.add, o)
                rmax(m, S, o)
                o = ts(nm, m, -SCALE, None, ALU.mult, None)
                for h in range(2):
                    e = fn(P[:, t, h, 0:ks], S[:, h, :], ACT.Exp, o, pbfree[i], bias=nm[:, h:h + 1],
                           scale=SCALE, acc=sm[:, h:h + 1])
                b.free = e
                o = recip(r, sm, e)
                if gate is not None:
                    o = tt(r, r, gate[:, t, :], ALU.mult)
                if lam is None:
                    pv = P[:, t, :, 0:ks]
                    o = pool(lambda e, pv=pv, r=r, ks=ks: e.tensor_tensor(pv, pv, end(r, ks), ALU.mult), o)
                else:
                    o = tt(r[:, 1:2], r[:, 1:2], lam, ALU.mult)
                    pool(lambda e, v=P[:, t, 0, 0:ks], r=r: e.tensor_scalar(v, v, r[:, 0:1], None, ALU.mult), o)
                    o = dve(lambda e, a=P[:, t, 1, 0:ks], c=P[:, t, 0, 0:ks], r=r:
                            e.scalar_tensor_tensor(c, a, r[:, 1:2], c, ALU.mult, ALU.add), Q.last["pool"])
                last.append(o)
            return i, P, last, causal

        def turned(st, heads=2):
            i, P, last, causal = st
            PT = PTb[0]
            for t in range(2):
                nk = t + 1 if causal else 2
                b = bank()
                for h in range(heads):
                    for k in range(nk):
                        o = tr(b.ap[:, (h * nk + k) * 128:(h * nk + k) * 128 + 128],
                               P[:, t, h, k * 128:k * 128 + 128], b.free, last[t])
                b.free = copy(PT[:, 0:heads, 0:nk, t * 128:t * 128 + 128],
                              b.ap[:, 0:heads * nk * 128].rearrange("p (h k t) -> p h k t", h=heads, k=nk),
                              o, ptfree[0])
            pbfree[i] = o
            return PT, [Q.last["dve"], Q.last["act"]], causal

        def values(pt, v, b, first, lastone, *deps, heads=2):
            PT, got, causal = pt
            for h in range(heads):
                ob = b.ap[64 * h:64 * h + 64, :] if heads == 2 else b.ap
                for k in range(2):
                    t0 = 128 * k if causal else 0
                    o = mm(ob[:, t0:256], v(k, h), PT[:, h, k, t0:256], first and k == 0,
                           lastone and k == 1, b.free, *got, *deps)
            ptfree[0] = o
            return o

        def attend(jobs):
            pend = None
            for j in [*jobs, None]:
                st = scores(*j[0]) if j else None
                if pend:
                    pst, pj = pend
                    pj[1](turned(pst, pj[2] if len(pj) > 2 else 2))
                pend = (st, j)

        cst = dve(lambda e: e.memset(MK, 0.0), g0)
        act(lambda e: e.activation(small(1), C("ones")[:, 0:1], ACT.Copy), g0)
        MT = area(3328, 2048).rearrange("p (c t) -> p c t", c=8)
        transposed(MT, MEM, g0)
        u = load(major(I["w_mem_kv"], 0, 512), 8, 512)
        dv, da = Q.last["dve"], Q.last["act"]
        for j in range(2):
            b, o = feat(u, j * 128, MT, dv, da)
            vcopy(MK[0:64, j, 0, :], b.ap[0:64, 0:256], o)
            b.free = vcopy(MK[64:128, j, 1, :], b.ap[64:128, 0:256])
        for t in range(2):
            b, o = toks(u, 256, 256, t, MT)
            b.free = acopy(MV[:, t, :], b.ap[:, 0:256], o)
        b = bank()
        o = tr(b.ap[:, 0:68], VR[0:68, :], b.free, g1)
        o = tr(b.ap[:, 68:132], PR[0:64, :])
        b.free = vcopy(VT[:, 0:132], b.ap[:, 0:132], o)
        b = bank()
        for j in range(6):
            o = tr(b.ap[:, j * 31:j * 31 + 31], DWR[0:31, j * 128:j * 128 + 128], b.free)
        DW = area(12600, 186)
        b.free = vcopy(DW, b.ap[:, 0:186], o)
        ang, kk = area(5376, 256), area(5632, 256)
        vcopy(ang, IS, g2)
        ts(ang, ang, C("freq"), None, ALU.mult, None)
        ts(kk, ang, 1.0 / (2 * math.pi), 12582912.0, ALU.mult, ALU.add)
        ts(kk, kk, -12582912.0, None, ALU.add, None)
        c1 = 6.28125
        c2 = float(np.float32(np.round((2 * math.pi - c1) * 2 ** 20) / 2 ** 20))
        c3 = float(np.float32(2 * math.pi - c1 - c2))
        for c in (c1, c2, c3):
            stt(ang, kk, -c, ang, ALU.mult, ALU.add)
        pi = float(np.nextafter(np.float32(math.pi), np.float32(0)))
        ts(ang, ang, pi, -pi, ALU.min, ALU.max)
        ts(kk, ang, math.pi / 2, -2 * math.pi, ALU.is_gt, ALU.mult)
        stt(kk, ang, math.pi / 2, kk, ALU.add, ALU.add)
        ts(kk, kk, pi, -pi, ALU.min, ALU.max)
        COS, SIN = CS[:, 0:256], CS[:, 256:512]
        o = Q.last["dve"]
        fn(COS, kk, ACT.Sin, o)
        fn(SIN, ang, ACT.Sin)
        LN_ = small(2)
        NLAM = sb("NLAM", 2)[:, :]
        lp = area(5888, 256).rearrange("p (l k d) -> p l k d", l=2, k=2)
        lv = LAM.rearrange("p (l k q d) -> p l k q d", l=2, k=2, q=2)
        tt(lp, lv[:, :, :, 0, :], lv[:, :, :, 1, :], ALU.mult, g2)
        ls = small(4)
        o = rsum(ls, lp.rearrange("p l k d -> p (l k) d"))
        le = small(4)
        o = fn(le, ls, ACT.Exp, o)
        l4 = le.rearrange("p (l k) -> p l k", k=2)
        tt(NLAM, l4[:, :, 1], l4[:, :, 0], ALU.subtract, o)
        for l in range(2):
            ts(NLAM[:, l:l + 1], NLAM[:, l:l + 1], -(0.8 - 0.6 * math.exp(-0.3 * l)), None, ALU.add, None)
        transposed(XT, X)
        Q.fence()

        YT = area(0, 2048).rearrange("p (c t) -> p c t", c=8)
        Pb[:] = [area(2048 + 1024 * i, 1024).rearrange("p (t h k) -> p t h k", t=2, h=2) for i in range(2)]
        PTb[:] = [area(4096, 1024).rearrange("p (h k t) -> p h k t", h=2, k=2)]
        QM = area(5120, 512).rearrange("p (j t) -> p j t", j=2)

        def mem_jobs():
            jobs = []
            for j in range(2):
                def fin(pt, j=j):
                    b = bank()
                    o = values(pt, lambda k, h: MV[:, k, j * 128 + h * 64:j * 128 + h * 64 + 64], b, True, True)
                    b.free = copy(YT[:, 6 + j, :], b.ap[:, 0:256], o)
                jobs.append(((QM[:, j, :], MK[:, j, :, :], False, None, None), fin))
            return jobs

        def conv_mix():
            HP = area(5632, 1716).rearrange("p (j t) -> p j t", j=6)
            A = area(7348, 1536).rearrange("p (j t) -> p j t", j=6)
            HC = area(8884, 1536).rearrange("p (j t) -> p j t", j=6)
            G = area(10420, 512)
            dve(lambda e: e.memset(HP[:, :, 0:30], 0.0))
            w = I["conv_w_in"][0]
            u = None
            gf = [None, None]
            for n in range(14):
                if n % 4 == 0:
                    wd = min(512, 1792 - n * 128)
                    u = load(major(w, n * 128, n * 128 + wd), 8, wd)
                b, o = feat(u, (n % 4) * 128, XT)
                pv = b.ap[:, 0:256]
                if n < 6:
                    b.free = copy(A[:, n, :], pv, o)
                elif n < 12:
                    j = n - 6
                    g = G[:, (j % 2) * 256:(j % 2) * 256 + 256]
                    o = b.free = fn(g, pv, ACT.Sigmoid, o, gf[j % 2])
                    gf[j % 2] = tt(HP[:, j, 30:286], A[:, j, :], g, ALU.mult, o)
                else:
                    b.free = acopy(QM[:, n - 12, :], pv, o)
            ready = Q.last["dve"]
            dw = DW.rearrange("p (j k) -> p j k", j=6)
            DG = area(11000, 1024).rearrange("p (n m) -> p n m", n=8)
            used = [None] * 8
            cb = [bank() for _ in range(3)]
            for k in range(31):
                for j in range(3, 6):
                    i = (k * 3 + j) % 8
                    o = fn(DG[:, i, :], C("ident"), ACT.Identity, used[i], scale=dw[:, j, k:k + 1])
                    used[i] = mm(cb[j - 3].ap[:, 0:256], DG[:, i, :], HP[:, j, k:k + 256], k == 0, k == 30,
                                 cb[j - 3].free, o, ready)
            for k in range(31):
                for j in range(3):
                    if k == 0:
                        ts(HC[:, j, :], HP[:, j, 0:256], dw[:, j, 0:1], VT[:, j:j + 1], ALU.mult, ALU.add)
                    else:
                        dve(lambda e, j=j, k=k: e.scalar_tensor_tensor(
                            HC[:, j, :], HP[:, j, k:k + 256], dw[:, j, k:k + 1], HC[:, j, :], ALU.mult, ALU.add))
            for j in range(3, 6):
                cb[j - 3].free = fn(HC[:, j, :], cb[j - 3].ap[:, 0:256], ACT.Identity, used[(30 * 3 + j) % 8],
                                    bias=VT[:, j:j + 1])
            both = [Q.last["dve"], Q.last["act"]]
            b = bank()
            for j in range(6):
                o = mm(b.ap[:, 0:256], C("ones"), HC[:, j, :], j == 0, j == 5, b.free, *both)
            mu = area(7348, 256)
            b.free = ts(mu, b.ap[:, 0:256], 1.0 / 768, None, ALU.mult, None, o)
            tt(HC, HC, mid(mu, 6), ALU.subtract)
            sq = area(5632, 1536).rearrange("p (j t) -> p j t", j=6)
            o = fn(sq, HC, ACT.Square, Q.last["dve"], *both)
            b = bank()
            for j in range(6):
                o2 = mm(b.ap[:, 0:256], C("ones"), sq[:, j, :], j == 0, j == 5, b.free, o)
            sd = area(7604, 256)
            b.free = ts(sd, b.ap[:, 0:256], 1.0 / 768, 1e-5, ALU.mult, ALU.add, o2)
            o = fn(sd, sd, ACT.Sqrt, b.free)
            recip(mu, sd, o)
            o = tt(HC, HC, mid(mu, 6), ALU.mult)
            for j in range(6):
                fn(YT[:, j, :], HC[:, j, :], ACT.Silu, o, bias=VT[:, 12 + j:13 + j], scale=VT[:, 6 + j:7 + j])
            attend(mem_jobs())

        def moba_mix():
            QQ = area(5632, 1536).rearrange("p (j t) -> p j t", j=6)
            KP = area(7168, 3072).rearrange("p (j h t) -> p j h t", j=6, h=2)
            V = area(10240, 1536).rearrange("p (t d) -> p t d", t=2)
            dve(lambda e: e.memset(KP, 0.0))
            w = I["moba_w_in"][0]
            for n in range(12):
                if n % 4 == 0:
                    u = load(major(w, n * 128, n * 128 + 512), 8, 512)
                b, o = feat(u, (n % 4) * 128, XT)
                if n < 6:
                    b.free = acopy(QQ[:, n, :], b.ap[:, 0:256], o)
                else:
                    vcopy(KP[0:64, n - 6, 0, :], b.ap[0:64, 0:256], o)
                    b.free = vcopy(KP[64:128, n - 6, 1, :], b.ap[64:128, 0:256])
            u = load(major(w, 1536, 2048), 8, 512)
            for t in range(2):
                b, o = toks(u, 0, 512, t, XT)
                b.free = copy(V[:, t, 0:512], b.ap, o)
            u = load(major(w, 2048, 2560), 8, 512)
            for t in range(2):
                b, o = toks(u, 0, 256, t, XT)
                b.free = copy(V[:, t, 512:768], b.ap[:, 0:256], o)
            for j in range(2):
                b, o = feat(u, 256 + j * 128, XT)
                b.free = acopy(QM[:, j, :], b.ap[:, 0:256], o)
            ins = [Q.last["dve"], Q.last["act"]]
            jobs = []
            for j in range(6):
                def fin(pt, j=j):
                    b = bank()
                    o = values(pt, lambda k, h: V[:, k, j * 128 + h * 64:j * 128 + h * 64 + 64], b, True, True)
                    b.free = copy(YT[:, j, :], b.ap[:, 0:256], o)
                jobs.append(((QQ[:, j, :], KP[:, j, :, :], True, None, None, *ins), fin))
            attend(jobs + mem_jobs())

        baton = [ctx.enter_context(nc.semaphore(f"f{i}")) for i in range(64)]

        def beyond(l, pos, comb, flag, main):
            ACC = area(0, 2048).rearrange("p (t d) -> p t d", t=2)
            XF = area(2048, 1024).rearrange("p (c s) -> p c s", c=8)
            PQ = area(3072, 128)
            PW = area(3200, 128)
            WB = area(4096, 2048)
            G = area(6144, 256).rearrange("p (t s) -> p t s", t=2)
            GW = area(6400, 256).rearrange("p (t s) -> p t s", t=2)
            CT = area(6656, 256).rearrange("p (t s) -> p t s", t=2)
            H = area(8192, 512)
            HT = area(8704, 512).rearrange("p (c s) -> p c s", c=4)
            Y = area(9216, 1024)
            B = [b.ap for b in banks]
            pq = PQ.rearrange("p (w t e) -> p w t e", w=2, t=2)
            flat = [PQ.rearrange("p (q e) -> p q e", e=32), PW.rearrange("p (q e) -> p q e", e=32)]
            gate = I["w_gate"][l].rearrange("g e (p c) n -> (g e) p c n", p=128)
            upw = I["w_up"][l].rearrange("g e (p c) n -> (g e) p c n", p=128)
            dn = I["w_down"][l].rearrange("g e (p c) n -> (g e) p c n", p=128)

            def one():
                st = []

                def step(eng):
                    return lambda f: st.append((eng, f))

                @step("dve")
                def _(e, i):
                    for t in range(2):
                        r = e.tensor_scalar(G[:, t, :], C("iota"), pq[:, 0, t, 0:1], None, ALU.is_equal)
                    return r

                @step("dve")
                def _(e, i):
                    for t in range(2):
                        r = e.tensor_scalar(GW[:, t, :], G[:, t, :], pq[:, 1, t, 0:1], None, ALU.mult)
                    return r

                @step("pe")
                def _(e, i):
                    for c in range(8):
                        for t in range(2):
                            r = e.matmul(B[c // 4][:, (c % 4) * 128:(c % 4) * 128 + 128],
                                         X[:, t, :].rearrange("p (d c) -> p c d", c=8)[:, c, :], G[:, t, :],
                                         start=t == 0, stop=t == 1)
                    for t in range(2):
                        r = e.transpose(B[2][:, t * 128:t * 128 + 128], GW[:, t, :], C("ident"))
                    return r

                @step("dve")
                def _(e, i):
                    for k in range(2):
                        e.tensor_copy(XF[:, 4 * k:4 * k + 4, :], B[k].rearrange("p (c s) -> p c s", c=4))
                    return e.tensor_copy(CT, B[2][:, 0:256].rearrange("p (t s) -> p t s", t=2))

                for w, b in ((gate, 3), (upw, 4)):
                    for hf in range(2):
                        wv = WB.rearrange("p (c n) -> p c n", c=4)

                        @step("act dma")
                        def _(e, i, w=w, hf=hf, wv=wv):
                            return e.dma_start(wv, w[bass.ds(i, 1), :, 4 * hf:4 * hf + 4, :]
                                               .rearrange("a p c n -> (a p) c n"))

                        @step("pe")
                        def _(e, i, b=b, hf=hf, wv=wv):
                            for c in range(4):
                                r = e.matmul(B[b], XF[:, 4 * hf + c, :], wv[:, c, :],
                                             start=hf == 0 and c == 0, stop=hf == 1 and c == 3)
                            return r

                @step("act")
                def _(e, i):
                    return e.activation(H, B[3], ACT.Silu)

                @step("dve")
                def _(e, i):
                    return e.tensor_tensor(H, H, B[4], ALU.mult)

                @step("pe")
                def _(e, i):
                    for c in range(4):
                        r = e.transpose(B[5][:, c * 128:c * 128 + 128], H.rearrange("p (f c) -> p c f", c=4)[:, c, :],
                                        C("ident"))
                    return r

                @step("dve")
                def _(e, i):
                    return e.tensor_copy(HT, B[5].rearrange("p (c s) -> p c s", c=4))

                for hf in range(2):
                    wv = WB.rearrange("p (c n) -> p c n", c=2)

                    @step("act dma")
                    def _(e, i, hf=hf, wv=wv):
                        return e.dma_start(wv, dn[bass.ds(i, 1), :, 2 * hf:2 * hf + 2, :]
                                           .rearrange("a p c n -> (a p) c n"))

                    @step("pe")
                    def _(e, i, hf=hf, wv=wv):
                        for c in range(2):
                            for n in range(2):
                                r = e.matmul(B[6 + n], HT[:, 2 * hf + c, :], wv[:, c, n * 512:n * 512 + 512],
                                             start=hf == 0 and c == 0, stop=hf == 1 and c == 1)
                        return r

                @step("dve")
                def _(e, i):
                    for n in range(2):
                        r = e.tensor_copy(Y[:, n * 512:n * 512 + 512], B[6 + n])
                    return r

                @step("pe")
                def _(e, i):
                    for n in range(2):
                        for t in range(2):
                            r = e.matmul(B[2 * n + t], CT[:, t, :], Y[:, n * 512:n * 512 + 512], start=True, stop=True)
                    return r

                @step("dve")
                def _(e, i):
                    for n in range(2):
                        for t in range(2):
                            a = ACC[:, t, n * 512:n * 512 + 512]
                            r = e.tensor_tensor(a, a, B[2 * n + t], ALU.add)
                    return r

                @step("dve")
                def _(e, i):
                    e.tensor_copy(flat[1][:, :, 0:31], flat[0][:, :, 1:32])
                    return e.tensor_copy(flat[1][:, :, 31:32], flat[0][:, :, 0:1])

                @step("dve")
                def _(e, i):
                    return e.tensor_copy(PQ, PW)

                return st

            steps = one()

            def walk(me):
                def body(e, i):
                    for k, (eng, f) in enumerate(steps):
                        if eng.split()[0] != me:
                            continue
                        if k:
                            by = 16 if "dma" in steps[k - 1][0] else 1
                            e.wait_ge(baton[k - 1], by)
                            e.sem_clear(baton[k - 1])
                        f(e, i).then_inc(baton[k], 16 if "dma" in eng else 1)
                    if me == "dve":
                        e.wait_ge(baton[len(steps) - 1], 1)
                        e.sem_clear(baton[len(steps) - 1])

                def own(e, f):
                    f().then_inc(baton[63], 1)
                    e.wait_ge(baton[63], 1)
                    e.sem_clear(baton[63])

                def run(e):
                    v = e.value_load(FLAG[0:1, l:l + 1], min_val=0, max_val=1)
                    with e.If(v > 0):
                        for r in range(2):
                            if me == "dve":
                                if r == 0:
                                    own(e, lambda: e.tensor_scalar(pq[:, 0], pos, -float(CAP), None, ALU.add))
                                    own(e, lambda: e.tensor_copy(pq[:, 1], comb))
                                else:
                                    own(e, lambda: e.tensor_scalar(pq[:, 0], pq[:, 0], -128.0, None, ALU.add))
                            with e.Fori(0, 32) as i:
                                body(e, i)
                return run

            for me in ("dve", "pe", "act"):
                for o in (flag, *main):
                    o.sig = True
                Q.q[me].append(Op(me, walk(me), [flag, *main]))

        def moe(l, gr_next):
            ACC = area(0, 2048).rearrange("p (t d) -> p t d", t=2)
            XG = [area(2048 + 2048 * i, 2048).rearrange("p (c s) -> p c s", c=8) for i in range(2)]
            G = area(6144, 512).rearrange("p (t s) -> p t s", t=2)
            GW = area(6656, 512).rearrange("p (t s) -> p t s", t=2)
            CT = [area(7168 + 512 * i, 512).rearrange("p (q t) -> p q t", q=2) for i in range(2)]
            H = area(8192, 512)
            HT = area(8704, 512).rearrange("p (c s) -> p c s", c=4)
            Y = area(9216, 1024)
            RT = area(10240, 2048)
            rn = [0]

            def rt(*shape):
                n = int(np.prod(shape))
                a = RT[:, rn[0]:rn[0] + n]
                rn[0] += n
                if len(shape) == 1:
                    return a
                names = "abcd"[:len(shape)]
                return a.rearrange(f"p ({' '.join(names)}) -> p {' '.join(names)}",
                                   **{k: v for k, v in zip(names[:-1], shape[:-1])})

            L = rt(2, 36)
            wr = WR[:, 288 * l:288 * l + 288].rearrange("p (c n) -> p c n", c=8)
            b = bank()
            for t in range(2):
                for c in range(8):
                    o = mm(b.ap[:, t * 36:t * 36 + 36], XT[:, c, t * 128:t * 128 + 128], wr[:, c, :],
                           c == 0, c == 7, b.free)
            b.free = tt(L, b.ap[:, 0:72].rearrange("p (t n) -> p t n", t=2),
                        mid(BR[:, 36 * l:36 * l + 36], 2), ALU.add, o)

            def onehot(lg, rev, n):
                m, k, km, oh = rt(2), rt(2, n), rt(2), rt(2, n)
                rmax(m, lg)
                tt(k, lg, end(m, n), ALU.is_equal)
                tt(k, k, mid(rev, 2), ALU.mult)
                rmax(km, k)
                tt(oh, k, end(km, n), ALU.is_equal)
                return m, oh

            lg = L[:, :, 0:4]
            gm, og = onehot(lg, C("rev4"), 4)
            eg = rt(2, 4)
            o = tt(eg, lg, end(gm, 4), ALU.subtract)
            o = fn(eg, eg, ACT.Exp, o)
            gw = rt(2)
            rsum(gw, eg, o)
            recip(gw, gw)
            pr = rt(2, 4, 8)
            og4 = end(og, 8)
            for t in range(2):
                tt(pr[:, t], og4[:, t], L[:, t, 4:36].rearrange("p (g e) -> p g e", g=4), ALU.mult)
            es = rt(2, 8)
            for t in range(2):
                rsum(es[:, t], pr[:, t].rearrange("p g e -> p e g"))
            m1, o1 = onehot(es, C("rev8"), 8)
            es2 = rt(2, 8)
            stt(es2, o1, NEG, es, ALU.mult, ALU.add)
            m2, o2 = onehot(es2, C("rev8"), 8)
            e2, w1, w2, wi, sl = rt(2), rt(2), rt(2), rt(2, 8), rt(2, 8)
            o = tt(e2, m2, m1, ALU.subtract)
            o = fn(e2, e2, ACT.Exp, o)
            ts(w1, e2, 1.0, None, ALU.add, None, o)
            recip(w1, w1)
            tt(w1, w1, gw, ALU.mult)
            tt(w2, w1, e2, ALU.mult)
            tt(sl, o1, o2, ALU.add)
            tt(o1, o1, end(w1, 8), ALU.mult)
            tt(o2, o2, end(w2, 8), ALU.mult)
            tt(wi, o1, o2, ALU.add)
            comb, sel, pos = rt(2, 32), rt(2, 32), rt(2, 32)
            for t in range(2):
                for dst, s in ((comb, wi), (sel, sl)):
                    o = tt(dst[:, t].rearrange("p (g e) -> p g e", g=4), og4[:, t], mid(s[:, t], 4), ALU.mult)
            b = bank()
            mm(b.ap[:, 0:32], C("before"), sel[:, 0, :], True, True, b.free, o)
            mm(b.ap[:, 32:64], C("ones"), sel[:, 0, :], True, False)
            mm(b.ap[:, 32:64], C("before"), sel[:, 1, :], False, True)
            mm(b.ap[:, 64:96], C("ones"), sel[:, 0, :], True, False)
            o = mm(b.ap[:, 64:96], C("ones"), sel[:, 1, :], False, True)
            ts(pos, b.ap[:, 0:64].rearrange("p (t e) -> p t e", t=2), 1.0, None, ALU.add, None, o)
            tt(pos, pos, sel, ALU.mult)
            ts(pos, pos, -1.0, None, ALU.add, None)
            cm = small(1)
            b.free = rmax(cm, b.ap[:, 64:96])
            ts(cm, cm, float(CAP), None, ALU.is_gt, None)
            flag = vcopy(FLAG[:, l:l + 1], cm)

            xgfree, ctfree = [None, None], [None, None]
            gfree = [None]

            def gather(g):
                i = g % 2
                for t in range(2):
                    tt(G[:, t].rearrange("p (e s) -> p e s", e=4), mid(C("iota")[:, 0:CAP], 4),
                       end(pos[:, t, 4 * g:4 * g + 4], CAP), ALU.is_equal, gfree[0])
                    o = tt(GW[:, t].rearrange("p (e s) -> p e s", e=4), G[:, t].rearrange("p (e s) -> p e s", e=4),
                           end(comb[:, t, 4 * g:4 * g + 4], CAP), ALU.mult)
                for c in range(0, 8, 2):
                    b = bg
                    for k in range(2):
                        for t in range(2):
                            sv = X[:, t, :].rearrange("p (d c) -> p c d", c=8)[:, c + k, :]
                            o2 = mm(b.ap[:, k * 256:k * 256 + 256], sv, G[:, t, :], t == 0,
                                    t == 1, b.free, o)
                    b.free = copy(XG[i][:, c:c + 2, :], b.ap.rearrange("p (k s) -> p k s", k=2), o2, xgfree[i])
                b = bg
                for q in range(2):
                    for t in range(2):
                        o2 = tr(b.ap[:, (q * 2 + t) * 128:(q * 2 + t) * 128 + 128],
                                GW[:, t, q * 128:q * 128 + 128], b.free)
                gfree[0] = o2
                b.free = copy(CT[i], b.ap.rearrange("p (q t) -> p q t", q=2), o2, ctfree[i])
                return [Q.last["dve"], Q.last["act"]]

            bG, bU, bT, bY0, bY1, bO0, bO1, bg = banks

            hfree = [None]
            yfree = [None]
            htfree = [None]

            def up(pair, got):
                i, s0 = (pair // 2) % 2, (pair % 2) * 128
                W = []
                for w in ("w_gate", "w_up"):
                    W.append([load(major(I[w][l, (2 * pair + x) // 8, (2 * pair + x) % 8], 0, 512), 8, 512)
                              for x in range(2)])
                for k, b in ((0, bG), (1, bU)):
                    for c in range(8):
                        for x in range(2):
                            o = mm(b.ap[64 * x:64 * x + 64, :], XG[i][:, c, s0 + 64 * x:s0 + 64 * x + 64],
                                   W[k][x].ap[:, c, :], c == 0, c == 7, b.free, W[k][x].got, *got)
                    for x in range(2):
                        W[k][x].free = o
                    if k == 0:
                        a = bG.free = fn(H, bG.ap, ACT.Silu, o, hfree[0])
                bU.free = tt(H, H, bU.ap, ALU.mult, o, a)
                if pair % 2:
                    xgfree[i] = o
                return bU.free

            def down(pair, h):
                hv = H.rearrange("p (f c) -> p c f", c=4)
                for c in range(4):
                    o = tr(bT.ap[:, c * 128:c * 128 + 128], hv[:, c, :], bT.free, h)
                hfree[0] = o
                bT.free = ht = vcopy(HT, bT.ap.rearrange("p (c s) -> p c s", c=4), o, htfree[0])
                W = []
                for x in range(2):
                    e = 2 * pair + x
                    W.append(load(I["w_down"][l, e // 8, e % 8].rearrange("(p c) n -> p c n", p=128), 4, 1024))
                ys = []
                for n, b in enumerate((bY0, bY1)):
                    for c in range(4):
                        for x in range(2):
                            o = mm(b.ap[64 * x:64 * x + 64, :], HT[:, c, 64 * x:64 * x + 64],
                                   W[x].ap[:, c, n * 512:n * 512 + 512], c == 0, c == 3, b.free, W[x].got, ht)
                    b.free = (acopy if n == 0 else vcopy)(Y[:, n * 512:n * 512 + 512], b.ap, o, yfree[0])
                    ys.append(b.free)
                htfree[0] = o
                W[0].free = W[1].free = o
                return ys

            def scatter(pair, ys):
                i = (pair // 2) % 2
                for n in range(2):
                    for t in range(2):
                        b = (bO0, bO1)[t]
                        o = mm(b.ap, CT[i][:, pair % 2, t * 128:t * 128 + 128], Y[:, n * 512:n * 512 + 512],
                               True, True, b.free, *ys)
                        a = ACC[:, t, n * 512:n * 512 + 512]
                        if pair == 0:
                            b.free = vcopy(a, b.ap, o)
                        else:
                            b.free = tt(a, a, b.ap, ALU.add, o)
                yfree[0] = o
                if pair % 2:
                    ctfree[i] = o

            got = gather(0)
            nxt = None
            ys = None
            for pair in range(16):
                h = up(pair, got)
                if pair:
                    scatter(pair - 1, ys)
                if pair % 2 == 0 and pair < 14:
                    nxt = gather(pair // 2 + 1)
                if pair % 2:
                    got = nxt
                ys = down(pair, h)
            scatter(15, ys)
            beyond(l, pos, comb, flag, [Q.last[x] for x in ("pe", "act", "dve")])
            for t in range(2):
                stt(X[:, t, :], X[:, t, :], ALPHA, ACC[:, t, :], ALU.mult, ALU.add)
            return layer_norm(gr_next)

        def rms_t(dst, norm, *deps):
            J = area(3072, 1024)
            ss, r = small(2), small(2)
            for t in range(2):
                o = fn(J, X[:, t, :], ACT.Square, Q.last["dve"], *deps, acc=ss[:, t:t + 1])
            rsqrt(r, ss, 1.0 / 1024, 1e-6, o)
            J2 = area(4096, 2048).rearrange("p (t d) -> p t d", t=2)
            for t in range(2):
                o = ts(J2[:, t, :], X[:, t, :], r[:, t:t + 1], None, ALU.mult, None)
            transposed(dst, J2, o, norm=norm)

        OT = area(0, 3072).rearrange("p (b c t) -> p b c t", b=3, c=4)

        def rope(raw, dst, tmp, *deps):
            b = bank()
            o = mm(b.ap[:, 0:256], C("perm"), raw, True, True, b.free, *deps)
            b.free = tt(tmp, b.ap[:, 0:256], SIN, ALU.mult, o, *deps)
            tt(dst, raw, COS, ALU.mult)
            return tt(dst, dst, tmp, ALU.add)

        def nsa(l):
            w = I["w_in_2"][l]
            QR = area(8192, 1024).rearrange("p (j t) -> p j t", j=4)
            QQ = area(9216, 1024).rearrange("p (j t) -> p j t", j=4)
            KS = area(10240, 1024).rearrange("p (g h t) -> p g h t", g=2, h=2)
            KW = area(11264, 1024).rearrange("p (g h t) -> p g h t", g=2, h=2)
            VS = area(12288, 256).rearrange("p (k d) -> p k d", k=2)
            VW = area(12544, 256).rearrange("p (k d) -> p k d", k=2)
            BK = area(3072, 480).rearrange("p (j g n) -> p j g n", j=16, g=2)
            BV = area(3552, 480).rearrange("p (j g n) -> p j g n", j=16, g=2)
            HK = area(4032, 256)
            TK = area(4288, 60).rearrange("p (c n) -> p c n", c=2)
            TR = area(4352, 512).rearrange("p (g c r n) -> p g c r n", g=2, c=2, r=4)
            RAW = area(4864, 256)
            TMP = area(6144, 256)
            KC = area(6400, 128).rearrange("p (g h n) -> p g h n", g=2, h=2)
            VC = area(6528, 512).rearrange("p (g r d) -> p g r d", g=2, r=2)
            PC = area(7040, 512)
            PT = area(7552, 512).rearrange("p (g t) -> p g t", g=2)
            GT = small(48).rearrange("p (t n) -> p t n", t=2)
            W2D = area(8064, 128).rearrange("p (h d) -> p h d", h=2)
            for a in (KS, KW, KC, VC, TR):
                dve(lambda e, a=a: e.memset(a, 0.0))
            u = load(major(w, 0, 512), 8, 512)
            for j in range(4):
                b, o = feat(u, j * 128, XT)
                o = b.free = acopy(QR[:, j, :], b.ap[:, 0:256], o)
                rope(QR[:, j, :], QQ[:, j, :], TMP, o)
            u = load(major(w, 512, 1024), 8, 512)
            for k, B in ((0, BK), (1, BV)):
                b, o = feat(u, k * 128, XT)
                bv = b.ap[:, 0:256].rearrange("p (n j i) -> p i j n", j=8, i=2)
                for i in range(2):
                    for g in range(2):
                        for hf in range(2):
                            vcopy(B[64 * i:64 * i + 64, 8 * hf:8 * hf + 8, g, :],
                                  bv[64 * g:64 * g + 64, i, :, hf:hf + 15], o)
                b.free = Q.last["dve"]
                pv = VT[:, 68 + 32 * k + 16 * l:84 + 32 * k + 16 * l]
                for g in range(2):
                    tt(B[:, :, g, :], B[:, :, g, :], end(pv, 15), ALU.add)

            def keys(u, n0, K, dep=None):
                b, o = feat(u, n0, XT)
                o = b.free = acopy(RAW, b.ap[:, 0:256], o, dep)
                rope(RAW, TMP2, TMP, o)
                for g in range(2):
                    for h in range(2):
                        o = vcopy(K[64 * h:64 * h + 64, g, h, :], TMP2[64 * g:64 * g + 64, :])
                return o

            TMP2 = area(5120, 256)
            o = keys(u, 256, KS)
            for t in range(2):
                b, o2 = toks(u, 384, 128, t, XT)
                b.free = acopy(VS[:, t, :], b.ap[:, 0:128], o2)
            u = load(major(w, 1024, 1304), 8, 280)
            keys(u, 0, KW, o)
            for t in range(2):
                b, o2 = toks(u, 128, 152, t, XT)
                acopy(VW[:, t, :], b.ap[:, 0:128], o2)
                b.free = fn(GT[:, t, :], b.ap[:, 128:152], ACT.Sigmoid)
            for k, (B, name) in enumerate(((BK, "cmp_k_w1_2"), (BV, "cmp_v_w1_2"))):
                u = load(I[name][l].rearrange("(j p) n -> p j n", p=128), 16, 256)
                b = bank()
                for j in range(16):
                    o = mm(b.ap[0:30, 0:256], B[:, j].rearrange("p g n -> p (g n)"), u.ap[:, j, :],
                           j == 0, j == 15, b.free, u.got, Q.last["dve"])
                u.free = o
                o = b.free = fn(HK[0:30, :], b.ap[0:30, 0:256], ACT.Gelu_apprx_tanh, o, Q.last["pe"])
                b = bank()
                for c in range(2):
                    o = tr(b.ap[:, c * 30:c * 30 + 30], HK[0:30, c * 128:c * 128 + 128], b.free, o)
                w2 = W2[:, 256 * l + 128 * k:256 * l + 128 * k + 128].rearrange("p (c d) -> p c d", c=2)
                if k == 0:
                    b.free = vcopy(TK, b.ap[:, 0:60].rearrange("p (c n) -> p c n", c=2), o)
                    hk = b.free
                    b = bank()
                    for c in range(2):
                        for h in range(2):
                            o = vcopy(W2D[:, h, :], w2[:, c, :], Q.last["pe"])
                        o = mm(b.ap[:, 0:30], W2D.rearrange("p h d -> p (h d)"), TK[:, c, :], c == 0, c == 1,
                               b.free, o)
                    for h in range(2):
                        vcopy(KC[64 * h:64 * h + 64, :, h, 0:15],
                              b.ap[64 * h:64 * h + 64, 0:30].rearrange("p (g n) -> p g n", g=2), o)
                    b.free = Q.last["dve"]
                else:
                    for c in range(2):
                        for g in range(2):
                            vcopy(TR[:, g, c, :, 0:15], mid(b.ap[:, c * 30 + g * 15:c * 30 + g * 15 + 15], 4), o)
                    b.free = Q.last["dve"]
                    b = bank()
                    for g in range(2):
                        for c in range(2):
                            o = mm(b.ap[:, g * 64:g * 64 + 64], TR[:, g, c].rearrange("p r n -> p (r n)"),
                                   w2[:, c, :], c == 0, c == 1, b.free, Q.last["dve"])
                    for g in range(2):
                        for r in range(4):
                            q0 = 32 * r
                            vcopy(VC[q0:q0 + 32, g, r // 2, (r % 2) * 64:(r % 2) * 64 + 64],
                                  b.ap[q0:q0 + 32, g * 64:g * 64 + 64], o)
                    b.free = Q.last["dve"]
            for t in range(2):
                b = bank()
                for j in range(4):
                    o = mm(b.ap[:, j * 64:j * 64 + 64], QR[:, j, t * 128:t * 128 + 128],
                           KC[:, j // 2].rearrange("p h n -> p (h n)"), True, True, b.free, Q.last["dve"])
                P = PC[:, t * 256:t * 256 + 256].rearrange("p (h n) -> p h n", h=8)
                b.free = tt(P, b.ap[:, 0:256].rearrange("p (h n) -> p h n", h=8),
                            mid(C("madd")[:, t * 32:t * 32 + 32], 8), ALU.add, o)
                m, sm = small(8), small(8)
                rmax(m, P)
                o = tt(P, P, end(m, 32), ALU.subtract)
                o = fn(P, P, ACT.Exp, o, scale=SCALE)
                rsum(sm, P if t else P, o)
                recip(sm, sm)
                tt(sm, sm, GT[:, t, :].rearrange("p (h b) -> p h b", b=3)[:, :, 0], ALU.mult)
                tt(P, P, end(sm, 32), ALU.mult)
                tt(P, P, mid(C("m01")[:, t * 32:t * 32 + 32], 8), ALU.mult)
            o = Q.last["dve"]
            b = bank()
            for g in range(2):
                for t in range(2):
                    o = tr(b.ap[:, g * 256 + t * 128:g * 256 + t * 128 + 128],
                           PC[:, t * 256 + g * 128:t * 256 + g * 128 + 128], b.free, o)
            b.free = vcopy(PT, b.ap.rearrange("p (g t) -> p g t", g=2), o)
            Q.fence()
            gt = GT.rearrange("p t (h b) -> p t h b", b=3)
            jobs = []
            ob = [None]
            for j in range(4):
                for br, (K, V) in ((1, (KS, VS)), (2, (KW, VW))):
                    def fin(pt, j=j, br=br, V=V):
                        if br == 1:
                            ob[0] = banks_o[j % 2]
                        b = ob[0]
                        o = values(pt, lambda k, h: V[:, k, (j // 2) * 64:(j // 2) * 64 + 64], b, br == 1, False)
                        if br == 2:
                            o = mm(b.ap[:, 0:256], VC[:, j // 2, j % 2, :], PT[:, j // 2, :], False, True)
                            b.free = copy(OT[:, 0, j, :], b.ap[:, 0:256], o)
                    jobs.append(((QQ[:, j, :], K[:, j // 2], True, gt[:, :, 2 * j:2 * j + 2, br], None), fin))
            hold(2)
            attend(jobs)
            hold(0)

        banks_o = banks[6:8]

        def diff(l):
            w = I["w_in_2"][l]
            QQ = area(8192, 1024).rearrange("p (j t) -> p j t", j=4)
            KP = area(9216, 2048).rearrange("p (j h t) -> p j h t", j=4, h=2)
            V = area(11264, 1024).rearrange("p (k d) -> p k d", k=2)
            RAW, TMP, TMP2 = area(6144, 256), area(6400, 256), area(6656, 256)
            O = area(7168, 1024).rearrange("p (j t) -> p j t", j=4)
            dve(lambda e: e.memset(KP, 0.0))
            rf = None
            for part in range(2):
                u = load(major(w, 1304 + 512 * part, 1816 + 512 * part), 8, 512)
                for j in range(4):
                    b, o = feat(u, j * 128, XT)
                    o = b.free = acopy(RAW, b.ap[:, 0:256], o, rf)
                    if part == 0:
                        rf = rope(RAW, QQ[:, j, :], TMP, o)
                    else:
                        rope(RAW, TMP2, TMP, o)
                        for h in range(2):
                            rf = vcopy(KP[64 * h:64 * h + 64, j, h, :], TMP2[64 * h:64 * h + 64, :])
            u = load(major(w, 2328, 2840), 8, 512)
            for t in range(2):
                b, o = toks(u, 0, 512, t, XT)
                b.free = copy(V[:, t, :], b.ap, o)
            ins = [Q.last["dve"], Q.last["act"]]
            jobs = []
            for j in range(4):
                def fin(pt, j=j):
                    b = bank()
                    o = values(pt, lambda k, h: V[:, k, j * 128:j * 128 + 128], b, True, True, heads=1)
                    b.free = copy(O[:, j, :], b.ap[:, 0:256], o)
                jobs.append(((QQ[:, j, :], KP[:, j], True, None, NLAM[:, l:l + 1], *ins), fin, 1))
            attend(jobs)
            SQ = area(8192, 1024)
            o = fn(SQ, O.rearrange("p j t -> p (j t)"), ACT.Square, Q.last["dve"], Q.last["pe"])
            R = area(9216, 1024)
            for k in range(2):
                b = bank()
                o2 = mm(b.ap, C("ones"), SQ[:, 512 * k:512 * k + 512], True, True, b.free, o)
                b.free = ts(R[:, 512 * k:512 * k + 512], b.ap, 1.0 / 128, 1e-6, ALU.mult, ALU.add, o2)
            o = fn(R, R, ACT.Sqrt, b.free)
            recip(R, R, o)
            tt(O.rearrange("p j t -> p (j t)"), O.rearrange("p j t -> p (j t)"), R, ALU.mult)
            init = 0.8 - 0.6 * math.exp(-0.3 * l)
            ts(OT[:, 1].rearrange("p c t -> p (c t)"), O.rearrange("p j t -> p (j t)"), VT[:, 66 + l:67 + l],
               1.0 - init, ALU.mult, ALU.mult)

        def sgu(l):
            w = I["w_in_2"][l]
            UT = area(8192, 1024).rearrange("p (g t) -> p g t", g=4)
            V = area(9216, 1024).rearrange("p (t d) -> p t d", t=2)
            WG = area(10240, 512).rearrange("p (g s) -> p g s", g=4)
            WT = area(10752, 512).rearrange("p (g t) -> p g t", g=4)
            BS = area(11264, 512)
            NG = area(11776, 512)
            J = area(12288, 512)
            gr = group()
            fr = [Q.last["dve"], Q.last["pe"], Q.last["pool"]]
            Q.dma("act", gr, WG, I["sgu_w_2"][l].rearrange("g t s -> t g s"), *fr)
            Q.dma("act", gr, BS, I["sgu_b_2"][l].rearrange("g t -> (g t)").partition_broadcast(128), *fr)
            Q.dma("act", gr, NG, I["sgu_norm_2"][l].partition_broadcast(128), *fr)
            u = load(major(w, 2840, 3352), 8, 512)
            for j in range(4):
                b, o = feat(u, j * 128, XT)
                b.free = fn(UT[:, j, :], b.ap[:, 0:256], ACT.Gelu_apprx_tanh, o)
            u = load(major(w, 3352, 3864), 8, 512)
            ss, r = small(2), small(2)
            for t in range(2):
                b, o = toks(u, 0, 512, t, XT)
                b.free = fn(V[:, t, :], b.ap, ACT.Gelu_apprx_tanh, o)
                o = fn(J, V[:, t, :], ACT.Square, acc=ss[:, t:t + 1])
            rsqrt(r, ss, 1.0 / 512, 1e-6, o)
            for t in range(2):
                v = stt(V[:, t, :], V[:, t, :], r[:, t:t + 1], NG, ALU.mult, ALU.mult, gr)
            b = bank()
            for g in range(4):
                o = tr(b.ap[:, g * 128:g * 128 + 128], WG[:, g, :], b.free, gr)
            v = b.free = tt(WT, b.ap.rearrange("p (g t) -> p g t", g=4), mid(C("upto"), 4), ALU.mult, o)
            bs = BS.rearrange("p (g t) -> p g t", g=4)
            for g in range(4):
                b = bank()
                for t in range(2):
                    o = mm(b.ap[:, t * 128:t * 128 + 128], V[:, t, g * 128:g * 128 + 128], WT[:, g, :], True, True,
                           b.free, v)
                S = J[:, (g % 2) * 256:(g % 2) * 256 + 256]
                b.free = tt(S.rearrange("p (n t) -> p n t", n=2), b.ap[:, 0:256].rearrange("p (n t) -> p n t", n=2),
                            mid(bs[:, g, :], 2), ALU.add, o)
                tt(OT[:, 2, g, :], S, UT[:, g, :], ALU.mult)

        def merge(l):
            MX = area(3072, 2048).rearrange("p (c t) -> p c t", c=8)
            SG = area(5120, 512).rearrange("p (k t) -> p k t", k=2)
            MB = area(5632, 512).rearrange("p (k t) -> p k t", k=2)
            n = 0
            sf, mf = [None, None], [None, None]
            for br in range(3):
                ub = load(I["w_branch_%s_2" % "abc"[br]][l].rearrange("(c p) n -> p c n", p=128), 4, 1024)
                for j in range(8):
                    if j % 4 == 0:
                        u = load(major(I["w_merge_2"][l], br * 1024 + j * 128, br * 1024 + j * 128 + 512), 8, 512)
                    b, o = feat(u, (j % 4) * 128, XT)
                    k = 18 + 24 * l + 8 * br + j
                    i = n % 2
                    n += 1
                    a = b.free = fn(SG[:, i, :], b.ap[:, 0:256], ACT.Sigmoid, o, sf[i], bias=VT[:, k:k + 1])
                    b, o = feat(ub, j * 128, OT[:, br], nk=4)
                    if br == 0:
                        sf[i] = b.free = tt(MX[:, j, :], b.ap[:, 0:256], SG[:, i, :], ALU.mult, o, a)
                    else:
                        sf[i] = b.free = tt(MB[:, i, :], b.ap[:, 0:256], SG[:, i, :], ALU.mult, o, a, mf[i])
                        mf[i] = pool(lambda e, j=j, i=i: e.tensor_tensor(MX[:, j, :], MX[:, j, :], MB[:, i, :],
                                                                         ALU.add), b.free)
            wo = I["w_out_2"][l].rearrange("(c p) n -> p c n", p=128)
            deps = [Q.last["dve"], Q.last["pool"]]
            for n in range(2):
                u = load(wo[:, :, n * 512:n * 512 + 512], 8, 512)
                for t in range(2):
                    b, o = toks(u, 0, 512, t, MX, *deps)
                    xs = X[:, t, n * 512:n * 512 + 512]
                    b.free = tt(xs, xs, b.ap, ALU.add, o)

        def ffn(l):
            FT = area(0, 5632).rearrange("p (c t) -> p c t", c=22)
            SG = area(6144, 512).rearrange("p (k t) -> p k t", k=2)
            sf = [None, None]
            for n in range(22):
                if n % 4 == 0:
                    wd = min(512, D_FF - n * 128)
                    u1 = load(major(I["w_ffn1_2"][l], n * 128, n * 128 + wd), 8, wd)
                    u3 = load(major(I["w_ffn3_2"][l], n * 128, n * 128 + wd), 8, wd)
                b, o = feat(u1, (n % 4) * 128, XT)
                i = n % 2
                a = b.free = fn(SG[:, i, :], b.ap[:, 0:256], ACT.Silu, o, sf[i])
                b, o = feat(u3, (n % 4) * 128, XT)
                sf[i] = b.free = tt(FT[:, n, :], b.ap[:, 0:256], SG[:, i, :], ALU.mult, o, a)
            w2 = I["w_ffn2_2"][l].rearrange("(c p) n -> p c n", p=128)
            bb = [bank() for _ in range(4)]
            done = Q.last["dve"]
            for c0 in range(0, 22, 4):
                nk = min(4, 22 - c0)
                u = load(w2[:, c0:c0 + nk, :], nk, 1024)
                for t in range(2):
                    for n in range(2):
                        b = bb[2 * t + n]
                        for c in range(nk):
                            o = mm(b.ap, FT[:, c0 + c, t * 128:t * 128 + 128], u.ap[:, c, n * 512:n * 512 + 512],
                                   c0 + c == 0, c0 + c == 21, b.free, u.got, done)
                        if c0 + nk == 22:
                            xs = X[:, t, n * 512:n * 512 + 512]
                            b.free = tt(xs, xs, b.ap, ALU.add, o)
                u.free = o

        def block2():
            for l in range(2):
                if stop == 20 + 10 * l:
                    return
                rms_t(XT, NRM[:, 8 * l:8 * l + 8])
                Q.fence()
                Pb[:] = [area(3072 + 1024 * i, 1024).rearrange("p (t h k) -> p t h k", t=2, h=2) for i in range(2)]
                PTb[:] = [area(5120, 1024).rearrange("p (h k t) -> p h k t", h=2, k=2)]
                nsa(l)
                Q.fence()
                diff(l)
                Q.fence()
                sgu(l)
                Q.fence()
                merge(l)
                if stop == 21 + 10 * l:
                    return
                Q.fence()
                rms_t(XT, NRM[:, 16 + 8 * l:24 + 8 * l])
                Q.fence()
                ffn(l)
                Q.fence()
                if stop == 22 + 10 * l:
                    return
            gr = load_gb(I["final_norm_2"], None, *gbfree)
            ss, r = small(2), small(2)
            J = area(3072, 1024)
            for t in range(2):
                o = fn(J, X[:, t, :], ACT.Square, acc=ss[:, t:t + 1])
            rsqrt(r, ss, 1.0 / 1024, 1e-6, o)
            for t in range(2):
                stt(X[:, t, :], X[:, t, :], r[:, t:t + 1], GB[:, 0, :], ALU.mult, ALU.mult, gr)

        gbfree = []

        def finish():
            og = group()
            last = [Q.last["dve"], Q.last["pool"]]
            Q.dma("sp", og, out.rearrange("a (t p) d -> p (a t) d", p=128), X, *last)
            op = Op("sp", None, [og])
            Q.q["sp"].append(op)
            op.fn = lambda e: e.nop()

        def run():
            nonlocal gb
            for l in range(2):
                (conv_mix if l == 0 else moba_mix)()
                wo = I["w_o"][l].rearrange("(c p) n -> p c n", p=128)
                deps = [Q.last["dve"], Q.last["act"]]
                for n in range(2):
                    u = load(wo[:, :, n * 512:n * 512 + 512], 8, 512)
                    for t in range(2):
                        b, o = toks(u, 0, 512, t, YT, *deps)
                        xs = X[:, t, n * 512:n * 512 + 512]
                        b.free = stt(xs, xs, ALPHA, b.ap, ALU.mult, ALU.add, o)
                ln = layer_norm(gb)
                if stop == 10 * l + 1:
                    return
                gb = load_gb(I["ln2_g"][l], I["ln2_b"][l], *ln)
                transposed(XT, X, *ln)
                Q.fence()
                ln = moe(l, gb)
                if stop == 10 * l + 2:
                    return
                if l == 0:
                    gb = load_gb(I["ln1_g"][1], I["ln1_b"][1], *ln)
                    transposed(XT, X, *ln)
                Q.fence()
            gbfree.extend(ln)
            block2()

        run()
        finish()
        Q.number()
        block = ctx.enter_context(nc.Block())

        @block.sync
        def _(e):
            Q.emit("sp", e)

        @block.tensor
        def _(e):
            Q.emit("pe", e)

        @block.scalar
        def _(e):
            Q.emit("act", e)

        @block.vector
        def _(e):
            Q.emit("dve", e)

        @block.gpsimd
        def _(e):
            Q.emit("pool", e)


NAMES = ["x", "mem", "w_mem_kv", "conv_w_in", "conv_dw_w", "conv_dw_b", "conv_ln_g", "conv_ln_b", "moba_w_in", "w_o",
         "ln1_g", "ln1_b", "w_rg", "b_rg", "w_re", "b_re", "w_gate", "w_up", "w_down", "ln2_g", "ln2_b",
         "positions_2", "attn_norm_2", "w_in_2", "cmp_pos_k_2", "cmp_k_w1_2", "cmp_k_w2_2", "cmp_pos_v_2",
         "cmp_v_w1_2", "cmp_v_w2_2", "diff_lq1_2", "diff_lk1_2", "diff_lq2_2", "diff_lk2_2", "diff_subln_2",
         "sgu_norm_2", "sgu_w_2", "sgu_b_2", "w_branch_a_2", "w_branch_b_2", "w_branch_c_2", "w_merge_2",
         "b_merge_2", "w_out_2", "ffn_norm_2", "w_ffn1_2", "w_ffn3_2", "w_ffn2_2", "final_norm_2"]


def kernel(**inputs):
    import concourse.bacc as bacc
    from concourse.bass_utils import run_bass_kernel_spmd

    nc = bacc.Bacc("TRN2", target_bir_lowering=False, num_devices=1)
    arrays, aps = {}, {}
    for name in NAMES + ["cst"]:
        a = constants()[1] if name == "cst" else np.ascontiguousarray(inputs[name])
        arrays[f"in_{name}"] = a
        aps[name] = nc.dram_tensor(f"in_{name}", a.shape, mybir.dt.from_np(a.dtype), kind="ExternalInput").ap()
    out = nc.dram_tensor("out_x", (1, T, D), F, kind="ExternalOutput").ap()
    program(nc, aps, out)
    r = run_bass_kernel_spmd(nc, [arrays], core_ids=[0])
    return r.results[0]["out_x"]
```

```python
import math
import numpy as np
import concourse.bass as bass
from concourse import mybir
from contextlib import ExitStack

F = mybir.dt.float32
FR = mybir.dt.float32r
I32 = mybir.dt.int32
ACT = mybir.ActivationFunctionType
ALU = mybir.AluOpType
AX = mybir.AxisListType

D = 1024
T = 256
ALPHA = 4 ** 0.25
NRING = 4
NEXTRA = 3
UNIT = 4096
SCALE = 64 ** -0.5
NEG = -1e30
CAP = 64
D_FF = 2816


def constants():
    c = {}
    p = np.arange(128)
    c["ident"] = np.eye(128)
    c["ones"] = np.ones((128, 128))
    c["before"] = (p[:, None] < p[None, :]).astype(float)
    c["upto"] = (p[:, None] <= p[None, :]).astype(float)
    c["cmask"] = np.where(p[None, :] <= p[:, None], 0.0, NEG)
    perm = np.zeros((128, 128))
    for m in range(128):
        if m % 64 < 32:
            perm[m + 32, m] = -1.0
        else:
            perm[m - 32, m] = 1.0
    c["perm"] = perm
    c["iota"] = np.tile(np.arange(128), (128, 1))
    c["rev4"] = np.tile(np.arange(4, 0, -1), (128, 1))
    c["rev8"] = np.tile(np.arange(8, 0, -1), (128, 1))
    half = np.float32(10000.0) ** (-(np.arange(32, dtype=np.float32)) / np.float32(32))
    c["freq"] = half.astype(np.float32)[p % 32][:, None]
    n = np.arange(32)
    ok = np.stack([(n[None, :] < 15) & (n[None, :] * 16 + 31 <= (t * 128 + p)[:, None]) for t in range(2)], 1)
    c["m01"] = ok.reshape(128, 64).astype(float)
    c["madd"] = np.where(ok, 0.0, NEG).reshape(128, 64)
    at, cols = {}, []
    k = 0
    for name, a in c.items():
        at[name] = (k, a.shape[1])
        cols.append(a.astype(np.float32))
        k += a.shape[1]
    return at, np.ascontiguousarray(np.concatenate(cols, 1))


class Op:

    def __init__(self, eng, fn, deps):
        self.eng, self.fn, self.deps = eng, fn, deps
        self.sig = False
        self.n = 0


class Group:

    def __init__(self, sem, base=0):
        self.sem, self.total = sem, base


class Queues:

    def __init__(self, sems):
        self.sems = sems
        self.q = {e: [] for e in ("pe", "act", "dve", "pool", "sp")}
        self.last = {}
        self.fences = {e: [] for e in self.q}

    def add(self, eng, fn, deps=(), chain=False):
        deps = [d for d in deps if d is not None] + self.fences[eng]
        self.fences[eng] = []
        if chain and eng in self.last:
            deps.append(self.last[eng])
        for d in deps:
            if isinstance(d, Op):
                d.sig = True
        op = Op(eng, fn, deps)
        self.q[eng].append(op)
        self.last[eng] = op
        return op

    def pe(self, fn, *deps):
        return self.add("pe", fn, deps)

    def act(self, fn, *deps):
        return self.add("act", fn, deps, True)

    def dve(self, fn, *deps):
        return self.add("dve", fn, deps, True)

    def pool(self, fn, *deps):
        return self.add("pool", fn, deps, True)

    def dma(self, eng, group, out, in_, *deps):
        deps = [d for d in deps if d is not None]
        for d in deps:
            if isinstance(d, Op):
                d.sig = True
        op = Op(eng, lambda e, s=group.sem: e.dma_start(out, in_).then_inc(s, 16), [*deps])
        op.n = -1
        self.q[eng].append(op)
        group.total += 16

    def fence(self):
        for e in ("pe", "act", "dve", "pool"):
            self.fences[e] = [o for x, o in self.last.items() if x != e]

    def number(self):
        for ops in self.q.values():
            n = 0
            for o in ops:
                if o.sig:
                    n += 1
                    o.n = n

    def emit(self, eng, e):
        seen = {}
        for o in self.q[eng]:
            need = {}
            for d in o.deps:
                if isinstance(d, Op):
                    s, v = self.sems[d.eng], d.n
                elif isinstance(d, Group):
                    s, v = d.sem, d.total
                else:
                    s, v = d
                k = id(s)
                if seen.get(k, 0) < v and need.get(k, (s, 0))[1] < v:
                    need[k] = (s, v)
            for k, (s, v) in need.items():
                e.wait_ge(s, v)
                seen[k] = v
            ins = o.fn(e)
            if o.sig:
                ins.then_inc(self.sems[eng], 1)


class Bank:

    def __init__(self, ap):
        self.ap, self.free = ap, None


class Unit:

    def __init__(self, ap, got):
        self.ap, self.got, self.free = ap, got, None


def program(nc, I, out, stop=99):
    at, _ = constants()
    ctx = ExitStack()
    with ctx:
        def sb(name, n, dt=F):
            return ctx.enter_context(nc.sbuf_tensor(name, [128, n], dt))

        sems = {e: ctx.enter_context(nc.semaphore("s_" + e)) for e in ("pe", "act", "dve", "pool", "sp")}
        Q = Queues(sems)
        pe, act, dve, pool = Q.pe, Q.act, Q.dve, Q.pool
        nsem = [0]

        def group():
            nsem[0] += 1
            return Group(ctx.enter_context(nc.semaphore(f"d{nsem[0]}")))

        class Slot:

            def __init__(self, ap, i):
                self.ap, self.sem, self.n, self.unit = ap, ctx.enter_context(nc.semaphore(f"r{i}")), 0, None
                self.after = []

        ring = [Slot(sb(f"ring{i}", UNIT)[:, :], i) for i in range(NRING)]
        extra = [Slot(None, NRING + i) for i in range(NEXTRA)]
        order = [0]

        def load(src, a, n, slots=None):
            slots = slots or ring
            sl = slots[order[0] % len(slots)]
            order[0] += 1
            ap = sl.ap[:, 0:a * n].rearrange("p (a n) -> p a n", a=a)
            sl.n += 16
            u = Unit(ap, (sl.sem, sl.n))
            deps = sl.after
            if sl.unit is not None:
                deps = [*deps, sl.unit.free]
            Q.dma("sp", Group(sl.sem), ap, src, *deps)
            sl.unit, sl.after = u, []
            return u

        def scope(*spec):
            with ExitStack() as s2:
                return [s2.enter_context(nc.sbuf_tensor(name, [128, n], dt)) for name, n, dt in spec]

        def major(w, n0, n1):
            return w.rearrange("(p c) n -> p c n", p=128)[:, :, n0:n1]

        X = sb("X", 2048)[:, :].rearrange("p (t d) -> p t d", t=2)
        XTH = sb("XTH", 2048, FR)[:, :].rearrange("p (c t) -> p c t", c=8)
        XTL = sb("XTL", 2048, FR)[:, :].rearrange("p (c t) -> p c t", c=8)
        XS = (XTH, XTL)
        _, cst_np = constants()
        CST = sb("CST", cst_np.shape[1])
        SM = sb("SM", 512)
        VT = sb("VT", 132)
        NRM = sb("NRM", 32)
        WR = sb("WR", 2 * 8 * 36)
        BR = sb("BR", 72)
        W2 = sb("W2", 512)
        CS = sb("CS", 512)
        FLAG = sb("FLAG", 2, I32)
        NLAM = sb("NLAM", 2)[:, :]
        ps = ctx.enter_context(nc.psum_tensor("ps", [128, 8, 512], F))
        banks = [Bank(ps[:, i, :]) for i in range(8)]
        turn = [0]
        held = [0]

        def hold(n):
            held[0] = n

        def bank():
            turn[0] += 1
            return banks[turn[0] % (8 - held[0])]

        def C(name):
            k, n = at[name]
            return CST[:, k:k + n]

        smn = [0]

        def small(n):
            if smn[0] + n > 512:
                smn[0] = 0
            a = SM[:, smn[0]:smn[0] + n]
            smn[0] += n
            return a

        DW = sb("DW", 186)[:, :]
        b1 = ctx.enter_context(ExitStack())
        GB, MK, MV = [b1.enter_context(nc.sbuf_tensor(name, [128, n], F))
                      for name, n in (("GB", 2048), ("MK", 1024), ("MV", 512))]
        GB = GB[:, :].rearrange("p (g d) -> p g d", g=2)
        MK = MK[:, :].rearrange("p (j h m) -> p j h m", j=2, h=2)
        MV = MV[:, :].rearrange("p (k d) -> p k d", k=2)
        NCV = 2
        tens = {}

        def mix_scope(tag, n, ny, rest):
            spec = [(f"WH{tag}{i}", 2048, FR) for i in range(NCV)] + [(f"WL{tag}{i}", 2048, FR) for i in range(NCV)]
            t = scope(*spec, (f"YH{tag}", ny, FR), (f"YL{tag}", ny, FR), (f"AR{tag}", n, F))
            tens["W"] = [(t[i], t[NCV + i]) for i in range(NCV)]
            tens["Y"] = t[2 * NCV:2 * NCV + 2]
            tens["A"] = t[-1]
            tens["rest"] = rest
            cvfree[:] = [None] * NCV

        cvfree = [None] * NCV

        def area(k, n):
            k -= tens.get("off", 0)
            return tens["A"][:, k:k + n]

        def tr(out, in_, *deps):
            k = in_.shape[0]
            return pe(lambda e: e.transpose(out, in_, C("ident")[0:k, 0:k]), *deps)

        def mm(out, l, r, start, stop, *deps):
            return pe(lambda e: e.matmul(out, l, r, start=start, stop=stop), *deps)

        def vcopy(out, in_, *deps):
            return dve(lambda e: e.tensor_copy(out, in_), *deps)

        def acopy(out, in_, *deps):
            return act(lambda e: e.activation(out, in_, ACT.Copy), *deps)

        def pcopy(out, in_, *deps):
            return pool(lambda e: e.tensor_copy(out, in_), *deps)

        cp = [0]

        def copy(out, in_, *deps):
            cp[0] += 1
            return (vcopy if cp[0] % 2 else acopy)(out, in_, *deps)

        def tt(out, a, b, op, *deps):
            return dve(lambda e: e.tensor_tensor(out, a, b, op), *deps)

        def ts(out, a, s1, s2, op0, op1, *deps):
            return dve(lambda e: e.tensor_scalar(out, a, s1, s2, op0, op1) if op1 is not None
                       else e.tensor_scalar(out, a, s1, None, op0), *deps)

        def stt(out, a, s, b, op0, op1, *deps):
            return dve(lambda e: e.scalar_tensor_tensor(out, a, s, b, op0, op1), *deps)

        def fn(out, in_, f, *deps, bias=0.0, scale=1.0, acc=None):
            if acc is None:
                return act(lambda e: e.activation(out, in_, f, bias=bias, scale=scale), *deps)
            return act(lambda e: e.activation(out, in_, f, bias=bias, scale=scale, accum_out=acc), *deps)

        def rmax(out, in_, *deps):
            return dve(lambda e: e.reduce_max(out, in_, AX.X), *deps)

        def rsum(out, in_, *deps):
            return dve(lambda e: e.reduce_sum(out, in_, AX.X), *deps)

        def recip(out, in_, *deps):
            return dve(lambda e: e.reciprocal(out, in_), *deps)

        def bc(a, shape):
            return a.broadcast_to(shape)

        def mid(a, k):
            return a.unsqueeze(1).broadcast_to([a.shape[0], k, a.shape[1]])

        def end(a, k):
            return a.unsqueeze(len(a.shape)).broadcast_to([*a.shape, k])

        def rsqrt(out, v, scale, eps, *deps):
            n = v.shape[1]
            w, y, t = small(n), out, small(n)
            ts(w, v, scale, eps, ALU.mult, ALU.add, *deps)
            dve(lambda e: e.tensor_scalar(t.bitcast(I32), w.bitcast(I32), 1, None, ALU.logical_shift_right))
            dve(lambda e: e.tensor_scalar(y.bitcast(I32), t.bitcast(I32), -1.0, 1597463007.0, ALU.mult, ALU.add))
            for _ in range(3):
                tt(t, y, y, ALU.mult)
                stt(t, t, -0.5, w, ALU.mult, ALU.mult)
                o = stt(y, t, 1.5, y, ALU.add, ALU.mult)
            return o

        def split(hi, lo, v, *deps):
            a = act(lambda e: e.activation(hi, v, ACT.Copy), *deps)
            return tt(lo, v, hi.bitcast(F), ALU.subtract, a)

        cvn = [0]

        class Piece:
            pass

        def convert(u, ap, a, n):
            i = cvn[0] % NCV
            cvn[0] += 1
            H, L = (t[:, 0:a * n].rearrange("p (a n) -> p a n", a=a) for t in tens["W"][i])
            for q in (slice(0, a // 2), slice(a // 2, a)):
                x = act(lambda e, q=q: e.activation(H[:, q], ap[:, q], ACT.Copy), u.got, cvfree[i])
                o = tt(L[:, q], ap[:, q], H[:, q].bitcast(F), ALU.subtract, x, u.got, cvfree[i])
            u.free = o
            p = Piece()
            p.hi, p.lo, p.got, p.i = H, L, o, i
            return p

        class Feed:

            def __init__(self, plan, ahead=1):
                self.todo, self.made, self.ahead = [], [], ahead
                for src, a, n, how in plan:
                    self.todo.append((src, a, n, how))
                self.plan = iter(self.todo)
                self.half = None
                self.n = 0

            def make(self):
                if self.half is None:
                    nxt = next(self.plan, None)
                    if nxt is None:
                        return
                    src, a, n, how = nxt
                    u = load(src, a, n)
                    if how == "raw":
                        self.made.append(u)
                        return
                    if how == "a" and a * n > 2048:
                        k = (a + 1) // 2
                        parts = [(u.ap[:, 0:k], k, n), (u.ap[:, k:a], a - k, n)]
                    elif a * n <= 2048:
                        parts = [(u.ap, a, n)]
                    else:
                        parts = [(u.ap[:, :, 0:256], a, 256), (u.ap[:, :, 256:n], a, n - 256)]
                    self.half = (u, parts)
                u, parts = self.half
                self.made.append(convert(u, *parts[0]))
                self.half = (u, parts[1:]) if len(parts) > 1 else None

            def next(self):
                while len(self.made) < self.n + 1 + self.ahead:
                    k = len(self.made)
                    self.make()
                    if len(self.made) == k:
                        break
                self.n += 1
                return self.made[self.n - 1]

        def used(p, o):
            cvfree[p.i] = o

        tens["A"], = scope(("AR0", 6700, F))
        g0, g1, g2 = group(), group(), group()
        Q.dma("act", g0, CST[:, :], I["cst"])
        Q.dma("act", g0, X, I["x"][0].rearrange("(t p) d -> p t d", p=128))
        MEM = area(0, 2048).rearrange("p (t d) -> p t d", t=2)
        Q.dma("act", g0, MEM, I["mem"][0].rearrange("(t p) d -> p t d", p=128))
        VR = area(2048, 128)
        PR = area(2176, 128)
        DWR = area(2304, 768)
        LAM = area(6144, 512)
        ISB = area(3072, 256)
        for k, (name, n) in enumerate((("conv_dw_b", 6), ("conv_ln_g", 6), ("conv_ln_b", 6))):
            Q.dma("act", g1, VR[6 * k:6 * k + 6, :], I[name].rearrange("a (j p) -> (a j) p", p=128))
        Q.dma("act", g1, VR[18:66, :], I["b_merge_2"].rearrange("l (j p) -> (l j) p", p=128))
        Q.dma("act", g1, VR[66:68, :], I["diff_subln_2"])
        for k, name in enumerate(("cmp_pos_k_2", "cmp_pos_v_2")):
            Q.dma("act", g1, PR[32 * k:32 * k + 32, :], I[name].rearrange("l (j i) d -> (l j) (i d)", i=2))
        Q.dma("act", g1, DWR[0:31, :], I["conv_dw_w"][0])
        for l in range(2):
            Q.dma("act", g1, NRM[:, 8 * l:8 * l + 8], I["attn_norm_2"][l].rearrange("(p c) -> p c", c=8))
            Q.dma("act", g1, NRM[:, 16 + 8 * l:24 + 8 * l], I["ffn_norm_2"][l].rearrange("(p c) -> p c", c=8))
            w = WR[:, 288 * l:288 * l + 288].rearrange("p (c n) -> p c n", c=8)
            Q.dma("act", g1, w[:, :, 0:4], major(I["w_rg"][l], 0, 4))
            Q.dma("act", g1, w[:, :, 4:36], major(I["w_re"][l], 0, 32))
            Q.dma("act", g1, BR[:, 36 * l:36 * l + 4], I["b_rg"][l].partition_broadcast(128))
            Q.dma("act", g1, BR[:, 36 * l + 4:36 * l + 36], I["b_re"][l].partition_broadcast(128))
            for k, name in enumerate(("cmp_k_w2_2", "cmp_v_w2_2")):
                Q.dma("act", g2, W2[:, 256 * l + 128 * k:256 * l + 128 * k + 128].rearrange("p (c d) -> p c d", c=2),
                      I[name][l].rearrange("(c p) d -> p c d", p=128))
            for k, name in enumerate(("diff_lq1_2", "diff_lk1_2", "diff_lq2_2", "diff_lk2_2")):
                o = 256 * l + 64 * k
                Q.dma("act", g2, LAM[:, o:o + 64], I[name][l].partition_broadcast(128))
        IS = ISB.bitcast(I32)
        Q.dma("act", g2, IS, I["positions_2"][0].partition_broadcast(128))

        def load_gb(g, b, *deps):
            gr = group()
            Q.dma("act", gr, GB[:, 0, :], g.partition_broadcast(128), *deps)
            if b is not None:
                Q.dma("act", gr, GB[:, 1, :], b.partition_broadcast(128), *deps)
            return gr

        gb = load_gb(I["ln1_g"][0], I["ln1_b"][0])

        def transposed(dst, src, *deps, norm=None):
            sv = [src[:, t, :].rearrange("p (d c) -> p c d", c=8) for t in range(2)]
            for c0 in range(0, 8, 2):
                b = bank()
                for c in range(2):
                    for t in range(2):
                        o = tr(b.ap[:, c * 256 + t * 128:c * 256 + t * 128 + 128], sv[t][:, c0 + c, :], b.free, *deps)
                pv = b.ap.rearrange("p (c t) -> p c t", c=2)
                if not isinstance(dst, tuple):
                    b.free = copy(dst[:, c0:c0 + 2, :], pv, o)
                elif norm is None:
                    b.free = split(dst[0][:, c0:c0 + 2, :], dst[1][:, c0:c0 + 2, :], pv, o)
                else:
                    for c in range(2):
                        k = c0 + c
                        a = act(lambda e, k=k, c=c, pv=pv: e.activation(dst[0][:, k, :], pv[:, c, :], ACT.Copy,
                                                                       scale=norm[:, k:k + 1]), o)
                    for c in range(2):
                        k = c0 + c
                        b.free = stt(dst[1][:, k, :], pv[:, c, :], norm[:, k:k + 1], dst[0][:, k, :].bitcast(F),
                                     ALU.mult, ALU.subtract, a)
            return Q.last["dve"], Q.last["act"]

        def feat(p, n0, src, *deps, nk=8):
            b = bank()
            out = b.ap[:, 0:256]
            for c in range(nk):
                w = (p.hi[:, c, n0:n0 + 128], p.lo[:, c, n0:n0 + 128])
                mm(out, w[0], src[0][:, c, :], c == 0, False, b.free, p.got, *deps)
                mm(out, w[0], src[1][:, c, :], False, False)
                o = mm(out, w[1], src[0][:, c, :], False, c == nk - 1)
            used(p, o)
            return b, o

        def toks(p, n, t, src, *deps, nk=8, b=None, at=0):
            b = b or bank()
            out = b.ap[:, at:at + n]
            for c in range(nk):
                x = [v[:, c, t * 128:t * 128 + 128] for v in src]
                mm(out, x[0], p.hi[:, c, 0:n], c == 0, False, b.free, p.got, *deps)
                mm(out, x[1], p.hi[:, c, 0:n], False, False)
                o = mm(out, x[0], p.lo[:, c, 0:n], False, c == nk - 1)
            used(p, o)
            return b, o

        def stats(t, src, *deps):
            st, mv = small(12), small(2)
            for k in range(2):
                dve(lambda e, k=k: e.bn_stats(st[:, 6 * k:6 * k + 6], src[:, t, 512 * k:512 * k + 512]), *deps)
            dve(lambda e: e.bn_aggr(mv, st.rearrange("p (g s) -> p g s", g=2)))
            return mv

        def layer_norm(gr):
            for t in range(2):
                mv = stats(t, X)
                r = small(1)
                rsqrt(r, mv[:, 1:2], 1.0, 1e-5)
                ts(X[:, t, :], X[:, t, :], mv[:, 0:1], r, ALU.subtract, ALU.mult)
                if t:
                    tt(X[:, t, :], X[:, t, :], GB[:, 0, :], ALU.mult, gr)
                    o = tt(X[:, t, :], X[:, t, :], GB[:, 1, :], ALU.add)
                else:
                    o = Q.last["dve"]
                    pool(lambda e: e.tensor_tensor(X[:, 0, :], X[:, 0, :], GB[:, 0, :], ALU.mult), gr, o)
                    o2 = pool(lambda e: e.tensor_tensor(X[:, 0, :], X[:, 0, :], GB[:, 1, :], ALU.add))
            return o, o2

        Pb = [None, None]
        PTb = [None, None]
        pbfree = [None, None]
        ptfree = [None, None]

        def scores(q, kp, causal, *deps):
            S, B, O = [], [], []
            for t in range(2):
                ks = 128 * (t + 1) if causal else 256
                b = bank()
                v = b.ap[:, 0:2 * ks].rearrange("p (h k) -> p h k", h=2)
                O.append(mm(v, q[:, t * 128:t * 128 + 128], kp[:, :, 0:ks], True, True, b.free, *deps))
                S.append(v)
                B.append(b)
            return S, B, O, causal

        def exped(i, sc):
            S, B, O, causal = sc
            P = Pb[i]
            sm = [small(2), small(2)]
            nm = []
            for t in range(2):
                m, n = small(2), small(2)
                if causal:
                    d = S[t][:, :, 128 * t:128 * t + 128]
                    tt(d, d, mid(C("cmask"), 2), ALU.add, O[t])
                rmax(m, S[t], O[t])
                nm.append((n, ts(n, m, -SCALE, None, ALU.mult, None)))
            for t in range(2):
                ks = S[t].shape[2]
                for h in range(2):
                    B[t].free = fn(P[:, t, h, 0:ks], S[t][:, h, :], ACT.Exp, nm[t][1], pbfree[i],
                                   bias=nm[t][0][:, h:h + 1], scale=SCALE, acc=sm[t][:, h:h + 1])
            return i, P, sm, [b.free for b in B], causal

        def normed(st, gate, lam):
            i, P, sm, got, causal = st
            last = []
            for t in range(2):
                ks = 128 * (t + 1) if causal else 256
                r = small(2)
                o = recip(r, sm[t], got[t])
                if gate is not None:
                    o = tt(r, r, gate[:, t, :], ALU.mult)
                if lam is None and (t or not causal):
                    for h in range(2):
                        o = ts(P[:, t, h, 0:ks], P[:, t, h, 0:ks], r[:, h:h + 1], None, ALU.mult, None)
                elif lam is None:
                    pv = P[:, t, :, 0:ks]
                    o = pool(lambda e, pv=pv, r=r, ks=ks: e.tensor_tensor(pv, pv, end(r, ks), ALU.mult), o)
                else:
                    tt(r[:, 1:2], r[:, 1:2], lam, ALU.mult)
                    a, c = P[:, t, 1, 0:ks], P[:, t, 0, 0:ks]
                    ts(c, c, r[:, 0:1], None, ALU.mult, None)
                    o = stt(c, a, r[:, 1:2], c, ALU.mult, ALU.add)
                last.append(o)
            return last

        def turned(st, last, heads=2):
            i, P, sm, got, causal = st
            PT = PTb[i]
            for t in range(2):
                nk = t + 1 if causal else 2
                b = bank()
                for h in range(heads):
                    for k in range(nk):
                        o = tr(b.ap[:, (h * nk + k) * 128:(h * nk + k) * 128 + 128],
                               P[:, t, h, k * 128:k * 128 + 128], b.free, last[t])
                b.free = (acopy if t else vcopy)(
                    PT[:, 0:heads, 0:nk, t * 128:t * 128 + 128],
                    b.ap[:, 0:heads * nk * 128].rearrange("p (h k t) -> p h k t", h=heads, k=nk), o, ptfree[i])
            pbfree[i] = o
            return i, PT, [Q.last["dve"], Q.last["act"]], causal

        def values(pt, v, b, first, lastone, *deps, heads=2):
            i, PT, got, causal = pt
            for h in range(heads):
                ob = b.ap[64 * h:64 * h + 64, :] if heads == 2 else b.ap
                for k in range(2):
                    t0 = 128 * k if causal else 0
                    o = mm(ob[:, t0:256], v(k, h), PT[:, h, k, t0:256], first and k == 0,
                           lastone and k == 1, b.free, *got, *deps)
            ptfree[i] = o
            return o

        def attend(jobs):
            n = len(jobs)
            st, pt = {}, {}
            for j in range(n + 2):
                if j < n:
                    q, kp, causal, gate, lam, *deps = jobs[j][0]
                    sc = scores(q, kp, causal, *deps)
                if 0 < j <= n:
                    k = j - 1
                    last = normed(st[k], jobs[k][0][3], jobs[k][0][4])
                if j < n:
                    st[j] = exped(j % 2, sc)
                if j > 1:
                    jobs[j - 2][1](pt[j - 2])
                if 0 < j <= n:
                    pt[k] = turned(st[k], last, jobs[k][2] if len(jobs[k]) > 2 else 2)

        cst = dve(lambda e: e.memset(MK, 0.0), g0)
        act(lambda e: e.activation(small(1), C("ones")[:, 0:1], ACT.Copy), g0)
        b = bank()
        o = tr(b.ap[:, 0:68], VR[0:68, :], b.free, g1)
        o = tr(b.ap[:, 68:132], PR[0:64, :])
        b.free = vcopy(VT[:, 0:132], b.ap[:, 0:132], o)
        b = bank()
        for j in range(6):
            o = tr(b.ap[:, j * 31:j * 31 + 31], DWR[0:31, j * 128:j * 128 + 128], b.free)
        b.free = vcopy(DW, b.ap[:, 0:186], o)
        ang, kk = area(3328, 256), area(3584, 256)
        vcopy(ang, IS, g2)
        ts(ang, ang, C("freq"), None, ALU.mult, None)
        ts(kk, ang, 1.0 / (2 * math.pi), 12582912.0, ALU.mult, ALU.add)
        ts(kk, kk, -12582912.0, None, ALU.add, None)
        c1 = 6.28125
        c2 = float(np.float32(np.round((2 * math.pi - c1) * 2 ** 20) / 2 ** 20))
        c3 = float(np.float32(2 * math.pi - c1 - c2))
        for c in (c1, c2, c3):
            stt(ang, kk, -c, ang, ALU.mult, ALU.add)
        pi = float(np.nextafter(np.float32(math.pi), np.float32(0)))
        ts(ang, ang, pi, -pi, ALU.min, ALU.max)
        ts(kk, ang, math.pi / 2, -2 * math.pi, ALU.is_gt, ALU.mult)
        stt(kk, ang, math.pi / 2, kk, ALU.add, ALU.add)
        ts(kk, kk, pi, -pi, ALU.min, ALU.max)
        COS, SIN = CS[:, 0:256], CS[:, 256:512]
        o = Q.last["dve"]
        fn(COS, kk, ACT.Sin, o)
        fn(SIN, ang, ACT.Sin)
        LN_ = small(2)
        lp = area(5888, 256).rearrange("p (l k d) -> p l k d", l=2, k=2)
        lv = LAM.rearrange("p (l k q d) -> p l k q d", l=2, k=2, q=2)
        tt(lp, lv[:, :, :, 0, :], lv[:, :, :, 1, :], ALU.mult, g2)
        ls = small(4)
        o = rsum(ls, lp.rearrange("p l k d -> p (l k) d"))
        le = small(4)
        o = fn(le, ls, ACT.Exp, o)
        l4 = le.rearrange("p (l k) -> p l k", k=2)
        tt(NLAM, l4[:, :, 1], l4[:, :, 0], ALU.subtract, o)
        for l in range(2):
            ts(NLAM[:, l:l + 1], NLAM[:, l:l + 1], -(0.8 - 0.6 * math.exp(-0.3 * l)), None, ALU.add, None)
        transposed(XS, MEM, g0)
        Q.fence()

        Pb[:] = [None, None]

        def mix_areas():
            Pb[:] = [area(1024 * i, 1024).rearrange("p (t h k) -> p t h k", t=2, h=2) for i in range(2)]
            PTb[:] = [area(k, 1024).rearrange("p (h k t) -> p h k t", h=2, k=2) for k in (2048, 9728)]
            return area(3072, 512).rearrange("p (j t) -> p j t", j=2)

        def yt(j):
            return [y[:, 256 * j:256 * j + 256] for y in tens["Y"]]

        def yts():
            return tuple(y[:, :].rearrange("p (c t) -> p c t", t=256) for y in tens["Y"])

        def wplan(w, lo, hi):
            return [(major(w, n, min(n + 512, hi)), 8, min(512, hi - n), "n") for n in range(lo, hi, 512)]

        def rows(w, step=512):
            v = w.rearrange("(c p) n -> p c n", p=128)
            return [(v[:, :, n:n + step], 8, step, "n") for n in range(0, 1024, step)]

        def mem_jobs(QM):
            jobs = []
            for j in range(2):
                def fin(pt, j=j):
                    b = bank()
                    o = values(pt, lambda k, h: MV[:, k, j * 128 + h * 64:j * 128 + h * 64 + 64], b, True, True)
                    b.free = split(*yt(6 + j), b.ap[:, 0:256], o)
                jobs.append(((QM[:, j, :], MK[:, j, :, :], False, None, None), fin))
            return jobs

        def mem_kv(fd):
            for k in range(2):
                p = fd.next()
                if k == 0:
                    for j in range(2):
                        b, o = feat(p, j * 128, XS)
                        vcopy(MK[0:64, j, 0, :], b.ap[0:64, 0:256], o)
                        b.free = vcopy(MK[64:128, j, 1, :], b.ap[64:128, 0:256])
                else:
                    for t in range(2):
                        b, o = toks(p, 256, t, XS)
                        b.free = acopy(MV[:, t, :], b.ap[:, 0:256], o)
            transposed(XS, X, Q.last["pe"])

        def conv_mix(fd):
            QM = mix_areas()
            HP = area(3584, 1716).rearrange("p (j t) -> p j t", j=6)
            A = area(5300, 1536).rearrange("p (j t) -> p j t", j=6)
            HC = area(6836, 1536).rearrange("p (j t) -> p j t", j=6)
            G = area(8372, 512)
            dve(lambda e: e.memset(HP[:, :, 0:30], 0.0))
            gf = [None, None]
            for n in range(14):
                if n % 2 == 0:
                    p = fd.next()
                b, o = feat(p, (n % 2) * 128, XS, Q.last["dve"] if n == 0 else None)
                pv = b.ap[:, 0:256]
                if n < 6:
                    b.free = copy(A[:, n, :], pv, o)
                elif n < 12:
                    j = n - 6
                    g = G[:, (j % 2) * 256:(j % 2) * 256 + 256]
                    o = b.free = fn(g, pv, ACT.Sigmoid, o, gf[j % 2])
                    gf[j % 2] = tt(HP[:, j, 30:286], A[:, j, :], g, ALU.mult, o)
                else:
                    b.free = acopy(QM[:, n - 12, :], pv, o)
            ready = Q.last["dve"]
            dw = DW.rearrange("p (j k) -> p j k", j=6)
            DG = area(8372, 1024).rearrange("p (n m) -> p n m", n=8)
            dgf = [Q.last["dve"]] * 8
            cb = [bank() for _ in range(3)]
            for k in range(31):
                for j in range(3, 6):
                    i = (k * 3 + j) % 8
                    o = fn(DG[:, i, :], C("ident"), ACT.Identity, dgf[i], scale=dw[:, j, k:k + 1])
                    dgf[i] = mm(cb[j - 3].ap[:, 0:256], DG[:, i, :], HP[:, j, k:k + 256], k == 0, k == 30,
                                 cb[j - 3].free, o, ready)
            for k in range(31):
                for j in range(3):
                    if k == 0:
                        ts(HC[:, j, :], HP[:, j, 0:256], dw[:, j, 0:1], VT[:, j:j + 1], ALU.mult, ALU.add)
                    else:
                        dve(lambda e, j=j, k=k: e.scalar_tensor_tensor(
                            HC[:, j, :], HP[:, j, k:k + 256], dw[:, j, k:k + 1], HC[:, j, :], ALU.mult, ALU.add))
            for j in range(3, 6):
                cb[j - 3].free = fn(HC[:, j, :], cb[j - 3].ap[:, 0:256], ACT.Identity, dgf[(30 * 3 + j) % 8],
                                    bias=VT[:, j:j + 1])
            both = [Q.last["dve"], Q.last["act"]]
            b = bank()
            for j in range(6):
                o = mm(b.ap[:, 0:256], C("ones"), HC[:, j, :], j == 0, j == 5, b.free, *both)
            mu = area(5300, 256)
            b.free = ts(mu, b.ap[:, 0:256], 1.0 / 768, None, ALU.mult, None, o)
            tt(HC, HC, mid(mu, 6), ALU.subtract)
            sq = area(3584, 1536).rearrange("p (j t) -> p j t", j=6)
            o = fn(sq, HC, ACT.Square, Q.last["dve"], *both)
            b = bank()
            for j in range(6):
                o2 = mm(b.ap[:, 0:256], C("ones"), sq[:, j, :], j == 0, j == 5, b.free, o)
            sd = area(5556, 256)
            b.free = ts(sd, b.ap[:, 0:256], 1.0 / 768, 1e-5, ALU.mult, ALU.add, o2)
            o = fn(sd, sd, ACT.Sqrt, b.free)
            recip(mu, sd, o)
            o = tt(HC, HC, mid(mu, 6), ALU.mult)
            for j in range(6):
                y = sq[:, j, :]
                a = fn(y, HC[:, j, :], ACT.Silu, o, bias=VT[:, 12 + j:13 + j], scale=VT[:, 6 + j:7 + j])
                split(*yt(j), y, a)
            attend(mem_jobs(QM))

        def moba_mix(fd):
            QM = mix_areas()
            QQ = area(3584, 1536).rearrange("p (j t) -> p j t", j=6)
            KP = area(5120, 3072).rearrange("p (j h t) -> p j h t", j=6, h=2)
            V = area(8192, 1536).rearrange("p (t d) -> p t d", t=2)
            dve(lambda e: e.memset(KP, 0.0))
            for n in range(12):
                if n % 2 == 0:
                    p = fd.next()
                b, o = feat(p, (n % 2) * 128, XS)
                if n < 6:
                    b.free = acopy(QQ[:, n, :], b.ap[:, 0:256], o)
                else:
                    vcopy(KP[0:64, n - 6, 0, :], b.ap[0:64, 0:256], o)
                    b.free = vcopy(KP[64:128, n - 6, 1, :], b.ap[64:128, 0:256])
            for k in range(3):
                p = fd.next()
                for t in range(2):
                    b, o = toks(p, 256, t, XS)
                    b.free = copy(V[:, t, 256 * k:256 * k + 256], b.ap[:, 0:256], o)
            p = fd.next()
            for j in range(2):
                b, o = feat(p, j * 128, XS)
                b.free = acopy(QM[:, j, :], b.ap[:, 0:256], o)
            ins = [Q.last["dve"], Q.last["act"]]
            jobs = []
            for j in range(6):
                def fin(pt, j=j):
                    b = bank()
                    o = values(pt, lambda k, h: V[:, k, j * 128 + h * 64:j * 128 + h * 64 + 64], b, True, True)
                    b.free = split(*yt(j), b.ap[:, 0:256], o)
                jobs.append(((QQ[:, j, :], KP[:, j, :, :], True, None, None, *ins), fin))
            attend(jobs + mem_jobs(QM))

        baton = [ctx.enter_context(nc.semaphore(f"f{i}")) for i in range(64)]

        def beyond(l, pos, comb, flag, main):
            ACC = area(0, 2048).rearrange("p (t d) -> p t d", t=2)
            XF = area(2048, 1024).rearrange("p (c s) -> p c s", c=8)
            PQ = area(3072, 128)
            PW = area(3200, 128)
            WB = area(4096, 2048)
            G = area(6144, 256).rearrange("p (t s) -> p t s", t=2)
            GW = area(6400, 256).rearrange("p (t s) -> p t s", t=2)
            CT = area(6656, 256).rearrange("p (t s) -> p t s", t=2)
            H = area(8192, 512)
            HT = area(8704, 512).rearrange("p (c s) -> p c s", c=4)
            Y = area(9216, 1024)
            B = [b.ap for b in banks]
            pq = PQ.rearrange("p (w t e) -> p w t e", w=2, t=2)
            flat = [PQ.rearrange("p (q e) -> p q e", e=32), PW.rearrange("p (q e) -> p q e", e=32)]
            gate = I["w_gate"][l].rearrange("g e (p c) n -> (g e) p c n", p=128)
            upw = I["w_up"][l].rearrange("g e (p c) n -> (g e) p c n", p=128)
            dn = I["w_down"][l].rearrange("g e (p c) n -> (g e) p c n", p=128)

            def one():
                st = []

                def step(eng):
                    return lambda f: st.append((eng, f))

                @step("dve")
                def _(e, i):
                    for t in range(2):
                        r = e.tensor_scalar(G[:, t, :], C("iota"), pq[:, 0, t, 0:1], None, ALU.is_equal)
                    return r

                @step("dve")
                def _(e, i):
                    for t in range(2):
                        r = e.tensor_scalar(GW[:, t, :], G[:, t, :], pq[:, 1, t, 0:1], None, ALU.mult)
                    return r

                @step("pe")
                def _(e, i):
                    for c in range(8):
                        for t in range(2):
                            r = e.matmul(B[c // 4][:, (c % 4) * 128:(c % 4) * 128 + 128],
                                         X[:, t, :].rearrange("p (d c) -> p c d", c=8)[:, c, :], G[:, t, :],
                                         start=t == 0, stop=t == 1)
                    for t in range(2):
                        r = e.transpose(B[2][:, t * 128:t * 128 + 128], GW[:, t, :], C("ident"))
                    return r

                @step("dve")
                def _(e, i):
                    for k in range(2):
                        e.tensor_copy(XF[:, 4 * k:4 * k + 4, :], B[k].rearrange("p (c s) -> p c s", c=4))
                    return e.tensor_copy(CT, B[2][:, 0:256].rearrange("p (t s) -> p t s", t=2))

                for w, b in ((gate, 3), (upw, 4)):
                    for hf in range(2):
                        wv = WB.rearrange("p (c n) -> p c n", c=4)

                        @step("act dma")
                        def _(e, i, w=w, hf=hf, wv=wv):
                            return e.dma_start(wv, w[bass.ds(i, 1), :, 4 * hf:4 * hf + 4, :]
                                               .rearrange("a p c n -> (a p) c n"))

                        @step("pe")
                        def _(e, i, b=b, hf=hf, wv=wv):
                            for c in range(4):
                                r = e.matmul(B[b], XF[:, 4 * hf + c, :], wv[:, c, :],
                                             start=hf == 0 and c == 0, stop=hf == 1 and c == 3)
                            return r

                @step("act")
                def _(e, i):
                    return e.activation(H, B[3], ACT.Silu)

                @step("dve")
                def _(e, i):
                    return e.tensor_tensor(H, H, B[4], ALU.mult)

                @step("pe")
                def _(e, i):
                    for c in range(4):
                        r = e.transpose(B[5][:, c * 128:c * 128 + 128], H.rearrange("p (f c) -> p c f", c=4)[:, c, :],
                                        C("ident"))
                    return r

                @step("dve")
                def _(e, i):
                    return e.tensor_copy(HT, B[5].rearrange("p (c s) -> p c s", c=4))

                for hf in range(2):
                    wv = WB.rearrange("p (c n) -> p c n", c=2)

                    @step("act dma")
                    def _(e, i, hf=hf, wv=wv):
                        return e.dma_start(wv, dn[bass.ds(i, 1), :, 2 * hf:2 * hf + 2, :]
                                           .rearrange("a p c n -> (a p) c n"))

                    @step("pe")
                    def _(e, i, hf=hf, wv=wv):
                        for c in range(2):
                            for n in range(2):
                                r = e.matmul(B[6 + n], HT[:, 2 * hf + c, :], wv[:, c, n * 512:n * 512 + 512],
                                             start=hf == 0 and c == 0, stop=hf == 1 and c == 1)
                        return r

                @step("dve")
                def _(e, i):
                    for n in range(2):
                        r = e.tensor_copy(Y[:, n * 512:n * 512 + 512], B[6 + n])
                    return r

                @step("pe")
                def _(e, i):
                    for n in range(2):
                        for t in range(2):
                            r = e.matmul(B[2 * n + t], CT[:, t, :], Y[:, n * 512:n * 512 + 512], start=True, stop=True)
                    return r

                @step("dve")
                def _(e, i):
                    for n in range(2):
                        for t in range(2):
                            a = ACC[:, t, n * 512:n * 512 + 512]
                            r = e.tensor_tensor(a, a, B[2 * n + t], ALU.add)
                    return r

                @step("dve")
                def _(e, i):
                    e.tensor_copy(flat[1][:, :, 0:31], flat[0][:, :, 1:32])
                    return e.tensor_copy(flat[1][:, :, 31:32], flat[0][:, :, 0:1])

                @step("dve")
                def _(e, i):
                    return e.tensor_copy(PQ, PW)

                return st

            steps = one()

            def walk(me):
                def body(e, i):
                    for k, (eng, f) in enumerate(steps):
                        if eng.split()[0] != me:
                            continue
                        if k:
                            by = 16 if "dma" in steps[k - 1][0] else 1
                            e.wait_ge(baton[k - 1], by)
                            e.sem_clear(baton[k - 1])
                        f(e, i).then_inc(baton[k], 16 if "dma" in eng else 1)
                    if me == "dve":
                        e.wait_ge(baton[len(steps) - 1], 1)
                        e.sem_clear(baton[len(steps) - 1])

                def own(e, f):
                    f().then_inc(baton[63], 1)
                    e.wait_ge(baton[63], 1)
                    e.sem_clear(baton[63])

                def run(e):
                    v = e.value_load(FLAG[0:1, l:l + 1], min_val=0, max_val=1)
                    with e.If(v > 0):
                        for r in range(2):
                            if me == "dve":
                                if r == 0:
                                    own(e, lambda: e.tensor_scalar(pq[:, 0], pos, -float(CAP), None, ALU.add))
                                    own(e, lambda: e.tensor_copy(pq[:, 1], comb))
                                else:
                                    own(e, lambda: e.tensor_scalar(pq[:, 0], pq[:, 0], -128.0, None, ALU.add))
                            with e.Fori(0, 32) as i:
                                body(e, i)
                return run

            for me in ("dve", "pe", "act"):
                for o in (flag, *main):
                    o.sig = True
                Q.q[me].append(Op(me, walk(me), [flag, *main]))

        def moe(l, gr_next, ln):
            ts_ = scope(*[(f"rx{l}{i}", UNIT, F) for i in range(NEXTRA)], (f"ARM{l}", 10900, F))
            tens["A"] = ts_[-1]
            slots = ring + extra
            for i, sl in enumerate(extra):
                sl.ap, sl.after = ts_[i][:, :], list(before_moe)
                sl.unit = None
            XT = area(2048, 2048).rearrange("p (c t) -> p c t", c=8)
            transposed(XT, X, *ln)
            ACC = area(0, 2048).rearrange("p (t d) -> p t d", t=2)
            XG = [area(2048 + 2048 * i, 2048).rearrange("p (c s) -> p c s", c=8) for i in range(2)]
            G = area(6144, 512).rearrange("p (t s) -> p t s", t=2)
            GW = area(6656, 512).rearrange("p (t s) -> p t s", t=2)
            CT = [area(7168 + 512 * i, 512).rearrange("p (q t) -> p q t", q=2) for i in range(2)]
            H = area(8192, 512)
            HT = area(8704, 512).rearrange("p (c s) -> p c s", c=4)
            Y = area(9216, 1024)
            RT = area(10240, 660)
            rn = [0]

            def rt(*shape):
                n = int(np.prod(shape))
                a = RT[:, rn[0]:rn[0] + n]
                rn[0] += n
                if len(shape) == 1:
                    return a
                names = "abcd"[:len(shape)]
                return a.rearrange(f"p ({' '.join(names)}) -> p {' '.join(names)}",
                                   **{k: v for k, v in zip(names[:-1], shape[:-1])})

            L = rt(2, 36)
            xgfree, ctfree = [None, None], [None, None]
            wr = WR[:, 288 * l:288 * l + 288].rearrange("p (c n) -> p c n", c=8)
            b = bank()
            xt = [Q.last["dve"], Q.last["act"]]
            for t in range(2):
                for c in range(8):
                    o = mm(b.ap[:, t * 36:t * 36 + 36], XT[:, c, t * 128:t * 128 + 128], wr[:, c, :],
                           c == 0, c == 7, b.free, *xt)
            xgfree[0] = o
            b.free = tt(L, b.ap[:, 0:72].rearrange("p (t n) -> p t n", t=2),
                        mid(BR[:, 36 * l:36 * l + 36], 2), ALU.add, o)

            def onehot(lg, rev, n):
                m, k, km, oh = rt(2), rt(2, n), rt(2), rt(2, n)
                rmax(m, lg)
                tt(k, lg, end(m, n), ALU.is_equal)
                tt(k, k, mid(rev, 2), ALU.mult)
                rmax(km, k)
                tt(oh, k, end(km, n), ALU.is_equal)
                return m, oh

            lg = L[:, :, 0:4]
            gm, og = onehot(lg, C("rev4"), 4)
            eg = rt(2, 4)
            o = tt(eg, lg, end(gm, 4), ALU.subtract)
            o = fn(eg, eg, ACT.Exp, o)
            gw = rt(2)
            rsum(gw, eg, o)
            recip(gw, gw)
            pr = rt(2, 4, 8)
            og4 = end(og, 8)
            for t in range(2):
                tt(pr[:, t], og4[:, t], L[:, t, 4:36].rearrange("p (g e) -> p g e", g=4), ALU.mult)
            es = rt(2, 8)
            for t in range(2):
                rsum(es[:, t], pr[:, t].rearrange("p g e -> p e g"))
            m1, o1 = onehot(es, C("rev8"), 8)
            es2 = rt(2, 8)
            stt(es2, o1, NEG, es, ALU.mult, ALU.add)
            m2, o2 = onehot(es2, C("rev8"), 8)
            e2, w1, w2, wi, sl = rt(2), rt(2), rt(2), rt(2, 8), rt(2, 8)
            o = tt(e2, m2, m1, ALU.subtract)
            o = fn(e2, e2, ACT.Exp, o)
            ts(w1, e2, 1.0, None, ALU.add, None, o)
            recip(w1, w1)
            tt(w1, w1, gw, ALU.mult)
            tt(w2, w1, e2, ALU.mult)
            tt(sl, o1, o2, ALU.add)
            tt(o1, o1, end(w1, 8), ALU.mult)
            tt(o2, o2, end(w2, 8), ALU.mult)
            tt(wi, o1, o2, ALU.add)
            comb, sel, pos = rt(2, 32), rt(2, 32), rt(2, 32)
            for t in range(2):
                for dst, s in ((comb, wi), (sel, sl)):
                    o = tt(dst[:, t].rearrange("p (g e) -> p g e", g=4), og4[:, t], mid(s[:, t], 4), ALU.mult)
            b = bank()
            mm(b.ap[:, 0:32], C("before"), sel[:, 0, :], True, True, b.free, o)
            mm(b.ap[:, 32:64], C("ones"), sel[:, 0, :], True, False)
            mm(b.ap[:, 32:64], C("before"), sel[:, 1, :], False, True)
            mm(b.ap[:, 64:96], C("ones"), sel[:, 0, :], True, False)
            o = mm(b.ap[:, 64:96], C("ones"), sel[:, 1, :], False, True)
            ts(pos, b.ap[:, 0:64].rearrange("p (t e) -> p t e", t=2), 1.0, None, ALU.add, None, o)
            tt(pos, pos, sel, ALU.mult)
            ts(pos, pos, -1.0, None, ALU.add, None)
            cm = small(1)
            b.free = rmax(cm, b.ap[:, 64:96])
            ts(cm, cm, float(CAP), None, ALU.is_gt, None)
            flag = vcopy(FLAG[:, l:l + 1], cm)

            gfree = [None]

            def gather(g):
                i = g % 2
                for t in range(2):
                    tt(G[:, t].rearrange("p (e s) -> p e s", e=4), mid(C("iota")[:, 0:CAP], 4),
                       end(pos[:, t, 4 * g:4 * g + 4], CAP), ALU.is_equal, gfree[0])
                    o = tt(GW[:, t].rearrange("p (e s) -> p e s", e=4), G[:, t].rearrange("p (e s) -> p e s", e=4),
                           end(comb[:, t, 4 * g:4 * g + 4], CAP), ALU.mult)
                for c in range(0, 8, 2):
                    b = bg
                    for k in range(2):
                        for t in range(2):
                            sv = X[:, t, :].rearrange("p (d c) -> p c d", c=8)[:, c + k, :]
                            o2 = mm(b.ap[:, k * 256:k * 256 + 256], sv, G[:, t, :], t == 0,
                                    t == 1, b.free, o)
                    b.free = copy(XG[i][:, c:c + 2, :], b.ap.rearrange("p (k s) -> p k s", k=2), o2, xgfree[i])
                b = bg
                for q in range(2):
                    for t in range(2):
                        o2 = tr(b.ap[:, (q * 2 + t) * 128:(q * 2 + t) * 128 + 128],
                                GW[:, t, q * 128:q * 128 + 128], b.free)
                gfree[0] = o2
                b.free = copy(CT[i], b.ap.rearrange("p (q t) -> p q t", q=2), o2, ctfree[i])
                return [Q.last["dve"], Q.last["act"]]

            bG, bU, bT, bY0, bY1, bO0, bO1, bg = banks

            hfree = [None]
            yfree = [None]
            htfree = [None]

            def up(pair, got):
                i, s0 = (pair // 2) % 2, (pair % 2) * 128
                W = []
                for w in ("w_gate", "w_up"):
                    W.append([load(major(I[w][l, (2 * pair + x) // 8, (2 * pair + x) % 8], 0, 512), 8, 512, slots)
                              for x in range(2)])
                for k, b in ((0, bG), (1, bU)):
                    for c in range(8):
                        for x in range(2):
                            o = mm(b.ap[64 * x:64 * x + 64, :], XG[i][:, c, s0 + 64 * x:s0 + 64 * x + 64],
                                   W[k][x].ap[:, c, :], c == 0, c == 7, b.free, W[k][x].got, *got)
                    for x in range(2):
                        W[k][x].free = o
                    if k == 0:
                        a = bG.free = fn(H, bG.ap, ACT.Silu, o, hfree[0])
                bU.free = tt(H, H, bU.ap, ALU.mult, o, a)
                if pair % 2:
                    xgfree[i] = o
                return bU.free

            def down(pair, h):
                hv = H.rearrange("p (f c) -> p c f", c=4)
                for c in range(4):
                    o = tr(bT.ap[:, c * 128:c * 128 + 128], hv[:, c, :], bT.free, h)
                hfree[0] = o
                bT.free = ht = vcopy(HT, bT.ap.rearrange("p (c s) -> p c s", c=4), o, htfree[0])
                W = []
                for x in range(2):
                    e = 2 * pair + x
                    W.append(load(I["w_down"][l, e // 8, e % 8].rearrange("(p c) n -> p c n", p=128), 4, 1024, slots))
                ys = []
                for n, b in enumerate((bY0, bY1)):
                    for c in range(4):
                        for x in range(2):
                            o = mm(b.ap[64 * x:64 * x + 64, :], HT[:, c, 64 * x:64 * x + 64],
                                   W[x].ap[:, c, n * 512:n * 512 + 512], c == 0, c == 3, b.free, W[x].got, ht)
                    b.free = (acopy if n == 0 else vcopy)(Y[:, n * 512:n * 512 + 512], b.ap, o, yfree[0])
                    ys.append(b.free)
                htfree[0] = o
                W[0].free = W[1].free = o
                return ys

            def scatter(pair, ys):
                i = (pair // 2) % 2
                for n in range(2):
                    for t in range(2):
                        b = (bO0, bO1)[t]
                        o = mm(b.ap, CT[i][:, pair % 2, t * 128:t * 128 + 128], Y[:, n * 512:n * 512 + 512],
                               True, True, b.free, *ys)
                        a = ACC[:, t, n * 512:n * 512 + 512]
                        if pair == 0:
                            b.free = vcopy(a, b.ap, o)
                        else:
                            b.free = tt(a, a, b.ap, ALU.add, o)
                yfree[0] = o
                if pair % 2:
                    ctfree[i] = o

            got = gather(0)
            nxt = None
            ys = None
            for pair in range(16):
                h = up(pair, got)
                if pair:
                    scatter(pair - 1, ys)
                if pair % 2 == 0 and pair < 14:
                    nxt = gather(pair // 2 + 1)
                if pair % 2:
                    got = nxt
                ys = down(pair, h)
            scatter(15, ys)
            beyond(l, pos, comb, flag, [Q.last[x] for x in ("pe", "act", "dve")])
            for t in range(2):
                stt(X[:, t, :], X[:, t, :], ALPHA, ACC[:, t, :], ALU.mult, ALU.add)
            return layer_norm(gr_next)

        def rms_t(dst, norm, *deps):
            J = area(3072, 1024)
            ss, r = small(2), small(2)
            for t in range(2):
                o = fn(J, X[:, t, :], ACT.Square, Q.last["dve"], *deps, acc=ss[:, t:t + 1])
            rsqrt(r, ss, 1.0 / 1024, 1e-6, o)
            J2 = area(4096, 2048).rearrange("p (t d) -> p t d", t=2)
            for t in range(2):
                o = ts(J2[:, t, :], X[:, t, :], r[:, t:t + 1], None, ALU.mult, None)
            transposed(dst, J2, o, norm=norm)

        def ot(br, c):
            k = (4 * br + c) * 256
            return [y[:, k:k + 256] for y in tens["Y"]]

        def ots(br):
            return tuple(y[:, 1024 * br:1024 * br + 1024].rearrange("p (c t) -> p c t", c=4) for y in tens["Y"])

        def rope(raw, dst, tmp, *deps):
            b = bank()
            o = mm(b.ap[:, 0:256], C("perm"), raw, True, True, b.free, *deps)
            b.free = tt(tmp, b.ap[:, 0:256], SIN, ALU.mult, o, *deps)
            tt(dst, raw, COS, ALU.mult)
            return tt(dst, dst, tmp, ALU.add)

        def nsa(l, fd):
            w = I["w_in_2"][l]
            QR = area(8192, 1024).rearrange("p (j t) -> p j t", j=4)
            QQ = area(9216, 1024).rearrange("p (j t) -> p j t", j=4)
            KS = area(10240, 1024).rearrange("p (g h t) -> p g h t", g=2, h=2)
            KW = area(11264, 1024).rearrange("p (g h t) -> p g h t", g=2, h=2)
            VS = area(12288, 256).rearrange("p (k d) -> p k d", k=2)
            VW = area(12544, 256).rearrange("p (k d) -> p k d", k=2)
            BK = area(3072, 480).rearrange("p (j g n) -> p j g n", j=16, g=2)
            BV = area(3552, 480).rearrange("p (j g n) -> p j g n", j=16, g=2)
            HK = area(4032, 256)
            TK = area(4288, 60).rearrange("p (c n) -> p c n", c=2)
            TR = area(4352, 512).rearrange("p (g c r n) -> p g c r n", g=2, c=2, r=4)
            RAW = area(4864, 256)
            TMP = area(6144, 256)
            KC = area(6400, 128).rearrange("p (g h n) -> p g h n", g=2, h=2)
            VC = area(6528, 512).rearrange("p (g r d) -> p g r d", g=2, r=2)
            PC = area(7040, 512)
            PT = area(7552, 512).rearrange("p (g t) -> p g t", g=2)
            GT = small(48).rearrange("p (t n) -> p t n", t=2)
            W2D = area(8064, 128).rearrange("p (h d) -> p h d", h=2)
            for a in (KS, KW, KC, VC, TR):
                dve(lambda e, a=a: e.memset(a, 0.0))
            for j in range(4):
                if j % 2 == 0:
                    p = fd.next()
                b, o = feat(p, (j % 2) * 128, XS)
                o = b.free = acopy(QR[:, j, :], b.ap[:, 0:256], o)
                rope(QR[:, j, :], QQ[:, j, :], TMP, o)
            p = fd.next()
            for k, B in ((0, BK), (1, BV)):
                b, o = feat(p, k * 128, XS)
                bv = b.ap[:, 0:256].rearrange("p (n j i) -> p i j n", j=8, i=2)
                for i in range(2):
                    for g in range(2):
                        for hf in range(2):
                            vcopy(B[64 * i:64 * i + 64, 8 * hf:8 * hf + 8, g, :],
                                  bv[64 * g:64 * g + 64, i, :, hf:hf + 15], o)
                b.free = Q.last["dve"]
                pv = VT[:, 68 + 32 * k + 16 * l:84 + 32 * k + 16 * l]
                for g in range(2):
                    tt(B[:, :, g, :], B[:, :, g, :], end(pv, 15), ALU.add)
            TMP2 = area(5120, 256)
            VTT = area(5376, 256)
            dep = [None]

            def keys(p, n0, K):
                b, o = feat(p, n0, XS)
                o = b.free = acopy(RAW, b.ap[:, 0:256], o, dep[0])
                rope(RAW, TMP2, TMP, o)
                for g in range(2):
                    for h in range(2):
                        dep[0] = vcopy(K[64 * h:64 * h + 64, g, h, :], TMP2[64 * g:64 * g + 64, :])

            def turn_back(p, n0, n, outs, f):
                b, o = feat(p, n0, XS)
                a = b.free = acopy(VTT[0:n, :], b.ap[0:n, 0:256], o, Q.last["pe"])
                b = bank()
                for t in range(2):
                    o = tr(b.ap[:, t * 128:t * 128 + n], VTT[0:n, t * 128:t * 128 + 128], b.free, a)
                for t in range(2):
                    b.free = fn(outs(t), b.ap[:, t * 128:t * 128 + n], f, o)

            p = fd.next()
            keys(p, 0, KS)
            turn_back(p, 128, 128, lambda t: VS[:, t, :], ACT.Copy)
            p = fd.next()
            keys(p, 0, KW)
            turn_back(p, 128, 128, lambda t: VW[:, t, :], ACT.Copy)
            p = fd.next()
            turn_back(p, 0, 24, lambda t: GT[:, t, :], ACT.Sigmoid)
            for k, (B, name) in enumerate(((BK, "cmp_k_w1_2"), (BV, "cmp_v_w1_2"))):
                u = fd.next()
                b = bank()
                for j in range(16):
                    o = mm(b.ap[0:30, 0:256], B[:, j].rearrange("p g n -> p (g n)"), u.ap[:, j, :],
                           j == 0, j == 15, b.free, u.got, Q.last["dve"])
                u.free = o
                o = b.free = fn(HK[0:30, :], b.ap[0:30, 0:256], ACT.Gelu_apprx_tanh, o, Q.last["pe"])
                b = bank()
                for c in range(2):
                    o = tr(b.ap[:, c * 30:c * 30 + 30], HK[0:30, c * 128:c * 128 + 128], b.free, o)
                w2 = W2[:, 256 * l + 128 * k:256 * l + 128 * k + 128].rearrange("p (c d) -> p c d", c=2)
                if k == 0:
                    b.free = vcopy(TK, b.ap[:, 0:60].rearrange("p (c n) -> p c n", c=2), o)
                    hk = b.free
                    b = bank()
                    for c in range(2):
                        for h in range(2):
                            o = vcopy(W2D[:, h, :], w2[:, c, :], Q.last["pe"])
                        o = mm(b.ap[:, 0:30], W2D.rearrange("p h d -> p (h d)"), TK[:, c, :], c == 0, c == 1,
                               b.free, o)
                    for h in range(2):
                        vcopy(KC[64 * h:64 * h + 64, :, h, 0:15],
                              b.ap[64 * h:64 * h + 64, 0:30].rearrange("p (g n) -> p g n", g=2), o)
                    b.free = Q.last["dve"]
                else:
                    for c in range(2):
                        for g in range(2):
                            vcopy(TR[:, g, c, :, 0:15], mid(b.ap[:, c * 30 + g * 15:c * 30 + g * 15 + 15], 4), o)
                    b.free = Q.last["dve"]
                    b = bank()
                    for g in range(2):
                        for c in range(2):
                            o = mm(b.ap[:, g * 64:g * 64 + 64], TR[:, g, c].rearrange("p r n -> p (r n)"),
                                   w2[:, c, :], c == 0, c == 1, b.free, Q.last["dve"])
                    for g in range(2):
                        for r in range(4):
                            q0 = 32 * r
                            vcopy(VC[q0:q0 + 32, g, r // 2, (r % 2) * 64:(r % 2) * 64 + 64],
                                  b.ap[q0:q0 + 32, g * 64:g * 64 + 64], o)
                    b.free = Q.last["dve"]
            for t in range(2):
                b = bank()
                for j in range(4):
                    o = mm(b.ap[:, j * 64:j * 64 + 64], QR[:, j, t * 128:t * 128 + 128],
                           KC[:, j // 2].rearrange("p h n -> p (h n)"), True, True, b.free, Q.last["dve"])
                P = PC[:, t * 256:t * 256 + 256].rearrange("p (h n) -> p h n", h=8)
                b.free = tt(P, b.ap[:, 0:256].rearrange("p (h n) -> p h n", h=8),
                            mid(C("madd")[:, t * 32:t * 32 + 32], 8), ALU.add, o)
                m, sm = small(8), small(8)
                rmax(m, P)
                o = tt(P, P, end(m, 32), ALU.subtract)
                o = fn(P, P, ACT.Exp, o, scale=SCALE)
                rsum(sm, P if t else P, o)
                recip(sm, sm)
                tt(sm, sm, GT[:, t, :].rearrange("p (h b) -> p h b", b=3)[:, :, 0], ALU.mult)
                tt(P, P, end(sm, 32), ALU.mult)
                tt(P, P, mid(C("m01")[:, t * 32:t * 32 + 32], 8), ALU.mult)
            o = Q.last["dve"]
            b = bank()
            for g in range(2):
                for t in range(2):
                    o = tr(b.ap[:, g * 256 + t * 128:g * 256 + t * 128 + 128],
                           PC[:, t * 256 + g * 128:t * 256 + g * 128 + 128], b.free, o)
            b.free = vcopy(PT, b.ap.rearrange("p (g t) -> p g t", g=2), o)
            Q.fence()
            gt = GT.rearrange("p t (h b) -> p t h b", b=3)
            jobs = []
            ob = [None]
            for j in range(4):
                for br, (K, V) in ((1, (KS, VS)), (2, (KW, VW))):
                    def fin(pt, j=j, br=br, V=V):
                        if br == 1:
                            ob[0] = banks_o[j % 2]
                        b = ob[0]
                        o = values(pt, lambda k, h: V[:, k, (j // 2) * 64:(j // 2) * 64 + 64], b, br == 1, False)
                        if br == 2:
                            o = mm(b.ap[:, 0:256], VC[:, j // 2, j % 2, :], PT[:, j // 2, :], False, True)
                            b.free = split(*ot(0, j), b.ap[:, 0:256], o)
                    jobs.append(((QQ[:, j, :], K[:, j // 2], True, gt[:, :, 2 * j:2 * j + 2, br], None), fin))
            hold(2)
            attend(jobs)
            hold(0)

        banks_o = banks[6:8]

        def diff(l, fd):
            w = I["w_in_2"][l]
            QQ = area(8192, 1024).rearrange("p (j t) -> p j t", j=4)
            KP = area(9216, 2048).rearrange("p (j h t) -> p j h t", j=4, h=2)
            V = area(11264, 1024).rearrange("p (k d) -> p k d", k=2)
            RAW, TMP, TMP2 = area(6144, 256), area(6400, 256), area(6656, 256)
            O = area(7168, 1024).rearrange("p (j t) -> p j t", j=4)
            dve(lambda e: e.memset(KP, 0.0))
            rf = None
            for part in range(2):
                for j in range(4):
                    if j % 2 == 0:
                        p = fd.next()
                    b, o = feat(p, (j % 2) * 128, XS)
                    o = b.free = acopy(RAW, b.ap[:, 0:256], o, rf)
                    if part == 0:
                        rf = rope(RAW, QQ[:, j, :], TMP, o)
                    else:
                        rope(RAW, TMP2, TMP, o)
                        for h in range(2):
                            rf = vcopy(KP[64 * h:64 * h + 64, j, h, :], TMP2[64 * h:64 * h + 64, :])
            for k in range(2):
                p = fd.next()
                for t in range(2):
                    b, o = toks(p, 256, t, XS)
                    b.free = copy(V[:, t, 256 * k:256 * k + 256], b.ap[:, 0:256], o)
            ins = [Q.last["dve"], Q.last["act"]]
            jobs = []
            for j in range(4):
                def fin(pt, j=j):
                    b = bank()
                    o = values(pt, lambda k, h: V[:, k, j * 128:j * 128 + 128], b, True, True, heads=1)
                    b.free = copy(O[:, j, :], b.ap[:, 0:256], o)
                jobs.append(((QQ[:, j, :], KP[:, j], True, None, NLAM[:, l:l + 1], *ins), fin, 1))
            attend(jobs)
            SQ = area(8192, 1024)
            o = fn(SQ, O.rearrange("p j t -> p (j t)"), ACT.Square, Q.last["dve"], Q.last["pe"])
            R = area(9216, 1024)
            for k in range(2):
                b = bank()
                o2 = mm(b.ap, C("ones"), SQ[:, 512 * k:512 * k + 512], True, True, b.free, o)
                b.free = ts(R[:, 512 * k:512 * k + 512], b.ap, 1.0 / 128, 1e-6, ALU.mult, ALU.add, o2)
            o = fn(R, R, ACT.Sqrt, b.free)
            recip(R, R, o)
            tt(O.rearrange("p j t -> p (j t)"), O.rearrange("p j t -> p (j t)"), R, ALU.mult)
            init = 0.8 - 0.6 * math.exp(-0.3 * l)
            o = ts(R, O.rearrange("p j t -> p (j t)"), VT[:, 66 + l:67 + l], 1.0 - init, ALU.mult, ALU.mult)
            split(tens["Y"][0][:, 1024:2048], tens["Y"][1][:, 1024:2048], R, o)

        def sgu(l, fd):
            w = I["w_in_2"][l]
            UT = area(8192, 1024).rearrange("p (g t) -> p g t", g=4)
            V = area(9216, 1024).rearrange("p (t d) -> p t d", t=2)
            WG = area(10240, 512).rearrange("p (g s) -> p g s", g=4)
            WT = area(10752, 512).rearrange("p (g t) -> p g t", g=4)
            BS = area(11264, 512)
            NG = area(11776, 512)
            J = area(12288, 512)
            gr = group()
            fr = [Q.last["dve"], Q.last["pe"], Q.last["pool"]]
            Q.dma("act", gr, WG, I["sgu_w_2"][l].rearrange("g t s -> t g s"), *fr)
            Q.dma("act", gr, BS, I["sgu_b_2"][l].rearrange("g t -> (g t)").partition_broadcast(128), *fr)
            Q.dma("act", gr, NG, I["sgu_norm_2"][l].partition_broadcast(128), *fr)
            for j in range(4):
                if j % 2 == 0:
                    p = fd.next()
                b, o = feat(p, (j % 2) * 128, XS)
                b.free = fn(UT[:, j, :], b.ap[:, 0:256], ACT.Gelu_apprx_tanh, o)
            ss, r = small(2), small(2)
            for k in range(2):
                p = fd.next()
                for t in range(2):
                    b, o = toks(p, 256, t, XS)
                    b.free = fn(V[:, t, 256 * k:256 * k + 256], b.ap[:, 0:256], ACT.Gelu_apprx_tanh, o)
            for t in range(2):
                o = fn(J, V[:, t, :], ACT.Square, acc=ss[:, t:t + 1])
            rsqrt(r, ss, 1.0 / 512, 1e-6, o)
            for t in range(2):
                v = stt(V[:, t, :], V[:, t, :], r[:, t:t + 1], NG, ALU.mult, ALU.mult, gr)
            b = bank()
            for g in range(4):
                o = tr(b.ap[:, g * 128:g * 128 + 128], WG[:, g, :], b.free, gr)
            v = b.free = tt(WT, b.ap.rearrange("p (g t) -> p g t", g=4), mid(C("upto"), 4), ALU.mult, o)
            bs = BS.rearrange("p (g t) -> p g t", g=4)
            for g in range(4):
                b = bank()
                for t in range(2):
                    o = mm(b.ap[:, t * 128:t * 128 + 128], V[:, t, g * 128:g * 128 + 128], WT[:, g, :], True, True,
                           b.free, v)
                S = J[:, (g % 2) * 256:(g % 2) * 256 + 256]
                b.free = tt(S.rearrange("p (n t) -> p n t", n=2), b.ap[:, 0:256].rearrange("p (n t) -> p n t", n=2),
                            mid(bs[:, g, :], 2), ALU.add, o)
                o = tt(S, S, UT[:, g, :], ALU.mult)
                split(*ot(2, g), S, o)

        def merge(l, fd):
            MXH, MXL, tens["A"] = scope((f"MXH{l}", 2048, FR), (f"MXL{l}", 2048, FR), (f"AM{l}", 4608, F))
            MX = area(3072, 2048).rearrange("p (c t) -> p c t", c=8)
            SG = area(5120, 2048).rearrange("p (s k t) -> p s k t", s=2, k=4)
            MB = area(7168, 512).rearrange("p (k t) -> p k t", k=2)
            mf = [None, None]
            sf = [None, None]
            for n in range(6):
                br, hf, i = n // 2, n % 2, n % 2
                for j in range(4):
                    if j % 2 == 0:
                        p = fd.next()
                    b, o = feat(p, (j % 2) * 128, XS)
                    k = 18 + 24 * l + 8 * br + 4 * hf + j
                    a = b.free = fn(SG[:, i, j, :], b.ap[:, 0:256], ACT.Sigmoid, o, sf[i], bias=VT[:, k:k + 1])
                p = fd.next()
                for j in range(4):
                    m = 4 * hf + j
                    b, o = feat(p, j * 128, ots(br), nk=4)
                    if br == 0:
                        b.free = tt(MX[:, m, :], b.ap[:, 0:256], SG[:, i, j, :], ALU.mult, o, a)
                    else:
                        q = j % 2
                        b.free = tt(MB[:, q, :], b.ap[:, 0:256], SG[:, i, j, :], ALU.mult, o, a, mf[q])
                        mf[q] = pool(lambda e, m=m, q=q: e.tensor_tensor(MX[:, m, :], MX[:, m, :], MB[:, q, :],
                                                                         ALU.add), b.free)
                        if br == 2:
                            k = slice(256 * m, 256 * m + 256)
                            split(MXH[:, k], MXL[:, k], MX[:, m, :], mf[q])
                sf[i] = Q.last["dve"]
            ms = tuple(v[:, :].rearrange("p (c t) -> p c t", c=8) for v in (MXH, MXL))
            deps = [Q.last["dve"], Q.last["act"]]
            for n in range(4):
                p = fd.next()
                for t in range(2):
                    b, o = toks(p, 256, t, ms, *deps)
                    xs = X[:, t, n * 256:n * 256 + 256]
                    b.free = tt(xs, xs, b.ap[:, 0:256], ALU.add, o)

        def ffn(l):
            mix_scope(f"f{l}", 1536, 5632, None)
            FH, FL = (y[:, :].rearrange("p (c t) -> p c t", t=256) for y in tens["Y"])
            SG = area(3072, 1024).rearrange("p (k t) -> p k t", k=4)
            FV = area(4096, 512).rearrange("p (k t) -> p k t", k=2)
            plan = []
            for n in range(0, D_FF, 512):
                for w in ("w_ffn1_2", "w_ffn3_2"):
                    plan += wplan(I[w][l][:, n:min(n + 512, D_FF)], 0, min(512, D_FF - n))
            halves = []
            k = 0
            for n in range(0, D_FF, 512):
                m = 2 if n + 512 <= D_FF else 1
                halves.append(m)
            w2 = I["w_ffn2_2"][l].rearrange("(c p) n -> p c n", p=128)
            for c0 in range(0, 22, 4):
                nk = min(4, 22 - c0)
                plan.append((w2[:, c0:c0 + nk, :], nk, 1024, "a"))
            fd = Feed(plan)
            sf = [None, None]
            vf = [None, None]
            n = 0
            for m in halves:
                acts = []
                for h in range(m):
                    p = fd.next()
                    for j in range(2):
                        b, o = feat(p, j * 128, XS)
                        i = 2 * h + j
                        a = b.free = fn(SG[:, i, :], b.ap[:, 0:256], ACT.Silu, o, sf[0])
                for h in range(m):
                    p = fd.next()
                    for j in range(2):
                        b, o = feat(p, j * 128, XS)
                        i = 2 * h + j
                        v = FV[:, i % 2, :]
                        b.free = tt(v, b.ap[:, 0:256], SG[:, i, :], ALU.mult, o, a, vf[i % 2])
                        vf[i % 2] = split(FH[:, n, :], FL[:, n, :], v, b.free)
                        n += 1
                sf[0] = Q.last["dve"]
            bb = [bank() for _ in range(4)]
            done = Q.last["dve"]
            for c0 in range(0, 22, 2):
                p = fd.next()
                for t in range(2):
                    for n in range(2):
                        b = bb[2 * t + n]
                        for c in range(2):
                            f = [v[:, c0 + c, t * 128:t * 128 + 128] for v in (FH, FL)]
                            w = [v[:, c, n * 512:n * 512 + 512] for v in (p.hi, p.lo)]
                            mm(b.ap, f[0], w[0], c0 + c == 0, False, b.free, p.got, done)
                            mm(b.ap, f[1], w[0], False, False)
                            o = mm(b.ap, f[0], w[1], False, c0 + c == 21)
                        if c0 == 20:
                            xs = X[:, t, n * 512:n * 512 + 512]
                            b.free = tt(xs, xs, b.ap, ALU.add, o)
                used(p, o)

        def block2():
            for l in range(2):
                if stop == 20 + 10 * l:
                    return
                mid_ = ctx.enter_context(ExitStack())
                nm = [f"{x}{l}{i}" for x in ("CH", "CL") for i in range(NCV)]
                cv = [mid_.enter_context(nc.sbuf_tensor(x, [128, 2048], FR)) for x in nm]
                tens["W"] = [(cv[i], cv[NCV + i]) for i in range(NCV)]
                tens["Y"] = [mid_.enter_context(nc.sbuf_tensor(f"{x}{l}", [128, 3072], FR)) for x in ("OH", "OL")]
                cvfree[:] = [None] * NCV
                tens["A"], = scope((f"AB{l}", 10752, F))
                tens["off"] = 3072
                w = I["w_in_2"][l]
                plan = wplan(w, 0, 1024) + wplan(w, 1024, 1408)
                plan += [(I[n][l].rearrange("(j p) n -> p j n", p=128), 16, 256, "raw")
                         for n in ("cmp_k_w1_2", "cmp_v_w1_2")]
                plan += wplan(w, 1304, 3864)
                for br in range(3):
                    wb = I["w_branch_%s_2" % "abc"[br]][l].rearrange("(c p) n -> p c n", p=128)
                    for h in range(2):
                        k = 1024 * br + 512 * h
                        plan += wplan(I["w_merge_2"][l], k, k + 512)
                        plan.append((wb[:, :, 512 * h:512 * h + 512], 4, 512, "n"))
                plan += rows(I["w_out_2"][l])
                fd = Feed(plan)
                rms_t(XS, NRM[:, 8 * l:8 * l + 8])
                Q.fence()
                Pb[:] = [area(3072 + 1024 * i, 1024).rearrange("p (t h k) -> p t h k", t=2, h=2) for i in range(2)]
                PTb[:] = [area(k, 1024).rearrange("p (h k t) -> p h k t", h=2, k=2) for k in (5120, 12800)]
                nsa(l, fd)
                Q.fence()
                diff(l, fd)
                Q.fence()
                sgu(l, fd)
                Q.fence()
                merge(l, fd)
                if stop == 21 + 10 * l:
                    return
                Q.fence()
                tens["A"], = scope((f"AC{l}", 9728, F))
                rms_t(XS, NRM[:, 16 + 8 * l:24 + 8 * l])
                Q.fence()
                mid_.close()
                ffn(l)
                Q.fence()
                if stop == 22 + 10 * l:
                    return
            tens["A"], = scope(("AZ", 9728, F))
            gr = group()
            G2 = area(5120, 1024)
            Q.dma("act", gr, G2, I["final_norm_2"].partition_broadcast(128), *[Q.last[x] for x in ("pe", "dve", "pool")])
            ss, r = small(2), small(2)
            J = area(3072, 1024)
            for t in range(2):
                o = fn(J, X[:, t, :], ACT.Square, acc=ss[:, t:t + 1])
            rsqrt(r, ss, 1.0 / 1024, 1e-6, o)
            for t in range(2):
                stt(X[:, t, :], X[:, t, :], r[:, t:t + 1], G2, ALU.mult, ALU.mult, gr)

        before_moe = []

        def finish():
            og = group()
            last = [Q.last["dve"], Q.last["pool"]]
            Q.dma("sp", og, out.rearrange("a (t p) d -> p (a t) d", p=128), X, *last)
            op = Op("sp", None, [og])
            Q.q["sp"].append(op)
            op.fn = lambda e: e.nop()

        def run():
            nonlocal gb, before_moe
            ln = []
            for l in range(2):
                mix_scope(f"m{l}", 10752, 2048, None)
                if l == 0:
                    plan = wplan(I["w_mem_kv"], 0, 512) + wplan(I["conv_w_in"][0], 0, 1792)
                else:
                    plan = wplan(I["moba_w_in"][0], 0, 2560)
                fd = Feed(plan + rows(I["w_o"][l]))
                if l == 0:
                    mem_kv(fd)
                    conv_mix(fd)
                else:
                    transposed(XS, X, *ln)
                    moba_mix(fd)
                ys = yts()
                deps = [Q.last["dve"], Q.last["act"]]
                for n in range(4):
                    p = fd.next()
                    for t in range(2):
                        b, o = toks(p, 256, t, ys, *deps)
                        xs = X[:, t, n * 256:n * 256 + 256]
                        b.free = stt(xs, xs, ALPHA, b.ap[:, 0:256], ALU.mult, ALU.add, o)
                before_moe = [Q.last.get(x) for x in ("pe", "act", "dve", "pool")]
                ln = layer_norm(gb)
                if stop == 10 * l + 1:
                    return
                gb = load_gb(I["ln2_g"][l], I["ln2_b"][l], *ln)
                Q.fence()
                ln = moe(l, gb, ln)
                if stop == 10 * l + 2:
                    return
                if l == 0:
                    gb = load_gb(I["ln1_g"][1], I["ln1_b"][1], *ln)
                Q.fence()
            b1.close()
            block2()

        run()
        finish()
        Q.number()
        block = ctx.enter_context(nc.Block())

        @block.sync
        def _(e):
            Q.emit("sp", e)

        @block.tensor
        def _(e):
            Q.emit("pe", e)

        @block.scalar
        def _(e):
            Q.emit("act", e)

        @block.vector
        def _(e):
            Q.emit("dve", e)

        @block.gpsimd
        def _(e):
            Q.emit("pool", e)


NAMES = ["x", "mem", "w_mem_kv", "conv_w_in", "conv_dw_w", "conv_dw_b", "conv_ln_g", "conv_ln_b", "moba_w_in", "w_o",
         "ln1_g", "ln1_b", "w_rg", "b_rg", "w_re", "b_re", "w_gate", "w_up", "w_down", "ln2_g", "ln2_b",
         "positions_2", "attn_norm_2", "w_in_2", "cmp_pos_k_2", "cmp_k_w1_2", "cmp_k_w2_2", "cmp_pos_v_2",
         "cmp_v_w1_2", "cmp_v_w2_2", "diff_lq1_2", "diff_lk1_2", "diff_lq2_2", "diff_lk2_2", "diff_subln_2",
         "sgu_norm_2", "sgu_w_2", "sgu_b_2", "w_branch_a_2", "w_branch_b_2", "w_branch_c_2", "w_merge_2",
         "b_merge_2", "w_out_2", "ffn_norm_2", "w_ffn1_2", "w_ffn3_2", "w_ffn2_2", "final_norm_2"]


def kernel(**inputs):
    import concourse.bacc as bacc
    from concourse.bass_utils import run_bass_kernel_spmd

    nc = bacc.Bacc("TRN2", target_bir_lowering=False, num_devices=1)
    arrays, aps = {}, {}
    for name in NAMES + ["cst"]:
        a = constants()[1] if name == "cst" else np.ascontiguousarray(inputs[name])
        arrays[f"in_{name}"] = a
        aps[name] = nc.dram_tensor(f"in_{name}", a.shape, mybir.dt.from_np(a.dtype), kind="ExternalInput").ap()
    out = nc.dram_tensor("out_x", (1, T, D), F, kind="ExternalOutput").ap()
    program(nc, aps, out)
    r = run_bass_kernel_spmd(nc, [arrays], core_ids=[0])
    return r.results[0]["out_x"]
```

```python
import math
import numpy as np
import concourse.bass as bass
from concourse import mybir
from contextlib import ExitStack

F = mybir.dt.float32
FR = mybir.dt.float32r
I32 = mybir.dt.int32
ACT = mybir.ActivationFunctionType
ALU = mybir.AluOpType
AX = mybir.AxisListType

D = 1024
T = 256
ALPHA = 4 ** 0.25
NRING = 4
NEXTRA = 4
UNIT = 4096
SCALE = 64 ** -0.5
NEG = -1e30
CAP = 64
D_FF = 2816


def constants():
    c = {}
    p = np.arange(128)
    c["ident"] = np.eye(128)
    c["ones"] = np.ones((128, 128))
    c["before"] = (p[:, None] < p[None, :]).astype(float)
    c["upto"] = (p[:, None] <= p[None, :]).astype(float)
    c["cmask"] = np.where(p[None, :] <= p[:, None], 0.0, NEG)
    perm = np.zeros((128, 128))
    for m in range(128):
        if m % 64 < 32:
            perm[m + 32, m] = -1.0
        else:
            perm[m - 32, m] = 1.0
    c["perm"] = perm
    c["iota"] = np.tile(np.arange(128), (128, 1))
    c["rev4"] = np.tile(np.arange(4, 0, -1), (128, 1))
    c["rev8"] = np.tile(np.arange(8, 0, -1), (128, 1))
    half = np.float32(10000.0) ** (-(np.arange(32, dtype=np.float32)) / np.float32(32))
    c["freq"] = half.astype(np.float32)[p % 32][:, None]
    n = np.arange(32)
    ok = np.stack([(n[None, :] < 15) & (n[None, :] * 16 + 31 <= (t * 128 + p)[:, None]) for t in range(2)], 1)
    c["m01"] = ok.reshape(128, 64).astype(float)
    c["madd"] = np.where(ok, 0.0, NEG).reshape(128, 64)
    at, cols = {}, []
    k = 0
    for name, a in c.items():
        at[name] = (k, a.shape[1])
        cols.append(a.astype(np.float32))
        k += a.shape[1]
    return at, np.ascontiguousarray(np.concatenate(cols, 1))


class Op:

    def __init__(self, eng, fn, deps):
        self.eng, self.fn, self.deps = eng, fn, deps
        self.sig = False
        self.n = 0


class Group:

    def __init__(self, sem, base=0):
        self.sem, self.total = sem, base


class Queues:

    def __init__(self, sems):
        self.sems = sems
        self.q = {e: [] for e in ("pe", "act", "dve", "pool", "sp")}
        self.last = {}
        self.fences = {e: [] for e in self.q}

    def add(self, eng, fn, deps=(), chain=False):
        deps = [d for d in deps if d is not None] + self.fences[eng]
        self.fences[eng] = []
        if chain and eng in self.last:
            deps.append(self.last[eng])
        for d in deps:
            if isinstance(d, Op):
                d.sig = True
        op = Op(eng, fn, deps)
        self.q[eng].append(op)
        self.last[eng] = op
        return op

    def pe(self, fn, *deps):
        return self.add("pe", fn, deps)

    def act(self, fn, *deps):
        return self.add("act", fn, deps, True)

    def dve(self, fn, *deps):
        return self.add("dve", fn, deps, True)

    def pool(self, fn, *deps):
        return self.add("pool", fn, deps, True)

    def dma(self, eng, group, out, in_, *deps):
        deps = [d for d in deps if d is not None]
        for d in deps:
            if isinstance(d, Op):
                d.sig = True
        op = Op(eng, lambda e, s=group.sem: e.dma_start(out, in_).then_inc(s, 16), [*deps])
        op.n = -1
        self.q[eng].append(op)
        group.total += 16

    def fence(self):
        for e in ("pe", "act", "dve", "pool"):
            self.fences[e] = [o for x, o in self.last.items() if x != e]

    def yield_to_pe(self):
        for e in ("act", "dve", "pool"):
            self.fences[e] = [o for x, o in self.last.items() if x != e]

    def number(self):
        for ops in self.q.values():
            n = 0
            for o in ops:
                if o.sig:
                    n += 1
                    o.n = n

    def emit(self, eng, e):
        seen = {}
        for o in self.q[eng]:
            need = {}
            for d in o.deps:
                if isinstance(d, Op):
                    s, v = self.sems[d.eng], d.n
                elif isinstance(d, Group):
                    s, v = d.sem, d.total
                else:
                    s, v = d
                k = id(s)
                if seen.get(k, 0) < v and need.get(k, (s, 0))[1] < v:
                    need[k] = (s, v)
            for k, (s, v) in need.items():
                e.wait_ge(s, v)
                seen[k] = v
            ins = o.fn(e)
            if o.sig:
                ins.then_inc(self.sems[eng], 1)


class Bank:

    def __init__(self, ap):
        self.ap, self.free = ap, None


class Unit:

    def __init__(self, ap, got):
        self.ap, self.got, self.free = ap, got, None


def program(nc, I, out, stop=99):
    at, _ = constants()
    ctx = ExitStack()
    with ctx:
        def sb(name, n, dt=F):
            return ctx.enter_context(nc.sbuf_tensor(name, [128, n], dt))

        sems = {e: ctx.enter_context(nc.semaphore("s_" + e)) for e in ("pe", "act", "dve", "pool", "sp")}
        Q = Queues(sems)
        pe, act, dve, pool = Q.pe, Q.act, Q.dve, Q.pool
        nsem = [0]

        def group():
            nsem[0] += 1
            return Group(ctx.enter_context(nc.semaphore(f"d{nsem[0]}")))

        class Slot:

            def __init__(self, ap, i):
                self.ap, self.sem, self.n, self.unit = ap, ctx.enter_context(nc.semaphore(f"r{i}")), 0, None
                self.after = []

        ring = [Slot(sb(f"ring{i}", UNIT)[:, :], i) for i in range(NRING)]
        extra = [Slot(None, NRING + i) for i in range(NEXTRA)]
        order = [0]

        def load(src, a, n, slots=None):
            if slots is None:
                sl = ring[order[0] % NRING]
                order[0] += 1
            else:
                sl = slots[0]
                slots.append(slots.pop(0))
            ap = sl.ap[:, 0:a * n].rearrange("p (a n) -> p a n", a=a)
            sl.n += 16
            u = Unit(ap, (sl.sem, sl.n))
            deps = sl.after
            if sl.unit is not None:
                deps = [*deps, sl.unit.free]
            Q.dma("sp", Group(sl.sem), ap, src, *deps)
            sl.unit, sl.after = u, []
            return u

        def scope(*spec):
            with ExitStack() as s2:
                return [s2.enter_context(nc.sbuf_tensor(name, [128, n], dt)) for name, n, dt in spec]

        def major(w, n0, n1):
            return w.rearrange("(p c) n -> p c n", p=128)[:, :, n0:n1]

        X = sb("X", 2048)[:, :].rearrange("p (t d) -> p t d", t=2)
        XS = None
        _, cst_np = constants()
        CST = sb("CST", cst_np.shape[1])
        SM = sb("SM", 512)
        VT = sb("VT", 132)
        WR = sb("WR", 2 * 8 * 36)
        BR = sb("BR", 72)
        W2 = sb("W2", 512)
        CS = sb("CS", 512)
        FLAG = sb("FLAG", 2, I32)
        NLAM = sb("NLAM", 2)[:, :]
        ps = ctx.enter_context(nc.psum_tensor("ps", [128, 8, 512], F))
        banks = [Bank(ps[:, i, :]) for i in range(8)]
        turn = [0]
        held = [0]

        def hold(n):
            held[0] = n

        def bank():
            turn[0] += 1
            return banks[turn[0] % (8 - held[0])]

        def C(name):
            k, n = at[name]
            return CST[:, k:k + n]

        smn = [0]

        def small(n):
            if smn[0] + n > 512:
                smn[0] = 0
            a = SM[:, smn[0]:smn[0] + n]
            smn[0] += n
            return a

        DW = sb("DW", 186)[:, :]
        b1 = ctx.enter_context(ExitStack())
        GB, MK, MV = [b1.enter_context(nc.sbuf_tensor(name, [128, n], F))
                      for name, n in (("GB", 2048), ("MK", 1024), ("MV", 512))]
        GB = GB[:, :].rearrange("p (g d) -> p g d", g=2)
        MK = MK[:, :].rearrange("p (j h m) -> p j h m", j=2, h=2)
        MV = MV[:, :].rearrange("p (k d) -> p k d", k=2)
        NCV = 2
        tens = {}

        def eights(t):
            return t[:, 0:2048].rearrange("p (c t) -> p c t", c=8)

        def mix_scope(tag):
            nonlocal XS
            spec = [(f"WH{tag}{i}", 2048, FR) for i in range(NCV)] + [(f"WL{tag}{i}", 2048, FR) for i in range(NCV)]
            spec += [(f"{k}{tag}", 2048, FR) for k in ("XH", "XL", "YH", "YL")]
            t = scope(*spec, (f"AR{tag}", 10752, F))
            tens["W"] = [(t[i], t[NCV + i]) for i in range(NCV)]
            XS = (eights(t[-5]), eights(t[-4]))
            tens["Y"] = t[-3:-1]
            tens["A"] = t[-1]
            cvfree[:] = [None] * NCV

        cvfree = [None] * NCV

        def area(k, n):
            k -= tens.get("off", 0)
            return tens["A"][:, k:k + n]

        def tr(out, in_, *deps):
            k = in_.shape[0]
            return pe(lambda e: e.transpose(out, in_, C("ident")[0:k, 0:k]), *deps)

        def mm(out, l, r, start, stop, *deps):
            return pe(lambda e: e.matmul(out, l, r, start=start, stop=stop), *deps)

        def vcopy(out, in_, *deps):
            return dve(lambda e: e.tensor_copy(out, in_), *deps)

        def acopy(out, in_, *deps):
            return act(lambda e: e.activation(out, in_, ACT.Copy), *deps)

        def qcopy(out, in_, *deps):
            return act(lambda e: e.activation(out, in_, ACT.Copy, scale=SCALE), *deps)

        def pcopy(out, in_, *deps):
            return pool(lambda e: e.tensor_copy(out, in_), *deps)

        cp = [0]

        def copy(out, in_, *deps):
            cp[0] += 1
            return (vcopy if cp[0] % 2 else acopy)(out, in_, *deps)

        def tt(out, a, b, op, *deps):
            return dve(lambda e: e.tensor_tensor(out, a, b, op), *deps)

        def ts(out, a, s1, s2, op0, op1, *deps):
            return dve(lambda e: e.tensor_scalar(out, a, s1, s2, op0, op1) if op1 is not None
                       else e.tensor_scalar(out, a, s1, None, op0), *deps)

        def stt(out, a, s, b, op0, op1, *deps):
            return dve(lambda e: e.scalar_tensor_tensor(out, a, s, b, op0, op1), *deps)

        def fn(out, in_, f, *deps, bias=0.0, scale=1.0, acc=None):
            if acc is None:
                return act(lambda e: e.activation(out, in_, f, bias=bias, scale=scale), *deps)
            return act(lambda e: e.activation(out, in_, f, bias=bias, scale=scale, accum_out=acc), *deps)

        def rmax(out, in_, *deps):
            return dve(lambda e: e.reduce_max(out, in_, AX.X), *deps)

        def rsum(out, in_, *deps):
            return dve(lambda e: e.reduce_sum(out, in_, AX.X), *deps)

        def recip(out, in_, *deps):
            return dve(lambda e: e.reciprocal(out, in_), *deps)

        def bc(a, shape):
            return a.broadcast_to(shape)

        def mid(a, k):
            return a.unsqueeze(1).broadcast_to([a.shape[0], k, a.shape[1]])

        def end(a, k):
            return a.unsqueeze(len(a.shape)).broadcast_to([*a.shape, k])

        def warm(f):
            fn(small(1), C("ones")[:, 0:1], f)

        def rsqrt(out, v, scale, eps, *deps):
            w = small(v.shape[1])
            o = ts(w, v, scale, eps, ALU.mult, ALU.add, *deps)
            o = fn(w, w, ACT.Sqrt, o)
            return recip(out, w, o)

        def split(hi, lo, v, *deps):
            a = act(lambda e: e.activation(hi, v, ACT.Copy), *deps)
            return tt(lo, v, hi.bitcast(F), ALU.subtract, a)

        def vsplit(hi, lo, v, *deps):
            vcopy(hi, v, *deps)
            return tt(lo, v, hi.bitcast(F), ALU.subtract)

        cvn = [0]

        class Piece:
            pass

        def convert(u, ap, a, n):
            i = cvn[0] % NCV
            cvn[0] += 1
            H, L = (t[:, 0:a * n].rearrange("p (a n) -> p a n", a=a) for t in tens["W"][i])
            for q in (slice(0, a // 2), slice(a // 2, a)):
                x = act(lambda e, q=q: e.activation(H[:, q], ap[:, q], ACT.Copy), u.got, cvfree[i])
                o = tt(L[:, q], ap[:, q], H[:, q].bitcast(F), ALU.subtract, x, u.got, cvfree[i])
            u.free = o
            p = Piece()
            p.hi, p.lo, p.got, p.i = H, L, o, i
            return p

        class Feed:

            def __init__(self, plan, ahead=1):
                self.todo, self.made, self.ahead = [], [], ahead
                for src, a, n, how in plan:
                    self.todo.append((src, a, n, how))
                self.plan = iter(self.todo)
                self.half = None
                self.n = 0

            def make(self):
                if self.half is None:
                    nxt = next(self.plan, None)
                    if nxt is None:
                        return
                    src, a, n, how = nxt
                    u = load(src, a, n)
                    if how == "raw":
                        self.made.append(u)
                        return
                    if how == "a" and a * n > 2048:
                        k = (a + 1) // 2
                        parts = [(u.ap[:, 0:k], k, n), (u.ap[:, k:a], a - k, n)]
                    elif a * n <= 2048:
                        parts = [(u.ap, a, n)]
                    else:
                        parts = [(u.ap[:, :, 0:256], a, 256), (u.ap[:, :, 256:n], a, n - 256)]
                    self.half = (u, parts)
                u, parts = self.half
                self.made.append(convert(u, *parts[0]))
                self.half = (u, parts[1:]) if len(parts) > 1 else None

            def next(self):
                while len(self.made) < self.n + 1 + self.ahead:
                    k = len(self.made)
                    self.make()
                    if len(self.made) == k:
                        break
                self.n += 1
                return self.made[self.n - 1]

        def used(p, o):
            cvfree[p.i] = o

        mix_scope("m0")
        g0, gm, gx, g1, g2 = group(), group(), group(), group(), group()
        MEM = area(0, 2048).rearrange("p (t d) -> p t d", t=2)
        Q.dma("act", g0, CST[:, :], I["cst"])
        Q.dma("sp", gm, MEM, I["mem"][0].rearrange("(t p) d -> p t d", p=128))
        Q.dma("act", gx, X, I["x"][0].rearrange("(t p) d -> p t d", p=128))
        VR = area(2048, 128)
        PR = area(2176, 128)
        DWR = area(2304, 768)
        for k, (name, n) in enumerate((("conv_dw_b", 6), ("conv_ln_g", 6), ("conv_ln_b", 6))):
            Q.dma("pool", g1, VR[6 * k:6 * k + 6, :], I[name].rearrange("a (j p) -> (a j) p", p=128))
        Q.dma("pool", g1, VR[18:66, :], I["b_merge_2"].rearrange("l (j p) -> (l j) p", p=128))
        Q.dma("pool", g1, VR[66:68, :], I["diff_subln_2"])
        for k, name in enumerate(("cmp_pos_k_2", "cmp_pos_v_2")):
            Q.dma("pool", g1, PR[32 * k:32 * k + 32, :], I[name].rearrange("l (j i) d -> (l j) (i d)", i=2))
        Q.dma("pool", g1, DWR[0:31, :], I["conv_dw_w"][0])
        for l in range(2):
            w = WR[:, 288 * l:288 * l + 288].rearrange("p (c n) -> p c n", c=8)
            Q.dma("pool", g2, w[:, :, 0:4], major(I["w_rg"][l], 0, 4))
            Q.dma("pool", g2, w[:, :, 4:36], major(I["w_re"][l], 0, 32))
            Q.dma("pool", g2, BR[:, 36 * l:36 * l + 4], I["b_rg"][l].partition_broadcast(128))
            Q.dma("pool", g2, BR[:, 36 * l + 4:36 * l + 36], I["b_re"][l].partition_broadcast(128))
            for k, name in enumerate(("cmp_k_w2_2", "cmp_v_w2_2")):
                Q.dma("pool", g2, W2[:, 256 * l + 128 * k:256 * l + 128 * k + 128].rearrange("p (c d) -> p c d", c=2),
                      I[name][l].rearrange("(c p) d -> p c d", p=128))

        def load_gb(g, b, *deps):
            gr = group()
            Q.dma("act", gr, GB[:, 0, :], g.partition_broadcast(128), *deps)
            if b is not None:
                Q.dma("act", gr, GB[:, 1, :], b.partition_broadcast(128), *deps)
            return gr

        gb = load_gb(I["ln1_g"][0], I["ln1_b"][0])

        def transposed(dst, src, *deps):
            for t in range(2):
                sv = src[:, t, :].rearrange("p (d c) -> p c d", c=8)
                need = deps[t:t + 1] if len(deps) == 2 else deps
                for c0 in (0, 4):
                    b = bank()
                    for c in range(4):
                        o = tr(b.ap[:, c * 128:c * 128 + 128], sv[:, c0 + c, :], b.free, *need)
                    pv = b.ap.rearrange("p (c t) -> p c t", c=4)
                    q = (slice(None), slice(c0, c0 + 4), slice(128 * t, 128 * t + 128))
                    if isinstance(dst, tuple):
                        b.free = split(dst[0][q], dst[1][q], pv, o)
                    else:
                        b.free = copy(dst[q], pv, o)

        def feat(p, n0, src, *deps, nk=8):
            b = bank()
            out = b.ap[:, 0:256]
            for c in range(nk):
                w = (p.hi[:, c, n0:n0 + 128], p.lo[:, c, n0:n0 + 128])
                mm(out, w[0], src[0][:, c, :], c == 0, False, b.free, p.got, *deps)
                mm(out, w[0], src[1][:, c, :], False, False)
                o = mm(out, w[1], src[0][:, c, :], False, c == nk - 1)
            used(p, o)
            return b, o

        def toks(p, n, t, src, ready=None, order_=None):
            b = bank()
            out = b.ap[:, 0:n]
            cs = order_ or list(range(8))
            for c in cs:
                x = [v[:, c, t * 128:t * 128 + 128] for v in src]
                mm(out, x[0], p.hi[:, c, 0:n], c == cs[0], False, b.free, p.got, ready and ready[c])
                mm(out, x[1], p.hi[:, c, 0:n], False, False)
                o = mm(out, x[0], p.lo[:, c, 0:n], False, c == cs[-1])
            used(p, o)
            return b, o

        class Stats:

            def __init__(self, parts):
                self.k, self.n = parts, [0, 0]
                self.st = small(12 * parts).rearrange("p (t g s) -> p t g s", t=2, g=parts)

            def take(self, t, v):
                g = self.n[t]
                self.n[t] += 1
                return dve(lambda e, o=self.st[:, t, g, :]: e.bn_stats(o, v))

        def layer_norm(t, gr, st, src=X):
            mv, w = small(2), small(1)
            o = dve(lambda e: e.bn_aggr(mv, st.st[:, t]))
            o = ts(w, mv[:, 1:2], 1.0, 1e-5, ALU.mult, ALU.add)
            o = fn(w, w, ACT.Sqrt, o)
            stt(X[:, t, :], src[:, t, :], mv[:, 0:1], GB[:, 0, :], ALU.subtract, ALU.mult, gr)
            recip(w, w, o)
            return stt(X[:, t, :], X[:, t, :], w, GB[:, 1, :], ALU.mult, ALU.add)

        Pb = [None, None]
        PTb = [None, None]
        pbfree = [None, None]
        ptfree = [None, None]

        def scores(q, kp, causal, *deps):
            S, B, O = [], [], []
            for t in range(2):
                ks = 128 * (t + 1) if causal else 256
                b = bank()
                v = b.ap[:, 0:2 * ks].rearrange("p (h k) -> p h k", h=2)
                o = mm(v, q[:, t * 128:t * 128 + 128], kp[:, :, 0:ks], True, not causal, b.free, *deps)
                if causal:
                    o = mm(v[:, :, 128 * t:128 * t + 128], C("ident"), mid(C("cmask"), 2), False, True)
                O.append(o)
                S.append(v)
                B.append(b)
            return S, B, O, causal

        def exped(i, sc):
            S, B, O, causal = sc
            P = Pb[i]
            sm, n = small(4), small(4)
            nm = [dve(lambda e, t=t: e.reduce_max(n[:, 2 * t:2 * t + 2], S[t], AX.X, negate=True), O[t])
                  for t in range(2)]
            for t in range(2):
                ks = S[t].shape[2]
                for h in range(2):
                    k = 2 * t + h
                    B[t].free = fn(P[:, t, h, 0:ks], S[t][:, h, :], ACT.Exp, nm[t], pbfree[i],
                                   bias=n[:, k:k + 1], acc=sm[:, k:k + 1])
            return i, P, sm, [b.free for b in B], causal

        def normed(st, gate, lam):
            i, P, sm, got, causal = st
            last = []
            r4 = small(4)
            o = recip(r4, sm, *got)
            rt_ = r4.rearrange("p (t h) -> p t h", t=2)
            if gate is not None:
                o = tt(rt_, rt_, gate, ALU.mult)
            if lam is not None:
                ts(rt_[:, :, 1], rt_[:, :, 1], lam, None, ALU.mult, None)
            for t in range(2):
                ks = 128 * (t + 1) if causal else 256
                r = rt_[:, t, :]
                if lam is None and (t or not causal):
                    for h in range(2):
                        o = ts(P[:, t, h, 0:ks], P[:, t, h, 0:ks], r[:, h:h + 1], None, ALU.mult, None)
                elif lam is None:
                    pv = P[:, t, :, 0:ks]
                    o = pool(lambda e, pv=pv, r=r, ks=ks: e.tensor_tensor(pv, pv, end(r, ks), ALU.mult), o)
                else:
                    a, c = P[:, t, 1, 0:ks], P[:, t, 0, 0:ks]
                    ts(c, c, r[:, 0:1], None, ALU.mult, None)
                    o = stt(c, a, r[:, 1:2], c, ALU.mult, ALU.add)
                last.append(o)
            return last

        def turned(st, last, heads=2):
            i, P, sm, got, causal = st
            PT = PTb[i]
            for t in range(2):
                nk = t + 1 if causal else 2
                b = bank()
                for h in range(heads):
                    for k in range(nk):
                        o = tr(b.ap[:, (h * nk + k) * 128:(h * nk + k) * 128 + 128],
                               P[:, t, h, k * 128:k * 128 + 128], b.free, last[t])
                b.free = (acopy if t else vcopy)(
                    PT[:, 0:heads, 0:nk, t * 128:t * 128 + 128],
                    b.ap[:, 0:heads * nk * 128].rearrange("p (h k t) -> p h k t", h=heads, k=nk), o, ptfree[i])
            pbfree[i] = o
            return i, PT, [Q.last["dve"], Q.last["act"]], causal

        def values(pt, v, b, first, lastone, *deps, heads=2):
            i, PT, got, causal = pt
            for h in range(heads):
                ob = b.ap[64 * h:64 * h + 64, :] if heads == 2 else b.ap
                for k in range(2):
                    t0 = 128 * k if causal else 0
                    o = mm(ob[:, t0:256], v(k, h), PT[:, h, k, t0:256], first and k == 0,
                           lastone and k == 1, b.free, *got, *deps)
            ptfree[i] = o
            return o

        def attend(jobs):
            n = len(jobs)
            st, pt = {}, {}
            for j in range(n + 2):
                if j < n:
                    q, kp, causal, gate, lam, *deps = jobs[j][0]
                    sc = scores(q, kp, causal, *deps)
                if 0 < j <= n:
                    k = j - 1
                    last = normed(st[k], jobs[k][0][3], jobs[k][0][4])
                if j < n:
                    st[j] = exped(j % 2, sc)
                if j > 1:
                    jobs[j - 2][1](pt[j - 2])
                if 0 < j <= n:
                    pt[k] = turned(st[k], last, jobs[k][2] if len(jobs[k]) > 2 else 2)

        COS, SIN = CS[:, 0:256], CS[:, 256:512]

        def vectors():
            b = bank()
            o = tr(b.ap[:, 0:68], VR[0:68, :], b.free, g1)
            o = tr(b.ap[:, 68:132], PR[0:64, :])
            b.free = vcopy(VT[:, 0:132], b.ap[:, 0:132], o)
            b = bank()
            for j in range(6):
                o = tr(b.ap[:, j * 31:j * 31 + 31], DWR[0:31, j * 128:j * 128 + 128], b.free)
            b.free = vcopy(DW, b.ap[:, 0:186], o)

        def angles():
            g = group()
            LAM, IS = (area(10900, 256), SIN), COS.bitcast(I32)
            for l in range(2):
                for k, name in enumerate(("diff_lq1_2", "diff_lk1_2", "diff_lq2_2", "diff_lk2_2")):
                    Q.dma("pool", g, LAM[l][:, 64 * k:64 * k + 64], I[name][l].partition_broadcast(128), *before_moe)
            Q.dma("pool", g, IS, I["positions_2"][0].partition_broadcast(128), *before_moe)
            yield
            ls, le = small(4), small(4)
            for l in range(2):
                lv = LAM[l].rearrange("p (k q d) -> p k q d", k=2, q=2)
                tt(lv[:, :, 0, :], lv[:, :, 0, :], lv[:, :, 1, :], ALU.mult, g)
                o = rsum(ls[:, 2 * l:2 * l + 2], lv[:, :, 0, :])
            o = fn(le, ls, ACT.Exp, o)
            l4 = le.rearrange("p (l k) -> p l k", k=2)
            tt(NLAM, l4[:, :, 1], l4[:, :, 0], ALU.subtract, o)
            for l in range(2):
                ts(NLAM[:, l:l + 1], NLAM[:, l:l + 1], -(0.8 - 0.6 * math.exp(-0.3 * l)), None, ALU.add, None)
            ang, kk = SIN, COS
            vcopy(ang, IS, g)
            ts(ang, ang, C("freq"), None, ALU.mult, None)
            ts(kk, ang, 1.0 / (2 * math.pi), 12582912.0, ALU.mult, ALU.add)
            ts(kk, kk, -12582912.0, None, ALU.add, None)
            c1 = 6.28125
            c2 = float(np.float32(np.round((2 * math.pi - c1) * 2 ** 20) / 2 ** 20))
            c3 = float(np.float32(2 * math.pi - c1 - c2))
            for c in (c1, c2, c3):
                stt(ang, kk, -c, ang, ALU.mult, ALU.add)
            pi = float(np.nextafter(np.float32(math.pi), np.float32(0)))
            ts(ang, ang, pi, -pi, ALU.min, ALU.max)
            ts(kk, ang, math.pi / 2, -2 * math.pi, ALU.is_gt, ALU.mult)
            stt(kk, ang, math.pi / 2, kk, ALU.add, ALU.add)
            o = ts(kk, kk, pi, -pi, ALU.min, ALU.max)
            fn(COS, kk, ACT.Sin, o)
            fn(SIN, ang, ACT.Sin)

        def mix_areas():
            Pb[:] = [area(1024 * i, 1024).rearrange("p (t h k) -> p t h k", t=2, h=2) for i in range(2)]
            PTb[:] = [area(k, 1024).rearrange("p (h k t) -> p h k t", h=2, k=2) for k in (2048, 9728)]
            return area(3072, 512).rearrange("p (j t) -> p j t", j=2)

        def yt(j):
            return [y[:, 256 * j:256 * j + 256] for y in tens["Y"]]

        ydone = [None] * 8

        def yts():
            return tuple(y[:, :].rearrange("p (c t) -> p c t", t=256) for y in tens["Y"])

        def wplan(w, lo, hi):
            return [(major(w, n, min(n + 512, hi)), 8, min(512, hi - n), "n") for n in range(lo, hi, 512)]

        def rows(w, step=512):
            v = w.rearrange("(c p) n -> p c n", p=128)
            return [(v[:, :, n:n + step], 8, step, "n") for n in range(0, 1024, step)]

        def mem_jobs(QM):
            jobs = []
            for j in range(2):
                def fin(pt, j=j):
                    b = bank()
                    o = values(pt, lambda k, h: MV[:, k, j * 128 + h * 64:j * 128 + h * 64 + 64], b, True, True)
                    b.free = ydone[6 + j] = vsplit(*yt(6 + j), b.ap[:, 0:256], o)
                jobs.append(((QM[:, j, :], MK[:, j, :, :], False, None, None), fin))
            return jobs

        def mem_kv(fd):
            pool(lambda e: e.memset(MK, 0.0))
            mz = pool(lambda e, a=area(3584, 1716): e.memset(a, 0.0))
            ms = tuple(eights(y) for y in tens["Y"])
            transposed(ms, MEM, g0, gm, None)
            ready = [Q.last["dve"], Q.last["act"]]
            p = fd.next()
            for j in range(2):
                b, o = feat(p, j * 128, ms, *ready)
                vcopy(MK[0:64, j, 0, :], b.ap[0:64, 0:256], o, mz)
                b.free = vcopy(MK[64:128, j, 1, :], b.ap[64:128, 0:256])
            transposed(XS, X, gx)
            p = fd.next()
            for t in range(2):
                b, o = toks(p, 256, t, ms)
                b.free = acopy(MV[:, t, :], b.ap[:, 0:256], o)
            vectors()

        def conv_mix(fd):
            QM = mix_areas()
            HP = area(3584, 1716).rearrange("p (j t) -> p j t", j=6)
            A = area(5300, 1536).rearrange("p (j t) -> p j t", j=6)
            HC = area(6836, 1536).rearrange("p (j t) -> p j t", j=6)
            G = area(8372, 512)
            gf = [None, None]
            ready = [Q.last["dve"], Q.last["act"]]
            for n in range(14):
                if n % 2 == 0:
                    p = fd.next()
                b, o = feat(p, (n % 2) * 128, XS, *ready)
                pv = b.ap[:, 0:256]
                if n < 6:
                    b.free = copy(A[:, n, :], pv, o)
                elif n < 12:
                    j = n - 6
                    g = G[:, (j % 2) * 256:(j % 2) * 256 + 256]
                    o = b.free = fn(g, pv, ACT.Sigmoid, o, gf[j % 2])
                    gf[j % 2] = tt(HP[:, j, 30:286], A[:, j, :], g, ALU.mult, o)
                else:
                    b.free = qcopy(QM[:, n - 12, :], pv, o)
            mj = mem_jobs(QM)
            sc = [scores(*mj[j][0][:3], Q.last["act"]) for j in range(2)]
            ready = Q.last["dve"]
            dw = DW.rearrange("p (j k) -> p j k", j=6)
            DG = area(8372, 1024).rearrange("p (n m) -> p n m", n=8)
            dgf = [Q.last["dve"]] * 8
            KP2, dn, jd = 9, 0, {}
            cb = [bank() for _ in range(4)]
            for k in range(31):
                if k == 6:
                    at_ = [exped(j, sc[j]) for j in range(2)]
                    warm(ACT.Sqrt)
                    rows_ = [normed(at_[j], None, None) for j in range(2)]
                for j in (3, 4, 5, 2) if k < KP2 else (3, 4, 5):
                    i = dn % 8
                    dn += 1
                    lastk = KP2 - 1 if j == 2 else 30
                    o = fn(DG[:, i, :], C("ident"), ACT.Identity, dgf[i], scale=dw[:, j, k:k + 1])
                    dgf[i] = mm(cb[j - 3].ap[:, 0:256], DG[:, i, :], HP[:, j, k:k + 256], k == 0, k == lastk,
                                 cb[j - 3].free, o, ready)
                    jd[j] = dgf[i]
            for k in range(31):
                for j in range(3):
                    if k < KP2 and j == 2:
                        continue
                    if k == (KP2 if j == 2 else 0):
                        ts(HC[:, j, :], HP[:, j, k:k + 256], dw[:, j, k:k + 1], VT[:, j:j + 1], ALU.mult, ALU.add)
                    else:
                        dve(lambda e, j=j, k=k: e.scalar_tensor_tensor(
                            HC[:, j, :], HP[:, j, k:k + 256], dw[:, j, k:k + 1], HC[:, j, :], ALU.mult, ALU.add))
            for j in range(3, 6):
                cb[j - 3].free = fn(HC[:, j, :], cb[j - 3].ap[:, 0:256], ACT.Identity, jd[j],
                                    bias=VT[:, j:j + 1])
            cb[3].free = tt(HC[:, 2, :], HC[:, 2, :], cb[3].ap[:, 0:256], ALU.add, jd[2])
            both = [Q.last["dve"], Q.last["act"]]
            b = bank()
            for j in range(6):
                o = mm(b.ap[:, 0:256], C("ones"), HC[:, j, :], j == 0, j == 5, b.free, *both)
            mu = area(5300, 256)
            b.free = ts(mu, b.ap[:, 0:256], 1.0 / 768, None, ALU.mult, None, o)
            tt(HC, HC, mid(mu, 6), ALU.subtract)
            sq = area(3584, 1536).rearrange("p (j t) -> p j t", j=6)
            o = fn(sq, HC, ACT.Square, Q.last["dve"], *both)
            pt = [turned(at_[j], rows_[j]) for j in range(2)]
            b = bank()
            for j in range(6):
                o2 = mm(b.ap[:, 0:256], C("ones"), sq[:, j, :], j == 0, j == 5, b.free, o)
            for j in range(2):
                mj[j][1](pt[j])
            sd = area(5556, 256)
            b.free = ts(sd, b.ap[:, 0:256], 1.0 / 768, 1e-5, ALU.mult, ALU.add, o2)
            o = fn(sd, sd, ACT.Sqrt, b.free)
            recip(mu, sd, o)
            o = tt(HC, HC, mid(mu, 6), ALU.mult)
            for j in range(6):
                y = sq[:, j, :]
                a = fn(y, HC[:, j, :], ACT.Silu, o, bias=VT[:, 12 + j:13 + j], scale=VT[:, 6 + j:7 + j])
                hi, lo = yt(j)
                vcopy(hi, y, a)
                ydone[j] = tt(lo, y, hi.bitcast(F), ALU.subtract)

        def moba_mix(fd):
            QM = mix_areas()
            QQ = area(3584, 1536).rearrange("p (j t) -> p j t", j=6)
            KP = area(5120, 3072).rearrange("p (j h t) -> p j h t", j=6, h=2)
            V = area(8192, 1536).rearrange("p (t d) -> p t d", t=2)
            ready, kz = [Q.last["dve"], Q.last["act"]], Q.last["pool"]
            for n in range(12):
                if n % 2 == 0:
                    p = fd.next()
                b, o = feat(p, (n % 2) * 128, XS, *ready)
                if n < 6:
                    b.free = qcopy(QQ[:, n, :], b.ap[:, 0:256], o)
                else:
                    vcopy(KP[0:64, n - 6, 0, :], b.ap[0:64, 0:256], o, kz)
                    b.free = vcopy(KP[64:128, n - 6, 1, :], b.ap[64:128, 0:256])
            for k in range(3):
                p = fd.next()
                for t in range(2):
                    b, o = toks(p, 256, t, XS)
                    b.free = copy(V[:, t, 256 * k:256 * k + 256], b.ap[:, 0:256], o)
            p = fd.next()
            for j in range(2):
                b, o = feat(p, j * 128, XS)
                b.free = qcopy(QM[:, j, :], b.ap[:, 0:256], o)
            ins = [Q.last["dve"], Q.last["act"]]
            jobs = []
            for j in range(6):
                def fin(pt, j=j):
                    b = bank()
                    o = values(pt, lambda k, h: V[:, k, j * 128 + h * 64:j * 128 + h * 64 + 64], b, True, True)
                    b.free = ydone[j] = vsplit(*yt(j), b.ap[:, 0:256], o)
                jobs.append(((QQ[:, j, :], KP[:, j, :, :], True, None, None, *ins), fin))
            attend(jobs + mem_jobs(QM))

        baton = [ctx.enter_context(nc.semaphore(f"f{i}")) for i in range(64)]

        def beyond(l, pos, comb, flag, main, sums):
            ACC = area(0, 2048).rearrange("p (t d) -> p t d", t=2)
            XF = area(2048, 1024).rearrange("p (c s) -> p c s", c=8)
            PQ = area(3072, 128)
            PW = area(3200, 128)
            WB = area(4096, 2048)
            G = area(6144, 256).rearrange("p (t s) -> p t s", t=2)
            GW = area(6400, 256).rearrange("p (t s) -> p t s", t=2)
            CT = area(6656, 256).rearrange("p (t s) -> p t s", t=2)
            H = area(8192, 512)
            HT = area(8704, 512).rearrange("p (c s) -> p c s", c=4)
            Y = area(9216, 1024)
            B = [b.ap for b in banks]
            pq = PQ.rearrange("p (w t e) -> p w t e", w=2, t=2)
            flat = [PQ.rearrange("p (q e) -> p q e", e=32), PW.rearrange("p (q e) -> p q e", e=32)]
            gate = I["w_gate"][l].rearrange("g e (p c) n -> (g e) p c n", p=128)
            upw = I["w_up"][l].rearrange("g e (p c) n -> (g e) p c n", p=128)
            dn = I["w_down"][l].rearrange("g e (p c) n -> (g e) p c n", p=128)

            def one():
                st = []

                def step(eng):
                    return lambda f: st.append((eng, f))

                @step("dve")
                def _(e, i):
                    for t in range(2):
                        r = e.tensor_scalar(G[:, t, :], C("iota"), pq[:, 0, t, 0:1], None, ALU.is_equal)
                    return r

                @step("dve")
                def _(e, i):
                    for t in range(2):
                        r = e.tensor_scalar(GW[:, t, :], G[:, t, :], pq[:, 1, t, 0:1], None, ALU.mult)
                    return r

                @step("pe")
                def _(e, i):
                    for c in range(8):
                        for t in range(2):
                            r = e.matmul(B[c // 4][:, (c % 4) * 128:(c % 4) * 128 + 128],
                                         X[:, t, :].rearrange("p (d c) -> p c d", c=8)[:, c, :], G[:, t, :],
                                         start=t == 0, stop=t == 1)
                    for t in range(2):
                        r = e.transpose(B[2][:, t * 128:t * 128 + 128], GW[:, t, :], C("ident"))
                    return r

                @step("dve")
                def _(e, i):
                    for k in range(2):
                        e.tensor_copy(XF[:, 4 * k:4 * k + 4, :], B[k].rearrange("p (c s) -> p c s", c=4))
                    return e.tensor_copy(CT, B[2][:, 0:256].rearrange("p (t s) -> p t s", t=2))

                for w, b in ((gate, 3), (upw, 4)):
                    for hf in range(2):
                        wv = WB.rearrange("p (c n) -> p c n", c=4)

                        @step("act dma")
                        def _(e, i, w=w, hf=hf, wv=wv):
                            return e.dma_start(wv, w[bass.ds(i, 1), :, 4 * hf:4 * hf + 4, :]
                                               .rearrange("a p c n -> (a p) c n"))

                        @step("pe")
                        def _(e, i, b=b, hf=hf, wv=wv):
                            for c in range(4):
                                r = e.matmul(B[b], XF[:, 4 * hf + c, :], wv[:, c, :],
                                             start=hf == 0 and c == 0, stop=hf == 1 and c == 3)
                            return r

                @step("act")
                def _(e, i):
                    return e.activation(H, B[3], ACT.Silu)

                @step("dve")
                def _(e, i):
                    return e.tensor_tensor(H, H, B[4], ALU.mult)

                @step("pe")
                def _(e, i):
                    for c in range(4):
                        r = e.transpose(B[5][:, c * 128:c * 128 + 128], H.rearrange("p (f c) -> p c f", c=4)[:, c, :],
                                        C("ident"))
                    return r

                @step("dve")
                def _(e, i):
                    return e.tensor_copy(HT, B[5].rearrange("p (c s) -> p c s", c=4))

                for hf in range(2):
                    wv = WB.rearrange("p (c n) -> p c n", c=2)

                    @step("act dma")
                    def _(e, i, hf=hf, wv=wv):
                        return e.dma_start(wv, dn[bass.ds(i, 1), :, 2 * hf:2 * hf + 2, :]
                                           .rearrange("a p c n -> (a p) c n"))

                    @step("pe")
                    def _(e, i, hf=hf, wv=wv):
                        for c in range(2):
                            for n in range(2):
                                r = e.matmul(B[6 + n], HT[:, 2 * hf + c, :], wv[:, c, n * 512:n * 512 + 512],
                                             start=hf == 0 and c == 0, stop=hf == 1 and c == 1)
                        return r

                @step("dve")
                def _(e, i):
                    for n in range(2):
                        r = e.tensor_copy(Y[:, n * 512:n * 512 + 512], B[6 + n])
                    return r

                @step("pe")
                def _(e, i):
                    for n in range(2):
                        for t in range(2):
                            r = e.matmul(B[2 * n + t], CT[:, t, :], Y[:, n * 512:n * 512 + 512], start=True, stop=True)
                    return r

                @step("dve")
                def _(e, i):
                    for n in range(2):
                        for t in range(2):
                            a = ACC[:, t, n * 512:n * 512 + 512]
                            r = e.tensor_tensor(a, a, B[2 * n + t], ALU.add)
                    return r

                @step("dve")
                def _(e, i):
                    e.tensor_copy(flat[1][:, :, 0:31], flat[0][:, :, 1:32])
                    return e.tensor_copy(flat[1][:, :, 31:32], flat[0][:, :, 0:1])

                @step("dve")
                def _(e, i):
                    return e.tensor_copy(PQ, PW)

                return st

            steps = one()

            def walk(me):
                def body(e, i):
                    for k, (eng, f) in enumerate(steps):
                        if eng.split()[0] != me:
                            continue
                        if k:
                            by = 16 if "dma" in steps[k - 1][0] else 1
                            e.wait_ge(baton[k - 1], by)
                            e.sem_clear(baton[k - 1])
                        f(e, i).then_inc(baton[k], 16 if "dma" in eng else 1)
                    if me == "dve":
                        e.wait_ge(baton[len(steps) - 1], 1)
                        e.sem_clear(baton[len(steps) - 1])

                def own(e, f):
                    f().then_inc(baton[63], 1)
                    e.wait_ge(baton[63], 1)
                    e.sem_clear(baton[63])

                def run(e):
                    v = e.value_load(FLAG[0:1, l:l + 1], min_val=0, max_val=1)
                    with e.If(v > 0):
                        for r in range(2):
                            if me == "dve":
                                if r == 0:
                                    own(e, lambda: e.tensor_scalar(pq[:, 0], pos, -float(CAP), None, ALU.add))
                                    own(e, lambda: e.tensor_copy(pq[:, 1], comb))
                                else:
                                    own(e, lambda: e.tensor_scalar(pq[:, 0], pq[:, 0], -128.0, None, ALU.add))
                            with e.Fori(0, 32) as i:
                                body(e, i)
                        if me == "dve":
                            for t in range(2):
                                for n in range(2):
                                    own(e, lambda t=t, n=n: e.bn_stats(sums.st[:, t, n, :],
                                                                       ACC[:, t, 512 * n:512 * n + 512]))
                return run

            for me in ("dve", "pe", "act"):
                for o in (flag, *main):
                    o.sig = True
                Q.q[me].append(Op(me, walk(me), [flag, *main]))

        def moe(l, gr_next, ln):
            ts_ = scope(*[(f"rx{l}{i}", UNIT, F) for i in range(NEXTRA)], (f"ARM{l}", 11156, F))
            tens["A"] = ts_[-1]
            k = order[0] % NRING
            slots = ring[k:] + ring[:k] + extra
            for i, sl in enumerate(extra):
                sl.ap, sl.after = ts_[i][:, :], list(before_moe)
                sl.unit = None
            warm(ACT.Exp)
            side = angles() if l == 0 else iter(())
            next(side, None)
            XT = area(2048, 2048).rearrange("p (c t) -> p c t", c=8)
            transposed(XT, X, *ln)
            ACC = area(0, 2048).rearrange("p (t d) -> p t d", t=2)
            XG = [area(2048 + 2048 * i, 2048).rearrange("p (c s) -> p c s", c=8) for i in range(2)]
            G = area(6144, 512).rearrange("p (t s) -> p t s", t=2)
            GW = area(6656, 512).rearrange("p (t s) -> p t s", t=2)
            CT = [area(7168 + 512 * i, 512).rearrange("p (q t) -> p q t", q=2) for i in range(2)]
            H = area(8192, 512)
            HT = area(8704, 512).rearrange("p (c s) -> p c s", c=4)
            Y = area(9216, 1024)
            RT = area(10240, 660)
            rn = [0]

            def rt(*shape):
                n = int(np.prod(shape))
                a = RT[:, rn[0]:rn[0] + n]
                rn[0] += n
                if len(shape) == 1:
                    return a
                names = "abcd"[:len(shape)]
                return a.rearrange(f"p ({' '.join(names)}) -> p {' '.join(names)}",
                                   **{k: v for k, v in zip(names[:-1], shape[:-1])})

            L = rt(2, 36)
            xgfree, ctfree = [None, None], [None, None]
            wr = WR[:, 288 * l:288 * l + 288].rearrange("p (c n) -> p c n", c=8)
            b = bank()
            xt = [Q.last["dve"], Q.last["act"], g2]
            for t in range(2):
                for c in range(8):
                    o = mm(b.ap[:, t * 36:t * 36 + 36], XT[:, c, t * 128:t * 128 + 128], wr[:, c, :],
                           c == 0, c == 7, b.free, *xt)
            xgfree[0] = o
            b.free = tt(L, b.ap[:, 0:72].rearrange("p (t n) -> p t n", t=2),
                        mid(BR[:, 36 * l:36 * l + 36], 2), ALU.add, o)

            def onehot(lg, rev, n):
                m, k, km, oh = rt(2), rt(2, n), rt(2), rt(2, n)
                rmax(m, lg)
                tt(k, lg, end(m, n), ALU.is_equal)
                tt(k, k, mid(rev, 2), ALU.mult)
                rmax(km, k)
                tt(oh, k, end(km, n), ALU.is_equal)
                return m, oh

            lg = L[:, :, 0:4]
            gm, og = onehot(lg, C("rev4"), 4)
            pr = rt(2, 4, 8)
            og4 = end(og, 8)
            for t in range(2):
                tt(pr[:, t], og4[:, t], L[:, t, 4:36].rearrange("p (g e) -> p g e", g=4), ALU.mult)
            es = rt(2, 8)
            for t in range(2):
                rsum(es[:, t], pr[:, t].rearrange("p g e -> p e g"))
            m1, o1 = onehot(es, C("rev8"), 8)
            es2 = rt(2, 8)
            stt(es2, o1, NEG, es, ALU.mult, ALU.add)
            m2, o2 = onehot(es2, C("rev8"), 8)
            comb, sel, pos, sl = rt(2, 32), rt(2, 32), rt(2, 32), rt(2, 8)
            tt(sl, o1, o2, ALU.add)

            def by_expert(dst, s):
                for t in range(2):
                    o = tt(dst[:, t].rearrange("p (g e) -> p g e", g=4), og4[:, t], mid(s[:, t], 4), ALU.mult)
                return o

            o = by_expert(sel, sl)
            b = bank()
            mm(b.ap[:, 0:32], C("before"), sel[:, 0, :], True, True, b.free, o)
            mm(b.ap[:, 32:64], C("ones"), sel[:, 0, :], True, False)
            mm(b.ap[:, 32:64], C("before"), sel[:, 1, :], False, True)
            mm(b.ap[:, 64:96], C("ones"), sel[:, 0, :], True, False)
            o = mm(b.ap[:, 64:96], C("ones"), sel[:, 1, :], False, True)
            placed = o
            eg = rt(2, 4)
            o = tt(eg, lg, end(gm, 4), ALU.subtract)
            o = fn(eg, eg, ACT.Exp, o)
            gw = rt(2)
            rsum(gw, eg, o)
            recip(gw, gw)
            e2, w1, w2, wi = rt(2), rt(2), rt(2), rt(2, 8)
            o = tt(e2, m2, m1, ALU.subtract)
            o = fn(e2, e2, ACT.Exp, o)
            ts(w1, e2, 1.0, None, ALU.add, None, o)
            recip(w1, w1)
            tt(w1, w1, gw, ALU.mult)
            tt(w2, w1, e2, ALU.mult)
            tt(o1, o1, end(w1, 8), ALU.mult)
            tt(o2, o2, end(w2, 8), ALU.mult)
            tt(wi, o1, o2, ALU.add)
            by_expert(comb, wi)
            ts(pos, b.ap[:, 0:64].rearrange("p (t e) -> p t e", t=2), 1.0, None, ALU.add, None, placed)
            tt(pos, pos, sel, ALU.mult)
            ts(pos, pos, -1.0, None, ALU.add, None)
            cm = small(1)
            b.free = rmax(cm, b.ap[:, 64:96])

            gfree = [None]

            def gather(g):
                i = g % 2
                for t in range(2):
                    o = tt(G[:, t].rearrange("p (e s) -> p e s", e=4), mid(C("iota")[:, 0:CAP], 4),
                           end(pos[:, t, 4 * g:4 * g + 4], CAP), ALU.is_equal, gfree[0])
                for t in range(2):
                    ow = tt(GW[:, t].rearrange("p (e s) -> p e s", e=4), G[:, t].rearrange("p (e s) -> p e s", e=4),
                            end(comb[:, t, 4 * g:4 * g + 4], CAP), ALU.mult)
                for c in range(0, 8, 2):
                    b = bg if g else (bg, bO0, bO1, bY0)[c // 2]
                    for k in range(2):
                        for t in range(2):
                            sv = X[:, t, :].rearrange("p (d c) -> p c d", c=8)[:, c + k, :]
                            o2 = mm(b.ap[:, k * 256:k * 256 + 256], sv, G[:, t, :], t == 0,
                                    t == 1, b.free, o)
                    b.free = copy(XG[i][:, c:c + 2, :], b.ap.rearrange("p (k s) -> p k s", k=2), o2, xgfree[i])
                b = bg if g else bY1
                for q in range(2):
                    for t in range(2):
                        o2 = tr(b.ap[:, (q * 2 + t) * 128:(q * 2 + t) * 128 + 128],
                                GW[:, t, q * 128:q * 128 + 128], b.free, ow)
                gfree[0] = o2
                b.free = copy(CT[i], b.ap.rearrange("p (q t) -> p q t", q=2), o2, ctfree[i])
                return [Q.last["dve"], Q.last["act"]]

            bG, bU, bT, bY0, bY1, bO0, bO1, bg = banks

            hfree = [None]
            yfree = [None]
            htfree = [None]

            def up(pair, got):
                i, s0 = (pair // 2) % 2, (pair % 2) * 128
                W = []
                for w in ("w_gate", "w_up"):
                    W.append([load(major(I[w][l, (2 * pair + x) // 8, (2 * pair + x) % 8], 0, 512), 8, 512, slots)
                              for x in range(2)])
                for k, b in ((0, bG), (1, bU)):
                    for c in range(8):
                        for x in range(2):
                            o = mm(b.ap[64 * x:64 * x + 64, :], XG[i][:, c, s0 + 64 * x:s0 + 64 * x + 64],
                                   W[k][x].ap[:, c, :], c == 0, c == 7, b.free, W[k][x].got, *got)
                    for x in range(2):
                        W[k][x].free = o
                    if k == 0:
                        a = bG.free = fn(H, bG.ap, ACT.Silu, o, hfree[0])
                bU.free = tt(H, H, bU.ap, ALU.mult, o, a)
                if pair % 2:
                    xgfree[i] = o
                return bU.free

            def down(pair, h):
                hv = H.rearrange("p (f c) -> p c f", c=4)
                for c in range(4):
                    o = tr(bT.ap[:, c * 128:c * 128 + 128], hv[:, c, :], bT.free, h)
                hfree[0] = o
                bT.free = ht = vcopy(HT, bT.ap.rearrange("p (c s) -> p c s", c=4), o, htfree[0])
                W = []
                for x in range(2):
                    e = 2 * pair + x
                    W.append(load(I["w_down"][l, e // 8, e % 8].rearrange("(p c) n -> p c n", p=128), 4, 1024, slots))
                ys = []
                for n, b in enumerate((bY0, bY1)):
                    for c in range(4):
                        for x in range(2):
                            o = mm(b.ap[64 * x:64 * x + 64, :], HT[:, c, 64 * x:64 * x + 64],
                                   W[x].ap[:, c, n * 512:n * 512 + 512], c == 0, c == 3, b.free, W[x].got, ht)
                    b.free = (acopy if n == 0 else vcopy)(Y[:, n * 512:n * 512 + 512], b.ap, o, yfree[0])
                    ys.append(b.free)
                htfree[0] = o
                W[0].free = W[1].free = o
                return ys

            def scatter(pair, ys):
                i = (pair // 2) % 2
                for n, t in ((0, 0), (0, 1), (1, 0), (1, 1)) if pair < 15 else ((0, 0), (1, 0), (0, 1), (1, 1)):
                        b = (bO0, bO1)[(n if pair == 15 else t)]
                        o = mm(b.ap, CT[i][:, pair % 2, t * 128:t * 128 + 128], Y[:, n * 512:n * 512 + 512],
                               True, True, b.free, *ys)
                        a = ACC[:, t, n * 512:n * 512 + 512]
                        if pair == 0:
                            b.free = stt(a, X[:, t, n * 512:n * 512 + 512], ALPHA, b.ap, ALU.mult, ALU.add, o)
                        else:
                            b.free = tt(a, a, b.ap, ALU.add, o)
                        if pair == 15:
                            sums.take(t, a)
                yfree[0] = o
                if pair % 2:
                    ctfree[i] = o

            got = gather(0)
            ts(cm, cm, float(CAP), None, ALU.is_gt, None)
            flag = vcopy(FLAG[:, l:l + 1], cm)
            nxt = None
            ys = None
            for pair in range(16):
                h = up(pair, got)
                if pair:
                    scatter(pair - 1, ys)
                if pair % 2 == 0 and pair < 14:
                    nxt = gather(pair // 2 + 1)
                if pair % 2:
                    got = nxt
                ys = down(pair, h)
                if pair == 3:
                    next(side, None)
            sums = Stats(2)
            warm(ACT.Sqrt)
            scatter(15, ys)
            beyond(l, pos, comb, flag, [Q.last[x] for x in ("pe", "act", "dve")], sums)
            return [layer_norm(t, gr_next, sums, ACC) for t in range(2)]

        def load_gain(src, *deps):
            gr = group()
            Q.dma("act", gr, NG1[0], src.partition_broadcast(128), *deps)
            return gr

        def rms_norm(dst, t, st, gr):
            mv, ms = small(2), small(1)
            dve(lambda e: e.bn_aggr(mv, st.st[:, t]))
            stt(ms, mv[:, 0:1], mv[:, 0:1], mv[:, 1:2], ALU.mult, ALU.add)
            rsqrt(ms, ms, 1.0, 1e-6)
            return stt(dst[:, t, :], X[:, t, :], ms, NG1[0], ALU.mult, ALU.mult, gr)

        def rms_full(dst, t, gr):
            ss, r = small(1), small(1)
            o = fn(dst[:, t, :], X[:, t, :], ACT.Square, Q.last["dve"], acc=ss)
            rsqrt(r, ss, 1.0 / 1024, 1e-6, o)
            return stt(dst[:, t, :], X[:, t, :], r, NG1[0], ALU.mult, ALU.mult, gr)

        NG1 = [None]

        def ot(br, c):
            k = (4 * br + c) * 256
            return [y[:, k:k + 256] for y in tens["Y"]]

        def ots(br):
            return tuple(y[:, 1024 * br:1024 * br + 1024].rearrange("p (c t) -> p c t", c=4) for y in tens["Y"])

        def rope(raw, dst, tmp, *deps):
            b = bank()
            o = mm(b.ap[:, 0:256], C("perm"), raw, True, True, b.free, *deps)
            b.free = tt(tmp, b.ap[:, 0:256], SIN, ALU.mult, o, *deps)
            tt(dst, raw, COS, ALU.mult)
            return tt(dst, dst, tmp, ALU.add)

        def nsa(l, fd):
            QR = area(8192, 1024).rearrange("p (j t) -> p j t", j=4)
            QQ = area(9216, 1024).rearrange("p (j t) -> p j t", j=4)
            KS = area(10240, 1024).rearrange("p (g h t) -> p g h t", g=2, h=2)
            KW = area(11264, 1024).rearrange("p (g h t) -> p g h t", g=2, h=2)
            VS = area(12288, 256).rearrange("p (k d) -> p k d", k=2)
            VW = area(12544, 256).rearrange("p (k d) -> p k d", k=2)
            BK = area(3072, 480).rearrange("p (j g n) -> p j g n", j=16, g=2)
            BV = area(3552, 480).rearrange("p (j g n) -> p j g n", j=16, g=2)
            HK = area(4032, 256)
            TK = area(4288, 60).rearrange("p (c n) -> p c n", c=2)
            TR = area(4352, 512).rearrange("p (g c r n) -> p g c r n", g=2, c=2, r=4)
            RAW = area(4864, 256)
            TMP = area(6144, 256)
            KC = area(6400, 128).rearrange("p (g h n) -> p g h n", g=2, h=2)
            VC = area(6528, 512).rearrange("p (g r d) -> p g r d", g=2, r=2)
            PC = area(7040, 512)
            PT = area(7552, 512).rearrange("p (g t) -> p g t", g=2)
            GT = small(48).rearrange("p (t n) -> p t n", t=2)
            W2D = area(8064, 128).rearrange("p (h d) -> p h d", h=2)
            for a in (KS, KW, KC, VC, TR):
                nz = pool(lambda e, a=a: e.memset(a, 0.0))
            for j in range(4):
                if j % 2 == 0:
                    p = fd.next()
                b, o = feat(p, (j % 2) * 128, XS)
                o = b.free = qcopy(QR[:, j, :], b.ap[:, 0:256], o)
                rope(QR[:, j, :], QQ[:, j, :], TMP, o)
            p = fd.next()
            for k, B in ((0, BK), (1, BV)):
                b, o = feat(p, k * 128, XS)
                bv = b.ap[:, 0:256].rearrange("p (n j i) -> p i j n", j=8, i=2)
                for i in range(2):
                    for g in range(2):
                        for hf in range(2):
                            vcopy(B[64 * i:64 * i + 64, 8 * hf:8 * hf + 8, g, :],
                                  bv[64 * g:64 * g + 64, i, :, hf:hf + 15], o)
                b.free = Q.last["dve"]
                pv = VT[:, 68 + 32 * k + 16 * l:84 + 32 * k + 16 * l]
                for g in range(2):
                    tt(B[:, :, g, :], B[:, :, g, :], end(pv, 15), ALU.add)
            built = Q.last["dve"]
            TMP2 = area(5120, 256)
            VTT = area(5376, 256)
            dep = [None]

            def keys(p, n0, K):
                b, o = feat(p, n0, XS)
                o = b.free = acopy(RAW, b.ap[:, 0:256], o, dep[0])
                rope(RAW, TMP2, TMP, o)
                for g in range(2):
                    for h in range(2):
                        dep[0] = vcopy(K[64 * h:64 * h + 64, g, h, :], TMP2[64 * g:64 * g + 64, :], nz)

            def turn_back(p, n0, n, outs, f):
                b, o = feat(p, n0, XS)
                a = b.free = acopy(VTT[0:n, :], b.ap[0:n, 0:256], o, Q.last["pe"])
                b = bank()
                for t in range(2):
                    o = tr(b.ap[:, t * 128:t * 128 + n], VTT[0:n, t * 128:t * 128 + 128], b.free, a)
                for t in range(2):
                    b.free = fn(outs(t), b.ap[:, t * 128:t * 128 + n], f, o)

            u0 = fd.next()
            turn_back(u0, 0, 24, lambda t: GT[:, t, :], ACT.Sigmoid)
            us = [fd.next() for _ in range(2)]

            w2 = [W2[:, 256 * l + 128 * k:256 * l + 128 * k + 128].rearrange("p (c d) -> p c d", c=2) for k in range(2)]

            def hidden(k):
                B = (BK, BV)[k]
                u = us[k]
                b = bank()
                for j in range(16):
                    o = mm(b.ap[0:30, 0:256], B[:, j].rearrange("p g n -> p (g n)"), u.ap[:, j, :],
                           j == 0, j == 15, b.free, u.got, built)
                u.free = o
                o = b.free = fn(HK[0:30, :], b.ap[0:30, 0:256], ACT.Gelu_apprx_tanh, o, Q.last["pe"])
                return o

            def back(o):
                b = bank()
                for c in range(2):
                    o = tr(b.ap[:, c * 30:c * 30 + 30], HK[0:30, c * 128:c * 128 + 128], b.free, o)
                return b, o

            def small_keys(o):
                b = bank()
                for c in range(2):
                    for h in range(2):
                        o = vcopy(W2D[:, h, :], w2[0][:, c, :], Q.last["pe"])
                    o = mm(b.ap[:, 0:30], W2D.rearrange("p h d -> p (h d)"), TK[:, c, :], c == 0, c == 1,
                           b.free, o)
                for h in range(2):
                    b.free = vcopy(KC[64 * h:64 * h + 64, :, h, 0:15],
                                   b.ap[64 * h:64 * h + 64, 0:30].rearrange("p (g n) -> p g n", g=2), o, nz)
                return b.free

            def small_values(trd):
                b = bank()
                for g in range(2):
                    for c in range(2):
                        o = mm(b.ap[:, g * 64:g * 64 + 64], TR[:, g, c].rearrange("p r n -> p (r n)"),
                               w2[1][:, c, :], c == 0, c == 1, b.free, trd)
                for g in range(2):
                    for r in range(4):
                        q0 = 32 * r
                        b.free = vcopy(VC[q0:q0 + 32, g, r // 2, (r % 2) * 64:(r % 2) * 64 + 64],
                                       b.ap[q0:q0 + 32, g * 64:g * 64 + 64], o)

            def small_rows(t, kc):
                b = bank()
                for j in range(4):
                    o = mm(b.ap[:, j * 64:j * 64 + 64], QR[:, j, t * 128:t * 128 + 128],
                           KC[:, j // 2].rearrange("p h n -> p (h n)"), True, True, b.free, kc)
                P = PC[:, t * 256:t * 256 + 256].rearrange("p (h n) -> p h n", h=8)
                b.free = tt(P, b.ap[:, 0:256].rearrange("p (h n) -> p h n", h=8),
                            mid(C("madd")[:, t * 32:t * 32 + 32], 8), ALU.add, o)
                m, sm = small(8), small(8)
                rmax(m, P)
                o = tt(P, P, end(m, 32), ALU.subtract)
                yield
                o = fn(P, P, ACT.Exp, o)
                rsum(sm, P, o)
                recip(sm, sm)
                tt(sm, sm, GT[:, t, :].rearrange("p (h b) -> p h b", b=3)[:, :, 0], ALU.mult)
                tt(P, P, end(sm, 32), ALU.mult)
                tt(P, P, mid(C("m01")[:, t * 32:t * 32 + 32], 8), ALU.mult)
                yield

            h = hidden(0)
            p = fd.next()
            keys(p, 0, KS)
            b, o = back(h)
            tk = b.free = vcopy(TK, b.ap[:, 0:60].rearrange("p (c n) -> p c n", c=2), o)
            turn_back(p, 128, 128, lambda t: VS[:, t, :], ACT.Copy)
            kc = small_keys(tk)
            h = hidden(1)
            p = fd.next()
            r0, r1 = small_rows(0, kc), small_rows(1, kc)
            next(r0)
            next(r1)
            next(r0)
            next(r1)
            b, o = back(h)
            for c in range(2):
                for g in range(2):
                    trd = b.free = vcopy(TR[:, g, c, :, 0:15], mid(b.ap[:, c * 30 + g * 15:c * 30 + g * 15 + 15], 4),
                                         o, nz)
            keys(p, 0, KW)
            small_values(trd)
            rows_done = Q.last["dve"]
            turn_back(p, 128, 128, lambda t: VW[:, t, :], ACT.Copy)
            b = bank()
            for g in range(2):
                for t in range(2):
                    o = tr(b.ap[:, g * 256 + t * 128:g * 256 + t * 128 + 128],
                           PC[:, t * 256 + g * 128:t * 256 + g * 128 + 128], b.free, rows_done)
            b.free = vcopy(PT, b.ap.rearrange("p (g t) -> p g t", g=2), o)
            Q.fence()
            gt = GT.rearrange("p t (h b) -> p t h b", b=3)
            jobs = []
            ob = [None]
            for j in range(4):
                for br, (K, V) in ((1, (KS, VS)), (2, (KW, VW))):
                    def fin(pt, j=j, br=br, V=V):
                        if br == 1:
                            ob[0] = banks_o[j % 2]
                        b = ob[0]
                        o = values(pt, lambda k, h: V[:, k, (j // 2) * 64:(j // 2) * 64 + 64], b, br == 1, False)
                        if br == 2:
                            o = mm(b.ap[:, 0:256], VC[:, j // 2, j % 2, :], PT[:, j // 2, :], False, True)
                            b.free = otdone[0] = vsplit(*ot(0, j), b.ap[:, 0:256], o)
                    jobs.append(((QQ[:, j, :], K[:, j // 2], True, gt[:, :, 2 * j:2 * j + 2, br], None), fin))
            hold(2)
            attend(jobs)
            hold(0)

        banks_o = banks[6:8]
        otdone = [None] * 3

        def diff(l, fd):
            QQ = area(8192, 1024).rearrange("p (j t) -> p j t", j=4)
            KP = area(9216, 2048).rearrange("p (j h t) -> p j h t", j=4, h=2)
            V = area(11264, 1024).rearrange("p (k d) -> p k d", k=2)
            RAW, TMP, TMP2 = area(6144, 256), area(6400, 256), area(6656, 256)
            O = area(12800, 1024).rearrange("p (j t) -> p j t", j=4)
            kz = pool(lambda e: e.memset(KP, 0.0))
            rf = None
            for part in range(2):
                for j in range(4):
                    if j % 2 == 0:
                        p = fd.next()
                    b, o = feat(p, (j % 2) * 128, XS)
                    o = b.free = (acopy if part else qcopy)(RAW, b.ap[:, 0:256], o, rf)
                    if part == 0:
                        rf = rope(RAW, QQ[:, j, :], TMP, o)
                    else:
                        rope(RAW, TMP2, TMP, o)
                        for h in range(2):
                            rf = vcopy(KP[64 * h:64 * h + 64, j, h, :], TMP2[64 * h:64 * h + 64, :], kz)
            for k in range(2):
                p = fd.next()
                for t in range(2):
                    b, o = toks(p, 256, t, XS)
                    b.free = copy(V[:, t, 256 * k:256 * k + 256], b.ap[:, 0:256], o)
            ins = [Q.last["dve"], Q.last["act"]]
            jobs = []
            for j in range(4):
                def fin(pt, j=j):
                    b = bank()
                    o = values(pt, lambda k, h: V[:, k, j * 128:j * 128 + 128], b, True, True, heads=1)
                    b.free = copy(O[:, j, :], b.ap[:, 0:256], o)
                jobs.append(((QQ[:, j, :], KP[:, j], True, None, NLAM[:, l:l + 1], *ins), fin, 1))
            attend(jobs)
            SQ = area(8192, 1024)
            sq = fn(SQ, O.rearrange("p j t -> p (j t)"), ACT.Square, Q.last["dve"], Q.last["pe"])

            def sums():
                return [mm(b.ap, C("ones"), SQ[:, 512 * k:512 * k + 512], True, True, b.free, sq)
                        for k, b in enumerate(bs)]

            R = area(11776, 1024)

            def rest(o2):
                Of = O.rearrange("p j t -> p (j t)")
                for k, b in enumerate(bs):
                    b.free = ts(R[:, 512 * k:512 * k + 512], b.ap, 1.0 / 128, 1e-6, ALU.mult, ALU.add, o2[k])
                o = fn(R, R, ACT.Sqrt, b.free)
                yield
                init = 0.8 - 0.6 * math.exp(-0.3 * l)
                for k in range(4):
                    q = slice(256 * k, 256 * k + 256)
                    recip(R[:, q], R[:, q], o)
                    yield
                    tt(R[:, q], Of[:, q], R[:, q], ALU.mult)
                    o2 = ts(R[:, q], R[:, q], VT[:, 66 + l:67 + l], 1.0 - init, ALU.mult, ALU.mult)
                    otdone[1] = vsplit(*ot(1, k), R[:, q], o2)
                    yield
                hold(0)

            bs = banks[6:8]
            return sums, rest

        def sgu(l, fd, sums, rest):
            UT = area(3072, 1024).rearrange("p (g t) -> p g t", g=4)
            V = area(4096, 1024).rearrange("p (t d) -> p t d", t=2)
            WG = area(5120, 512).rearrange("p (g s) -> p g s", g=4)
            WT = area(5632, 512).rearrange("p (g t) -> p g t", g=4)
            BS = area(6144, 512)
            NG = area(6656, 512)
            J = area(7168, 512)
            S2 = area(5120, 512)
            gr = group()
            fr = [Q.last["dve"], Q.last["pe"], Q.last["pool"], Q.last["act"]]
            Q.dma("act", gr, WG, I["sgu_w_2"][l].rearrange("g t s -> t g s"), *fr)
            Q.dma("act", gr, BS, I["sgu_b_2"][l].rearrange("g t -> (g t)").partition_broadcast(128), *fr)
            Q.dma("act", gr, NG, I["sgu_norm_2"][l].partition_broadcast(128), *fr)
            ss, r = small(2), small(2)
            for k in range(2):
                p = fd.next()
                for t in range(2):
                    b, o = toks(p, 256, t, XS)
                    b.free = fn(V[:, t, 256 * k:256 * k + 256], b.ap[:, 0:256], ACT.Gelu_apprx_tanh, o)
            for t in range(2):
                sqd = fn(J, V[:, t, :], ACT.Square, acc=ss[:, t:t + 1])
            b = bank()
            for g in range(4):
                o = tr(b.ap[:, g * 128:g * 128 + 128], WG[:, g, :], b.free, gr)
            b.free = tt(WT, b.ap.rearrange("p (g t) -> p g t", g=4), mid(C("upto"), 4), ALU.mult, o)
            for j in range(4):
                if j % 2 == 0:
                    p = fd.next()
                if j == 2:
                    rsqrt(r, ss, 1.0 / 512, 1e-6, sqd)
                    for t in range(2):
                        v = stt(V[:, t, :], V[:, t, :], r[:, t:t + 1], NG, ALU.mult, ALU.mult, gr)
                b, o = feat(p, (j % 2) * 128, XS)
                b.free = fn(UT[:, j, :], b.ap[:, 0:256], ACT.Gelu_apprx_tanh, o)
            u = b.free
            fd.make()
            hold(2)
            sq = sums()

            def gated():
                bs = BS.rearrange("p (g t) -> p g t", g=4)
                for g in range(4):
                    b = bank()
                    for t in range(2):
                        o = mm(b.ap[:, t * 128:t * 128 + 128], V[:, t, g * 128:g * 128 + 128], WT[:, g, :], True, True,
                               b.free, v)
                    S = S2[:, (g % 2) * 256:(g % 2) * 256 + 256]
                    b.free = tt(S.rearrange("p (n t) -> p n t", n=2),
                                b.ap[:, 0:256].rearrange("p (n t) -> p n t", n=2), mid(bs[:, g, :], 2), ALU.add, o)
                    o = tt(S, S, UT[:, g, :], ALU.mult, u)
                    otdone[2] = vsplit(*ot(2, g), S, o)
                    yield

            r = rest(sq)
            next(r)
            return r, gated()

        def merge(l, fd, rest, gated, norm):
            MXH, MXL, tens["A"] = scope((f"MXH{l}", 2048, FR), (f"MXL{l}", 2048, FR), (f"AM{l}", 4608, F))
            MX = area(3072, 2048).rearrange("p (c t) -> p c t", c=8)
            SG = area(5120, 2048).rearrange("p (s k t) -> p s k t", s=2, k=4)
            MB = area(7168, 512).rearrange("p (k t) -> p k t", k=2)
            mf, sf, mdone = [None, None], [None, None], [None] * 8
            late = []

            def halves(m):
                k = slice(256 * m, 256 * m + 256)
                mdone[m] = vsplit(MXH[:, k], MXL[:, k], MX[:, m, :], late[m])

            for n in range(6):
                br, hf, i = n // 2, n % 2, n % 2
                for j in range(4):
                    if j % 2 == 0:
                        p = fd.next()
                    b, o = feat(p, (j % 2) * 128, XS)
                    k = 18 + 24 * l + 8 * br + 4 * hf + j
                    a = b.free = fn(SG[:, i, j, :], b.ap[:, 0:256], ACT.Sigmoid, o, sf[i], bias=VT[:, k:k + 1])
                    if j % 2:
                        next(rest, None)
                p = fd.next()
                for j in range(4):
                    m = 4 * hf + j
                    b, o = feat(p, j * 128, ots(br), otdone[br], nk=4)
                    if br == 0:
                        b.free = tt(MX[:, m, :], b.ap[:, 0:256], SG[:, i, j, :], ALU.mult, o, a)
                    else:
                        q = j % 2
                        b.free = tt(MB[:, q, :], b.ap[:, 0:256], SG[:, i, j, :], ALU.mult, o, a, mf[q])
                        mf[q] = pool(lambda e, m=m, q=q: e.tensor_tensor(MX[:, m, :], MX[:, m, :], MB[:, q, :],
                                                                         ALU.add), b.free)
                        if br == 2:
                            late.append(mf[q])
                            if m:
                                halves(m - 1)
                    if j % 2:
                        next(rest if br == 0 else gated, None)
                if n == 1:
                    for _ in rest:
                        pass
                if n == 3:
                    for _ in gated:
                        pass
                sf[i] = Q.last["dve"]
            halves(7)
            ms = tuple(eights(v) for v in (MXH, MXL))
            st = Stats(4)
            ln = []
            warm(ACT.Sqrt)
            for n in range(4):
                p = fd.next()
                for t in range(2):
                    b, o = toks(p, 256, t, ms, mdone)
                    xs = X[:, t, n * 256:n * 256 + 256]
                    b.free = tt(xs, xs, b.ap[:, 0:256], ALU.add, o)
                    st.take(t, xs)
                    if n == 3:
                        ln.append(norm(t, st))
            return ln

        def ffn_feed(l):
            plan = []
            for n in range(0, D_FF, 512):
                for w in ("w_ffn1_2", "w_ffn3_2"):
                    plan += wplan(I[w][l][:, n:min(n + 512, D_FF)], 0, min(512, D_FF - n))
            halves = []
            k = 0
            for n in range(0, D_FF, 512):
                m = 2 if n + 512 <= D_FF else 1
                halves.append(m)
            w2 = I["w_ffn2_2"][l].rearrange("(c p) n -> p c n", p=128)
            for c0 in range(0, 22, 4):
                nk = min(4, 22 - c0)
                plan.append((w2[:, c0:c0 + nk, :], nk, 1024, "a"))
            return Feed(plan), halves

        def ffn(l, fd, halves, dst, norm):
            *tens["Y"], tens["A"], _, J = scope((f"FH{l}", 5632, FR), (f"FL{l}", 5632, FR), (f"AF{l}", 1536, F),
                                                (f"PF{l}", 2048, F), (f"JF{l}", 2048, F))
            if dst is None:
                dst = J[:, :].rearrange("p (t d) -> p t d", t=2)
            FH, FL = (y[:, :].rearrange("p (c t) -> p c t", t=256) for y in tens["Y"])
            SG = area(3072, 1024).rearrange("p (k t) -> p k t", k=4)
            FV = area(4096, 512).rearrange("p (k t) -> p k t", k=2)
            st = Stats(2)
            sf = [None, None]
            vf = [None, None]
            n = 0
            for m in halves:
                acts = []
                for h in range(m):
                    p = fd.next()
                    for j in range(2):
                        b, o = feat(p, j * 128, XS)
                        i = 2 * h + j
                        a = b.free = fn(SG[:, i, :], b.ap[:, 0:256], ACT.Silu, o, sf[0])
                for h in range(m):
                    p = fd.next()
                    for j in range(2):
                        b, o = feat(p, j * 128, XS)
                        i = 2 * h + j
                        v = FV[:, i % 2, :]
                        b.free = tt(v, b.ap[:, 0:256], SG[:, i, :], ALU.mult, o, a, vf[i % 2])
                        vf[i % 2] = split(FH[:, n, :], FL[:, n, :], v, b.free)
                        n += 1
                sf[0] = Q.last["dve"]
            warm(ACT.Sqrt)
            ln = []
            bb = [bank() for _ in range(4)]
            done = Q.last["dve"]
            for c0 in range(0, 22, 2):
                p = fd.next()
                for t in range(2):
                    for n in range(2):
                        b = bb[2 * t + n]
                        for c in range(2):
                            f = [v[:, c0 + c, t * 128:t * 128 + 128] for v in (FH, FL)]
                            w = [v[:, c, n * 512:n * 512 + 512] for v in (p.hi, p.lo)]
                            mm(b.ap, f[0], w[0], c0 + c == 0, False, b.free, p.got, done)
                            mm(b.ap, f[1], w[0], False, False)
                            o = mm(b.ap, f[0], w[1], False, c0 + c == 21)
                        if c0 == 20:
                            xs = X[:, t, n * 512:n * 512 + 512]
                            b.free = tt(xs, xs, b.ap, ALU.add, o)
                            st.take(t, xs)
                    if c0 == 20:
                        ln.append(norm(t, st, dst))
                used(p, o)
            return dst, ln

        def mix_feed(l):
            w = I["w_in_2"][l]
            plan = wplan(w, 0, 512) + wplan(w, 512, 768) + wplan(w, 1280, 1408)
            plan += [(I[n][l].rearrange("(j p) n -> p j n", p=128), 16, 256, "raw")
                     for n in ("cmp_k_w1_2", "cmp_v_w1_2")]
            plan += wplan(w, 768, 1280) + wplan(w, 1304, 2840) + wplan(w, 3352, 3864) + wplan(w, 2840, 3352)
            for br in range(3):
                wb = I["w_branch_%s_2" % "abc"[br]][l].rearrange("(c p) n -> p c n", p=128)
                for h in range(2):
                    k = 1024 * br + 512 * h
                    plan += wplan(I["w_merge_2"][l], k, k + 512)
                    plan.append((wb[:, :, 512 * h:512 * h + 512], 4, 512, "n"))
            return Feed(plan + rows(I["w_out_2"][l]))

        def block2():
            nonlocal XS
            nm = [f"{x}{i}" for x in ("CH", "CL") for i in range(NCV)]
            cv = [ctx.enter_context(nc.sbuf_tensor(x, [128, 2048], FR)) for x in nm]
            XS = tuple(eights(sb(k, 2048, FR)) for k in ("XTH", "XTL"))
            NG1[0] = sb("NG1", 1024)[:, :]
            tens["W"] = [(cv[i], cv[NCV + i]) for i in range(NCV)]
            tens["off"] = 3072
            cvfree[:] = [None] * NCV
            gr = load_gain(I["attn_norm_2"][0], Q.last["pe"])
            cvfree[:] = [Q.last["dve"]] * NCV
            fd = mix_feed(0)
            two = lambda a: a.rearrange("p (t d) -> p t d", t=2)
            J2 = two(scope(("J2", 2048, F))[0][:, :])
            ln = [rms_full(J2, t, gr) for t in range(2)]
            fd.make()
            for l in range(2):
                if stop == 20 + 10 * l:
                    return
                with ExitStack() as m:
                    O2 = [m.enter_context(nc.sbuf_tensor(f"{x}{l}", [128, 3072], FR)) for x in ("OH", "OL")]
                    tens["Y"] = O2
                    tens["A"], = scope((f"AB{l}", 10752, F))
                    gr = load_gain(I["ffn_norm_2"][l], *ln)
                    transposed(XS, J2, *ln)
                    Q.fence()
                    Pb[:] = [area(3072 + 1024 * i, 1024).rearrange("p (t h k) -> p t h k", t=2, h=2) for i in range(2)]
                    PTb[:] = [area(k, 1024).rearrange("p (h k t) -> p h k t", h=2, k=2) for k in (5120, 12800)]
                    nsa(l, fd)
                    Q.yield_to_pe()
                    PTb[1] = area(7168, 1024).rearrange("p (h k t) -> p h k t", h=2, k=2)
                    left = diff(l, fd)
                    Q.yield_to_pe()
                    rest, gated = sgu(l, fd, *left)
                    Q.yield_to_pe()
                    J2 = two(area(11776, 2048))
                    ln = merge(l, fd, rest, gated, lambda t, st, gr=gr, J2=J2: rms_norm(J2, t, st, gr))
                    if stop == 21 + 10 * l:
                        return
                    gr = load_gain(I["attn_norm_2"][1] if l == 0 else I["final_norm_2"], *ln)
                    fd, halves = ffn_feed(l)
                    transposed(XS, J2, *ln)
                    Q.fence()
                J2 = X if l else None
                J2, ln = ffn(l, fd, halves, J2, lambda t, st, J2, gr=gr: rms_norm(J2, t, st, gr))
                if l == 0:
                    fd = mix_feed(1)
                    Q.yield_to_pe()
                if stop == 22 + 10 * l:
                    return

        before_moe = []

        def finish():
            og = group()
            last = [Q.last["dve"]]
            Q.dma("sp", og, out.rearrange("a (t p) d -> p (a t) d", p=128), X, *last)
            op = Op("sp", None, [og])
            Q.q["sp"].append(op)
            op.fn = lambda e: e.nop()

        def run():
            nonlocal gb, before_moe
            ln = []
            for l in range(2):
                if l:
                    mix_scope("m1")
                if l == 0:
                    plan = wplan(I["w_mem_kv"], 0, 512) + wplan(I["conv_w_in"][0], 0, 1792)
                else:
                    plan = wplan(I["moba_w_in"][0], 0, 2560)
                fd = Feed(plan + rows(I["w_o"][l]))
                if l == 0:
                    mem_kv(fd)
                    conv_mix(fd)
                else:
                    pool(lambda e, a=area(5120, 3072): e.memset(a, 0.0))
                    fd.make()
                    transposed(XS, X, *ln)
                    moba_mix(fd)
                ys = yts()
                st = Stats(4)
                warm(ACT.Sqrt)
                ln = []
                for n in range(4):
                    p = fd.next()
                    for t in range(2):
                        b, o = toks(p, 256, t, ys, ydone, [6, 7, 0, 1, 2, 3, 4, 5] if l == 0 else None)
                        xs = X[:, t, n * 256:n * 256 + 256]
                        b.free = stt(xs, xs, ALPHA, b.ap[:, 0:256], ALU.mult, ALU.add, o)
                        st.take(t, xs)
                        if n == 3:
                            ln.append(layer_norm(t, gb, st))
                before_moe = [Q.last.get(x) for x in ("pe", "act", "dve", "pool")]
                if stop == 10 * l + 1:
                    return
                gb = load_gb(I["ln2_g"][l], I["ln2_b"][l], *ln)
                Q.fence()
                ln = moe(l, gb, ln)
                if stop == 10 * l + 2:
                    return
                if l == 0:
                    gb = load_gb(I["ln1_g"][1], I["ln1_b"][1], *ln)
                Q.fence()
            b1.close()
            block2()

        run()
        finish()
        Q.number()
        block = ctx.enter_context(nc.Block())

        @block.sync
        def _(e):
            Q.emit("sp", e)

        @block.tensor
        def _(e):
            Q.emit("pe", e)

        @block.scalar
        def _(e):
            Q.emit("act", e)

        @block.vector
        def _(e):
            Q.emit("dve", e)

        @block.gpsimd
        def _(e):
            Q.emit("pool", e)


NAMES = ["x", "mem", "w_mem_kv", "conv_w_in", "conv_dw_w", "conv_dw_b", "conv_ln_g", "conv_ln_b", "moba_w_in", "w_o",
         "ln1_g", "ln1_b", "w_rg", "b_rg", "w_re", "b_re", "w_gate", "w_up", "w_down", "ln2_g", "ln2_b",
         "positions_2", "attn_norm_2", "w_in_2", "cmp_pos_k_2", "cmp_k_w1_2", "cmp_k_w2_2", "cmp_pos_v_2",
         "cmp_v_w1_2", "cmp_v_w2_2", "diff_lq1_2", "diff_lk1_2", "diff_lq2_2", "diff_lk2_2", "diff_subln_2",
         "sgu_norm_2", "sgu_w_2", "sgu_b_2", "w_branch_a_2", "w_branch_b_2", "w_branch_c_2", "w_merge_2",
         "b_merge_2", "w_out_2", "ffn_norm_2", "w_ffn1_2", "w_ffn3_2", "w_ffn2_2", "final_norm_2"]


def kernel(**inputs):
    import concourse.bacc as bacc
    from concourse.bass_utils import run_bass_kernel_spmd

    nc = bacc.Bacc("TRN2", target_bir_lowering=False, num_devices=1)
    arrays, aps = {}, {}
    for name in NAMES + ["cst"]:
        a = constants()[1] if name == "cst" else np.ascontiguousarray(inputs[name])
        arrays[f"in_{name}"] = a
        aps[name] = nc.dram_tensor(f"in_{name}", a.shape, mybir.dt.from_np(a.dtype), kind="ExternalInput").ap()
    out = nc.dram_tensor("out_x", (1, T, D), F, kind="ExternalOutput").ap()
    program(nc, aps, out)
    r = run_bass_kernel_spmd(nc, [arrays], core_ids=[0])
    return r.results[0]["out_x"]
```
